# Optimizing a Trainium2 kernel written in Bass

```python
import math
import jax, jax.numpy as jnp
from jax import lax
import numpy as np

D_MODEL = 2048
BATCH = 1
SEQ = 256
DEPTH = 2

CHUNK = 64
NORM_EPS = 1e-6
MLSTM_HEADS = 4
MLSTM_DQK = 128
MLSTM_DV = 256
GATE_SOFTCAP = 15.0
RET_HEADS = 4
RET_DK = 256
RET_DV = 256
ROPE_BASE = 10000.0
GDN_QK_HEADS = 16
GDN_V_HEADS = 32
GDN_DK = 128
GDN_DV = 128
CONV_WIDTH = 4
D_FF = -(-8 * D_MODEL // (3 * 256)) * 256

MLSTM_QK_W = MLSTM_HEADS * MLSTM_DQK
MLSTM_V_W = MLSTM_HEADS * MLSTM_DV
RET_QK_W = RET_HEADS * RET_DK
RET_V_W = RET_HEADS * RET_DV
L0_SPLITS = [MLSTM_QK_W, MLSTM_QK_W, MLSTM_V_W, MLSTM_V_W, 2 * MLSTM_HEADS,
             RET_QK_W, RET_QK_W, RET_V_W, RET_V_W]
L0_IN_W = sum(L0_SPLITS)
L0_MIX_W = MLSTM_V_W + RET_V_W
GDN_QK_W = GDN_QK_HEADS * GDN_DK
GDN_V_W = GDN_V_HEADS * GDN_DV
GDN_CONV_C = 2 * GDN_QK_W + GDN_V_W
L1_SPLITS = [GDN_CONV_C, GDN_V_W, GDN_V_HEADS, GDN_V_HEADS]
L1_IN_W = sum(L1_SPLITS)

kernel_name = 'hybrid_mlstm_retention_gdn_trunk'

def _rmsnorm(x, w):
    xf = x.astype(jnp.float32)
    y = xf * lax.rsqrt(jnp.mean(xf * xf, axis=-1, keepdims=True) + NORM_EPS)
    return (y * w.astype(jnp.float32)).astype(x.dtype)

def _head_rmsnorm(t):
    return t * lax.rsqrt(jnp.mean(t * t, axis=-1, keepdims=True) + NORM_EPS)

def _l2norm(t):
    return t * lax.rsqrt(jnp.sum(t * t, axis=-1, keepdims=True) + NORM_EPS)

def _split(h, sizes):
    return jnp.split(h, [int(c) for c in np.cumsum(sizes)[:-1]], axis=-1)

def _to_chunks(t):
    b, s, h, d = t.shape
    return t.reshape(b, s // CHUNK, CHUNK, h, d).transpose(0, 3, 1, 2, 4)

def _from_chunks(t):
    b, h, n, l, d = t.shape
    return t.transpose(0, 2, 3, 1, 4).reshape(b, n * l, h, d)

def _gate_chunks(t):
    b, s, h = t.shape
    return t.reshape(b, s // CHUNK, CHUNK, h).transpose(0, 3, 1, 2)

def _causal_mask(strict=False):
    return jnp.tril(jnp.ones((CHUNK, CHUNK), dtype=bool), -1 if strict else 0)

def _chunk_major(t):
    return jnp.moveaxis(t, 2, 0)

def _rotary(t, positions):
    d = t.shape[-1]
    inv_freq = ROPE_BASE ** (-jnp.arange(0, d, 2, dtype=jnp.float32) / d)
    ang = positions.astype(jnp.float32)[..., None] * inv_freq
    cos = jnp.cos(ang)[:, :, None, :]
    sin = jnp.sin(ang)[:, :, None, :]
    t1, t2 = t[..., 0::2], t[..., 1::2]
    return jnp.stack([t1 * cos - t2 * sin, t1 * sin + t2 * cos], axis=-1).reshape(t.shape)

def _mlstm_chunkwise(q, k, v, log_i, log_f):
    causal = _causal_mask()
    b_cum = jnp.cumsum(log_f, axis=-1)
    g = b_cum[..., -1]
    log_d = jnp.where(causal, b_cum[..., :, None] - b_cum[..., None, :] + log_i[..., None, :], -jnp.inf)
    m_intra = jnp.max(log_d, axis=-1)
    log_w = g[..., None] - b_cum + log_i
    m_w = jnp.max(log_w, axis=-1)
    bsz, nh, _, _, dk = q.shape
    dv = v.shape[-1]

    def step(carry, xs):
        c_mat, n_vec, m_run = carry
        q_c, k_c, v_c, lw_c, mw_c, g_c = xs
        qc_out = jnp.einsum('bhld,bhde->bhle', q_c, c_mat)
        qn_out = jnp.einsum('bhld,bhd->bhl', q_c, n_vec)
        m_new = jnp.maximum(g_c + m_run, mw_c)
        decay = jnp.exp(g_c + m_run - m_new)
        kw = k_c * jnp.exp(lw_c - m_new[..., None])[..., None]
        c_mat = decay[..., None, None] * c_mat + jnp.einsum('bhld,bhle->bhde', kw, v_c)
        n_vec = decay[..., None] * n_vec + jnp.sum(kw, axis=-2)
        return (c_mat, n_vec, m_new), (qc_out, qn_out, m_run)

    init = (jnp.zeros((bsz, nh, dk, dv), jnp.float32),
            jnp.zeros((bsz, nh, dk), jnp.float32),
            jnp.full((bsz, nh), -jnp.inf, dtype=jnp.float32))
    _, (qc, qn, m_prev) = lax.scan(
        step, init,
        (_chunk_major(q), _chunk_major(k), _chunk_major(v), _chunk_major(log_w), _chunk_major(m_w), _chunk_major(g)))
    qc = jnp.moveaxis(qc, 0, 2)
    qn = jnp.moveaxis(qn, 0, 2)
    m_prev = jnp.moveaxis(m_prev, 0, 2)
    m_inter = b_cum + m_prev[..., None]
    m_t = jnp.maximum(m_inter, m_intra)
    inter_scale = jnp.exp(m_inter - m_t)
    s = jnp.einsum('bhnld,bhnsd->bhnls', q, k) * jnp.exp(log_d - m_t[..., None])
    num = jnp.einsum('bhnls,bhnse->bhnle', s, v) + inter_scale[..., None] * qc
    den = jnp.sum(s, axis=-1) + inter_scale * qn
    return num / jnp.maximum(jnp.abs(den), jnp.exp(-m_t))[..., None]

def _retention_chunkwise(q, k, v, log_gamma):
    causal = _causal_mask()
    pos = jnp.arange(CHUNK, dtype=jnp.float32)
    rel = jnp.where(causal, pos[:, None] - pos[None, :], 0.0)
    d_intra = jnp.where(causal, jnp.exp(rel * log_gamma[:, None, None]), 0.0)
    scores = jnp.einsum('bhnld,bhnsd->bhnls', q, k) * d_intra[:, None]
    intra = jnp.einsum('bhnls,bhnse->bhnle', scores, v)
    lg = log_gamma[:, None]
    k_w = k * jnp.exp((CHUNK - 1 - pos) * lg)[:, None, :, None]
    q_w = q * jnp.exp((pos + 1) * lg)[:, None, :, None]
    chunk_decay = jnp.exp(CHUNK * log_gamma)[None, :, None, None]

    def step(r, xs):
        qw_c, kw_c, v_c = xs
        out = jnp.einsum('bhld,bhde->bhle', qw_c, r)
        r = chunk_decay * r + jnp.einsum('bhld,bhle->bhde', kw_c, v_c)
        return r, out

    bsz, nh, _, _, dk = q.shape
    init = jnp.zeros((bsz, nh, dk, v.shape[-1]), jnp.float32)
    _, inter = lax.scan(step, init, (_chunk_major(q_w), _chunk_major(k_w), _chunk_major(v)))
    return intra + jnp.moveaxis(inter, 0, 2)

def _gated_delta_chunkwise(q, k, v, log_alpha, beta):
    causal = _causal_mask()
    strict = _causal_mask(strict=True)
    g_cum = jnp.cumsum(log_alpha, axis=-1)
    decay = jnp.exp(jnp.where(causal, g_cum[..., :, None] - g_cum[..., None, :], -jnp.inf))
    k_beta = k * beta[..., None]
    a = jnp.where(strict, jnp.einsum('bhnld,bhnsd->bhnls', k_beta, k) * decay, 0.0)
    dv = v.shape[-1]
    rhs = jnp.concatenate([v * beta[..., None], k_beta * jnp.exp(g_cum)[..., None]], axis=-1)
    sol = lax.linalg.triangular_solve(a, rhs, left_side=True, lower=True, unit_diagonal=True)
    u, w = sol[..., :dv], sol[..., dv:]
    attn = jnp.where(causal, jnp.einsum('bhnld,bhnsd->bhnls', q, k) * decay, 0.0)
    q_g = q * jnp.exp(g_cum)[..., None]
    k_tail = k * jnp.exp(g_cum[..., -1:] - g_cum)[..., None]
    g_tot = jnp.exp(g_cum[..., -1])

    def step(s, xs):
        qg_c, w_c, u_c, attn_c, kt_c, gt_c = xs
        v_new = u_c - jnp.einsum('bhld,bhde->bhle', w_c, s)
        out = jnp.einsum('bhld,bhde->bhle', qg_c, s) + jnp.einsum('bhls,bhse->bhle', attn_c, v_new)
        s = gt_c[..., None, None] * s + jnp.einsum('bhld,bhle->bhde', kt_c, v_new)
        return s, out

    bsz, nh, _, _, dk = q.shape
    init = jnp.zeros((bsz, nh, dk, dv), jnp.float32)
    _, out = lax.scan(step, init, (_chunk_major(q_g), _chunk_major(w), _chunk_major(u),
                                   _chunk_major(attn), _chunk_major(k_tail), _chunk_major(g_tot)))
    return jnp.moveaxis(out, 0, 2)

def _causal_depthwise_conv(x, w):
    return lax.conv_general_dilated(
        x, w[:, None, :].astype(x.dtype), window_strides=(1,), padding=[(CONV_WIDTH - 1, 0)],
        dimension_numbers=('NWC', 'WIO', 'NWC'), feature_group_count=x.shape[-1])

def _mlstm_retention_mixer(h, positions, w_in, gate_bias, mlstm_norm, w_out):
    bsz, s, _ = h.shape
    f32 = jnp.float32
    proj = h @ w_in
    q_m, k_m, v_m, o_m, if_m, q_r, k_r, v_r, g_r = _split(proj, L0_SPLITS)
    q_m = q_m.reshape(bsz, s, MLSTM_HEADS, MLSTM_DQK).astype(f32) * (MLSTM_DQK ** -0.5)
    k_m = k_m.reshape(bsz, s, MLSTM_HEADS, MLSTM_DQK).astype(f32)
    v_m = v_m.reshape(bsz, s, MLSTM_HEADS, MLSTM_DV).astype(f32)
    gates = if_m.astype(f32) + gate_bias.astype(f32)
    gates = GATE_SOFTCAP * jnp.tanh(gates / GATE_SOFTCAP)
    log_i = gates[..., :MLSTM_HEADS]
    log_f = jax.nn.log_sigmoid(gates[..., MLSTM_HEADS:])
    h_m = _from_chunks(_mlstm_chunkwise(_to_chunks(q_m), _to_chunks(k_m), _to_chunks(v_m),
                                        _gate_chunks(log_i), _gate_chunks(log_f)))
    h_m = _head_rmsnorm(h_m) * mlstm_norm.astype(f32).reshape(MLSTM_HEADS, MLSTM_DV)
    h_m = jax.nn.sigmoid(o_m.astype(f32)) * h_m.reshape(bsz, s, MLSTM_V_W)
    q_r = _rotary(q_r.reshape(bsz, s, RET_HEADS, RET_DK).astype(f32), positions)
    k_r = _rotary(k_r.reshape(bsz, s, RET_HEADS, RET_DK).astype(f32), positions) * (RET_DK ** -0.5)
    v_r = v_r.reshape(bsz, s, RET_HEADS, RET_DV).astype(f32)
    log_gamma = jnp.log(1.0 - 2.0 ** (-5.0 - jnp.arange(RET_HEADS, dtype=f32)))
    y_r = _from_chunks(_retention_chunkwise(_to_chunks(q_r), _to_chunks(k_r), _to_chunks(v_r), log_gamma))
    y_r = _head_rmsnorm(y_r).reshape(bsz, s, RET_V_W) * jax.nn.silu(g_r.astype(f32))
    mixed = jnp.concatenate([h_m, y_r], axis=-1).astype(h.dtype)
    return mixed @ w_out

def _gated_deltanet_mixer(h, w_in, conv_w, a_log, dt_bias, norm_w, w_out):
    bsz, s, _ = h.shape
    f32 = jnp.float32
    proj = h @ w_in
    qkv, z, b_pre, a_pre = _split(proj, L1_SPLITS)
    qkv = jax.nn.silu(_causal_depthwise_conv(qkv, conv_w))
    q, k, v = _split(qkv, [GDN_QK_W, GDN_QK_W, GDN_V_W])
    rep = GDN_V_HEADS // GDN_QK_HEADS
    q = jnp.repeat(_l2norm(q.reshape(bsz, s, GDN_QK_HEADS, GDN_DK).astype(f32)), rep, axis=2) * (GDN_DK ** -0.5)
    k = jnp.repeat(_l2norm(k.reshape(bsz, s, GDN_QK_HEADS, GDN_DK).astype(f32)), rep, axis=2)
    v = v.reshape(bsz, s, GDN_V_HEADS, GDN_DV).astype(f32)
    beta = jax.nn.sigmoid(b_pre.astype(f32))
    log_alpha = -jnp.exp(a_log.astype(f32)) * jax.nn.softplus(a_pre.astype(f32) + dt_bias.astype(f32))
    o = _from_chunks(_gated_delta_chunkwise(_to_chunks(q), _to_chunks(k), _to_chunks(v),
                                            _gate_chunks(log_alpha), _gate_chunks(beta)))
    o = _head_rmsnorm(o) * norm_w.astype(f32)
    o = o.reshape(bsz, s, GDN_V_W) * jax.nn.silu(z.astype(f32))
    return o.astype(h.dtype) @ w_out

def _swiglu(h, w_gate, w_up, w_down):
    return (jax.nn.silu(h @ w_gate) * (h @ w_up)) @ w_down

def setup_inputs(seed: int = 0) -> dict:
    key = jax.random.key(seed)
    ks = jax.random.split(key, 32)
    f32 = jnp.float32

    def dense(k, fan_in, fan_out):
        return jax.random.normal(k, (fan_in, fan_out), f32) * (fan_in ** -0.5)

    def gain(k, n):
        return 1.0 + 0.02 * jax.random.normal(k, (n,), f32)

    x = jax.random.normal(ks[0], (BATCH, SEQ, D_MODEL), f32)
    positions = jnp.broadcast_to(jnp.arange(SEQ, dtype=jnp.int32)[None, :], (BATCH, SEQ))
    i_bias = 0.1 * jax.random.normal(ks[1], (MLSTM_HEADS,), f32)
    f_bias = jnp.linspace(3.0, 6.0, MLSTM_HEADS, dtype=f32) + 0.1 * jax.random.normal(ks[2], (MLSTM_HEADS,), f32)
    dt = jnp.exp(jax.random.uniform(ks[3], (GDN_V_HEADS,), f32, minval=math.log(1e-3), maxval=math.log(1e-1)))
    return {
        'x': x,
        'positions': positions,
        'l0_norm_mix': gain(ks[4], D_MODEL),
        'l0_w_in': dense(ks[5], D_MODEL, L0_IN_W),
        'l0_gate_bias': jnp.concatenate([i_bias, f_bias]),
        'l0_mlstm_norm': gain(ks[6], MLSTM_V_W),
        'l0_w_out': dense(ks[7], L0_MIX_W, D_MODEL),
        'l0_norm_ffn': gain(ks[8], D_MODEL),
        'l0_w_gate': dense(ks[9], D_MODEL, D_FF),
        'l0_w_up': dense(ks[10], D_MODEL, D_FF),
        'l0_w_down': dense(ks[11], D_FF, D_MODEL),
        'l1_norm_mix': gain(ks[12], D_MODEL),
        'l1_w_in': dense(ks[13], D_MODEL, L1_IN_W),
        'l1_conv_w': jax.random.normal(ks[14], (CONV_WIDTH, GDN_CONV_C), f32) * (CONV_WIDTH ** -0.5),
        'l1_a_log': jnp.log(jax.random.uniform(ks[15], (GDN_V_HEADS,), f32, minval=1.0, maxval=16.0)),
        'l1_dt_bias': dt + jnp.log(-jnp.expm1(-dt)),
        'l1_gdn_norm': gain(ks[16], GDN_DV),
        'l1_w_out': dense(ks[17], GDN_V_W, D_MODEL),
        'l1_norm_ffn': gain(ks[18], D_MODEL),
        'l1_w_gate': dense(ks[19], D_MODEL, D_FF),
        'l1_w_up': dense(ks[20], D_MODEL, D_FF),
        'l1_w_down': dense(ks[21], D_FF, D_MODEL),
        'final_norm': gain(ks[22], D_MODEL),
    }

def reference(x, positions, l0_norm_mix, l0_w_in, l0_gate_bias, l0_mlstm_norm, l0_w_out,
              l0_norm_ffn, l0_w_gate, l0_w_up, l0_w_down,
              l1_norm_mix, l1_w_in, l1_conv_w, l1_a_log, l1_dt_bias, l1_gdn_norm, l1_w_out,
              l1_norm_ffn, l1_w_gate, l1_w_up, l1_w_down, final_norm):
    norm_mix = [l0_norm_mix, l1_norm_mix]
    norm_ffn = [l0_norm_ffn, l1_norm_ffn]
    ffn = [(l0_w_gate, l0_w_up, l0_w_down), (l1_w_gate, l1_w_up, l1_w_down)]
    for layer in range(DEPTH):
        h = _rmsnorm(x, norm_mix[layer])
        if layer % 2 == 0:
            x = x + _mlstm_retention_mixer(h, positions, l0_w_in, l0_gate_bias, l0_mlstm_norm, l0_w_out)
        else:
            x = x + _gated_deltanet_mixer(h, l1_w_in, l1_conv_w, l1_a_log, l1_dt_bias, l1_gdn_norm, l1_w_out)
        h = _rmsnorm(x, norm_ffn[layer])
        x = x + _swiglu(h, *ffn[layer])
    return _rmsnorm(x, final_norm)


_drawn_inputs = setup_inputs


def setup_inputs(seed=0):
    import zlib

    import numpy as np

    out = dict(_drawn_inputs(seed))
    spreads = {}
    factors = {'l0_mlstm_norm': 6.029,
     'l0_norm_ffn': 3.506,
     'l1_norm_mix': 3.893,
     'l1_gdn_norm': 6.219,
     'l1_norm_ffn': 14.561,
     'final_norm': 8.017}
    for name, (base, spread) in spreads.items():
        noise = np.random.default_rng([zlib.crc32(name.encode()), seed]).standard_normal(out[name].shape)
        drawn = base * np.exp(spread * noise) if base else spread * noise
        out[name] = __import__('jax').numpy.asarray(drawn.astype(out[name].dtype))
    for name, factor in factors.items():
        out[name] = (out[name] * factor).astype(out[name].dtype)
    return out
```

```python
from contextlib import ExitStack

import numpy as np

import concourse.bass as bass
from concourse import mybir

F32 = mybir.dt.float32
F32R = mybir.dt.float32r
I32 = mybir.dt.int32
ALU = mybir.AluOpType
ACT = mybir.ActivationFunctionType
AX = mybir.AxisListType

P = 128
SEQ, D = 256, 2048
M = SEQ // P
KT = D // P
FF = -(-8 * D // (3 * 256)) * 256
FKT = FF // P
NB = 512
EPS = 1e-6
SLOTS = 4
MH, MDQK, MDV = 4, 128, 256
RH, RD = 4, 256
QKH, VH, GD = 16, 32, 128
CW = 4
ROUNDS = 4
HQ, HV = QKH // ROUNDS, VH // ROUNDS
SOFTCAP = 15.0
NEG = -1e30
TWO_PI = [6.28125, np.floor((2 * np.pi - 6.28125) * 2 ** 20) / 2 ** 20]
TWO_PI = [float(v) for v in TWO_PI + [2 * np.pi - sum(TWO_PI)]]
PI_BELOW = 3.1415925

QM, KM, VM, OM, QR, KR, VR, GR, L0W = 0, 512, 1024, 2048, 3072, 4096, 5120, 6144, 7168
L0_GATES = 3072
L1_GATES = 12288

LEVELS = [1, 2, 4, 8, 16, 32, 64]
CONST_PARTS = [("ident", 128), ("upto", 128), ("after", 128), ("ones", 128), ("neg", 384),
               ("low_up", 256), ("levels", 128 * len(LEVELS)), ("decay", RH * 256), ("freq", 128)]
CONST_AT = {}
_n = 0
for _name, _w in CONST_PARTS:
    CONST_AT[_name] = (_n, _n + _w)
    _n += _w
CONST_W = _n


def shape_constants():
    a, b = np.arange(P)[:, None], np.arange(P)[None, :]
    c = np.zeros((P, CONST_W), np.float32)

    def put(name, v):
        lo, hi = CONST_AT[name]
        c[:, lo:hi] = v

    put("ident", a == b)
    put("upto", a <= b)
    put("after", a > b)
    put("ones", 1.0)
    neg = np.where(a >= b, 0.0, NEG)
    put("neg", np.concatenate([neg, np.zeros((P, P)), neg], 1))
    put("low_up", np.concatenate([a > b, a <= b], 1))
    put("levels", np.concatenate([((a // (2 * n)) == (b // (2 * n))) & ((a // n) % 2 == 1) & ((b // n) % 2 == 0)
                                  for n in LEVELS], 1))
    t = np.arange(SEQ)[None, :]
    rel = np.where(t >= a, t - a, 0).astype(np.float32)
    dec = []
    for h in range(RH):
        log_gamma = np.log(np.float32(1.0) - np.float32(2.0) ** np.float32(-5.0 - h))
        dec.append(np.where(t >= a, np.exp(rel * log_gamma), 0.0) * RD ** -0.5)
    put("decay", np.concatenate(dec, 1))
    put("freq", (np.float32(10000.0) ** (-np.arange(0, RD, 2, dtype=np.float32) / np.float32(RD)))[None, :])
    return c


PHASES = [("l0a", KT // 2, 6), ("l0t", 4, 0), ("l0b", KT // 2, 8), ("out0", KT // 2, 4), ("gu0", KT // 2, 2 * FF // NB),
          ("dn0", FKT // 2, 4), ("l1t", 4, 0), ("l1r", KT // 2, 24), ("out1", KT, 4),
          ("gu1", KT // 2, 2 * FF // NB), ("dn1", FKT // 2, 4)]
UNIT0, BLOCK0, UPB = {}, {}, {}
_u = _b = 0
for _name, _upb, _nb in PHASES:
    UNIT0[_name], BLOCK0[_name], UPB[_name] = _u, _b, _upb
    _u += _upb * max(_nb, 1)
    _b += _nb
UNIT_END, BLOCK_END = _u, _b

MLSTM_HEAD = ["rows", "d_psum", "d_max", "d_exp", "s_psum", "s_prod", "st_psum", "st_copy", "num_psum", "num_div"]
L0_STEPS = (["gates", "tanh", "cap", "exp", "log1p", "m_tr", "m_trc"]
            + [f"m{h}_{s}" for h in range(MH) for s in MLSTM_HEAD]
            + ["m_sq", "m_norm"]
            + ["pos", "sincos"]
            + [f"rot{i}_{s}" for i in range(2 * M) for s in ("mul", "tr", "copy")]
            + [f"r{h}_{s}" for h in range(RH) for s in ("s_psum", "s_dec", "o_psum", "o_copy")]
            + ["r_sq", "r_norm"]
            + [f"mix{g}_{s}" for g in range(4) for s in ("tr", "hi", "lo")])
L0_AT = {s: i + 1 for i, s in enumerate(L0_STEPS)}

GDN_GATE_STEPS = ["raw", "exp", "log1p", "sums", "sums_exp"]
GATE_AT = {s: i + 1 for i, s in enumerate(GDN_GATE_STEPS)}
CONV_BLOCK = ["x_tr", "tap3", "conv", "silu"]
LAST = len(LEVELS) - 1


def level_steps(n):
    return ["b", "q_psum"] + (["q", "t_psum"] if n else []) + ["t"]


GDN_STEPS = (["round"] + [f"c{b}_{s}" for b in range(4) for s in CONV_BLOCK]
             + [f"n{b}_{s}" for b in range(2) for s in ("sq", "sum", "sqrt", "mul")]
             + ["k_tr", "k_copy", "v0_tr", "v0_copy", "v1_tr", "v1_copy"]
             + [f"k{c}_{s}" for c in range(2) for s in
                ["kq_psum", "kq"]
                + [f"g{g}_{s}" for g in range(2) for s in
                   ["lam", "d_psum", "d_exp", "a"]
                   + [f"l{n}_{s}" for n in range(len(LEVELS)) for s in level_steps(n)]
                   + (["res_psum"] if c else []) + ["res", "vn_psum", "vn", "o_psum", "o"]
                   + ([] if c else ["s_copy"])]]
             + ["o_sq", "o_sum", "o_rs", "o_gate"])
GDN_AT = {s: i + 2 for i, s in enumerate(GDN_STEPS)}
GDN_N = len(GDN_STEPS)


def build(nc, A, out):
    with ExitStack() as ctx:
        def sb(name, shape, dt=F32):
            return ctx.enter_context(nc.sbuf_tensor(name, shape, dt))

        def sem(name):
            return ctx.enter_context(nc.semaphore(name))

        wraw = sb("wraw", [P, SLOTS, 2 * NB])
        whi = sb("whi", [P, SLOTS, 2 * NB], F32R)
        wlo = sb("wlo", [P, SLOTS, 2 * NB], F32R)
        x = sb("x", [P, M, D])
        xs = sb("xs", [P, M, NB])
        hT_at = nc.sbuf_base
        hT_hi = sb("hT_hi", [P, KT, SEQ], F32R)
        hT_lo = sb("hT_lo", [P, KT, SEQ], F32R)
        const = sb("const", [P, CONST_W])
        gains = sb("gains", [P, 4, KT])
        ssq = sb("ssq", [P, M, 4])
        mean = sb("mean", [P, M])
        rms = sb("rms", [P, M])
        rstd = sb("rstd", [P, M])
        epsc = sb("epsc", [P, 2])
        gate_t = sb("gate_t", [P, 10, 64])
        C = {name: const[:, lo:hi] for name, (lo, hi) in CONST_AT.items()}
        ident = C["ident"]

        arena0 = (nc.sbuf_base + 63) // 64 * 64
        arena_end = arena0
        names = iter(range(1000))

        def at(offset, shape, dt=F32):
            nonlocal arena_end
            size = 4 * int(np.prod(shape[1:]))
            arena_end = max(arena_end, arena0 + offset + size)
            return nc.alloc_sbuf_tensor_at(f"arena{next(names)}", shape, dt, offset=arena0 + offset)

        KB = 1024
        pr = at(0, [P, M, L0W])
        mixT_hi = at(56 * KB, [P, KT, SEQ], F32R)
        mixT_lo = at(72 * KB, [P, KT, SEQ], F32R)
        qmT = at(56 * KB, [P, MH, SEQ])
        kmT = at(60 * KB, [P, MH, SEQ])
        d_rows = at(64 * KB, [P, 6, P])
        d_sb = at(67 * KB, [P, 384])
        p_sb = at(69 * KB, [P, 384])
        st_sb = at(71 * KB, [P, 384])
        mnorm = at(73 * KB, [P, MH * MDV])
        qrT = at(56 * KB, [P, 2 * RH, SEQ])
        krT = at(64 * KB, [P, 2 * RH, SEQ])
        cs = at(72 * KB, [P, 2, M, P])
        ang = at(74 * KB, [P, 2, M, P])
        rot = at(76 * KB, [P, RH, 2, P])
        rot_a = at(80 * KB, [P, RH, P])
        rot_b = at(82 * KB, [P, RH, P])
        rs_sb = at(84 * KB, [P, 384])
        fT_hi = at(0, [P, FKT, SEQ], F32R)
        fT_lo = at(44 * KB, [P, FKT, SEQ], F32R)
        sg = at(88 * KB, [P, M, NB])
        prod = xs
        qkv = at(0, [P, M, 2048])
        k_tok = at(0, [P, M, 512])
        v_tok = at(4 * KB, [P, M, 1024])
        k_tail = at(12 * KB, [P, 4, P])
        zs = at(16 * KB, [P, M, 1024])
        qkT = at(24 * KB, [P, 8, SEQ])
        vT = at(32 * KB, [P, 8, SEQ])
        sq = at(40 * KB, [P, 4, SEQ])
        rn = at(44 * KB, [P, 4, SEQ])
        lam = at(32 * KB, [P, 4, P])
        EA = at(34 * KB, [P, 4, P])
        ET = at(36 * KB, [P, 4, P])
        kq = at(38 * KB, [P, 4, 2 * P])
        T = at(42 * KB, [P, 4, P])
        TT = at(44 * KB, [P, 4, P])
        Q1 = at(46 * KB, [P, 4, P])
        Bm = at(48 * KB, [P, 4, P])
        Rm = at(50 * KB, [P, 4, P])
        Vn = at(52 * KB, [P, 4, P])
        qs_sb = at(54 * KB, [P, 4, P])
        St = xs[:, :, :].rearrange("p m (h n) -> p (m h) n", n=P)
        conv_w = at(56 * KB, [P, 64, CW])
        gnorm = at(57 * KB, [P, GD])
        o_sq = at(42 * KB, [P, M, HV, GD])
        conv_r = at(57 * KB + 512, [P, 16, CW])
        gr = at(58 * KB, [P, 8, M, HV])
        o_ms = at(58 * KB + 512, [P, M, HV])
        o_all = at(60 * KB, [P, M, VH * GD])
        oT_hi = at(0, [P, 2 * KT, SEQ], F32R)
        oT_lo = at(32 * KB, [P, 2 * KT, SEQ], F32R)
        fgain = nc.alloc_sbuf_tensor_at("fgain", [P, D], F32, offset=hT_at)
        assert arena_end <= nc.sbuf_usable_end, (arena_end, nc.sbuf_usable_end)

        acc = [ctx.enter_context(nc.psum_tensor(f"acc{i}", [P, M, NB], F32)) for i in range(2)]
        aux = [ctx.enter_context(nc.psum_tensor(f"aux{i}", [P, 2 * NB], F32)) for i in range(2)]
        aux4 = [aux[i // 2][:, (i % 2) * NB:(i % 2 + 1) * NB] for i in range(4)]

        raw_in = [sem(f"raw_in{i}") for i in range(SLOTS)]
        hi_done = sem("hi_done")
        lo_done = sem("lo_done")
        unit_used = sem("unit_used")
        acc_read = [sem(f"acc_read{i}") for i in range(2)]
        consts_in = sem("consts_in")
        x_in = sem("x_in")
        eps_set = sem("eps_set")
        xs_copied = sem("xs_copied")
        xt_ready = sem("xt_ready")
        xhi_done = sem("xhi_done")
        xlo_done = sem("xlo_done")
        mean_done = sem("mean_done")
        rms_done = sem("rms_done")
        rstd_done = sem("rstd_done")
        tail_ready = sem("tail_ready")
        tail_read = sem("tail_read")
        ft_ready = sem("ft_ready")
        fhi_done = sem("fhi_done")
        flo_done = sem("flo_done")
        l0_step = sem("l0_step")
        gate_step = sem("gate_step")
        gdn_step = sem("gdn_step")
        o_tr = sem("o_tr")
        o_hi = sem("o_hi")
        o_lo = sem("o_lo")
        epi_step = sem("epi_step")
        l1_const = sem("l1_const")
        out_done = sem("out_done")

        def col_block(w, col):
            return w.rearrange("(k p) n -> p k n", p=P)[:, :, bass.ds(col, NB)]

        NORM_OF = {"out0": 1, "dn0": 2, "out1": 3, "dn1": 4}

        block = ctx.enter_context(nc.Block())

        @block.sync
        def _(sp):
            def unit(w, u, j, col):
                sp.wait_ge(lo_done, u - (SLOTS - 1))
                sp.dma_start(wraw[:, j % SLOTS, :].rearrange("p (k n) -> p k n", k=2),
                             col_block(w, col)[:, 2 * j:2 * j + 2, :]).then_inc(raw_in[j % SLOTS], 16)

            def first_units(w, n):
                for j in range(n):
                    sp.dma_start(wraw[:, j, :].rearrange("p (k n) -> p k n", k=2),
                                 col_block(w, 0)[:, 2 * j:2 * j + 2, :]).then_inc(raw_in[j], 16)

            def phase(name, w, n_body, lo, hi, cols):
                upb = UPB[name]
                with sp.Fori(lo, hi) as i:
                    for b, (wt, col) in enumerate(cols(i)):
                        for j in range(upb):
                            u = UNIT0[name] + (i * n_body + b) * upb + j
                            sp.wait_ge(lo_done, u - (SLOTS - 1))
                            s = (b * upb + j) % SLOTS
                            sp.dma_start(wraw[:, s, :].rearrange("p (k n) -> p k n", k=2),
                                         col_block(wt, col)[:, 2 * j:2 * j + 2, :]).then_inc(raw_in[s], 16)

            def tail(name, w, col, width):
                for j in range(4):
                    sp.wait_ge(lo_done, UNIT0[name] + j - (SLOTS - 1))
                    sp.dma_start(wraw[:, j, 0:4 * width].rearrange("p (k n) -> p k n", k=4),
                                 w.rearrange("(k p) n -> p k n", p=P)[:, 4 * j:4 * j + 4, col:col + width]
                                 ).then_inc(raw_in[j], 16)

            sp.dma_start(x[:], A["x"].rearrange("a (m p) n -> p (a m) n", p=P)).then_inc(x_in, 16)
            sp.dma_start(const[:], A["shape_constants"]).then_inc(consts_in, 16)
            sp.dma_start(gains[:], A["gains"].rearrange("p (n k) -> p n k", n=4)).then_inc(consts_in, 16)
            sp.dma_start(gate_t[:, 9, 0:2].bitcast(I32), A["positions"]
                         ).then_inc(consts_in, 16)
            sp.dma_start(gate_t[:, 8, 0:8], A["l0_gate_bias"].rearrange("(a n) -> a n", a=1).to_broadcast([P, 8])
                         ).then_inc(consts_in, 16)
            first_units(A["l0_w_in"], SLOTS)
            for j in range(SLOTS, 2 * UPB["l0a"]):
                unit(A["l0_w_in"], j, j % UPB["l0a"], NB * (j // UPB["l0a"]))
            phase("l0a", None, 2, 1, 3, lambda i: [(A["l0_w_in"], i * 2 * NB + b * NB) for b in range(2)])
            tail("l0t", A["l0_w_in"], L0_GATES, 8)
            phase("l0b", None, 2, 0, 4, lambda i: [(A["l0_w_in"], i * 2 * NB + (L0_GATES + 8 + b * NB)) for b in range(2)])
            sp.dma_start(mnorm[:], A["l0_mlstm_norm"].rearrange("(a n) -> a n", a=1).to_broadcast([P, MH * MDV])
                         ).then_inc(consts_in, 16)
            phase("out0", None, 2, 0, 2, lambda i: [(A["l0_w_out"], i * 2 * NB + b * NB) for b in range(2)])
            phase("gu0", None, 2, 0, FF // NB, lambda i: [(A["l0_w_gate"], i * NB), (A["l0_w_up"], i * NB)])
            phase("dn0", None, 2, 0, 2, lambda i: [(A["l0_w_down"], i * 2 * NB + b * NB) for b in range(2)])
            tail("l1t", A["l1_w_in"], L1_GATES, 64)
            sp.wait_ge(unit_used, UNIT0["l1t"])
            sp.dma_start(gnorm[:], A["l1_gdn_norm"].rearrange("(a n) -> a n", a=1).to_broadcast([P, GD])
                         ).then_inc(l1_const, 16)
            sp.dma_start(conv_w[:], A["conv"].rearrange("p (c w) -> p c w", w=CW)).then_inc(l1_const, 16)
            for n, g in enumerate(("l1_a_log", "l1_dt_bias")):
                sp.dma_start(gate_t[:, 8, 32 * n:32 * n + 32], A[g].rearrange("(a n) -> a n", a=1).to_broadcast([P, 32])
                             ).then_inc(l1_const, 16)
            w1 = A["l1_w_in"]
            phase("l1r", None, 6, 0, ROUNDS, lambda i: [(w1, i * NB), (w1, i * NB + 2048), (w1, i * 2 * NB + 4096),
                                                        (w1, i * 2 * NB + 4096 + NB), (w1, i * 2 * NB + 8192),
                                                        (w1, i * 2 * NB + 8192 + NB)])
            phase("out1", None, 2, 0, 2, lambda i: [(A["l1_w_out"], i * 2 * NB + b * NB) for b in range(2)])
            phase("gu1", None, 2, 0, FF // NB, lambda i: [(A["l1_w_gate"], i * NB), (A["l1_w_up"], i * NB)])
            sp.wait_ge(unit_used, UNIT0["dn1"])
            sp.dma_start(fgain[:], A["final_norm"].rearrange("(a n) -> a n", a=1).to_broadcast([P, D])
                         ).then_inc(consts_in, 16)
            phase("dn1", None, 2, 0, 2, lambda i: [(A["l1_w_down"], i * 2 * NB + b * NB) for b in range(2)])
            for m in range(M):
                sp.wait_ge(epi_step, m + 1)
                sp.dma_start(out[m * P:(m + 1) * P, :], x[:, m, :]).then_inc(out_done, 16)
            sp.wait_ge(out_done, 16 * M)

        @block.gpsimd
        def _(pool):
            def keep_x(name):
                with pool.Fori(0, 2) as i:
                    for b in range(2):
                        pool.wait_ge(acc_read[b], i + (BLOCK0[name] // 2 + 1))
                        nc.gpsimd.tensor_copy(x[:, :, bass.ds(i * 2 * NB + b * NB, NB)], xs[:]).then_inc(xs_copied, 1)

            for name in NORM_OF:
                keep_x(name)

        @block.tensor
        def _(pe):
            def products(pair, k, k_last, hi, lo, slot, kk, width, stride, first):
                for m in range(M):
                    tok = slice(m * P, (m + 1) * P)
                    o = pair[m]
                    a, b = hi[:, k, tok], lo[:, k, tok]
                    wh = whi[:, slot, kk * stride:kk * stride + width]
                    wl = wlo[:, slot, kk * stride:kk * stride + width]
                    nc.tensor.matmul(o, a, wh, start=first, stop=False)
                    nc.tensor.matmul(o, a, wl, start=False, stop=False)
                    mm = nc.tensor.matmul(o, b, wh, start=False, stop=k_last)
                return mm

            def gemm_block(name, base_u, base_b, hi, lo, slot0, parity, midway=None, fresh=False):
                upb = UPB[name]
                if not fresh:
                    pe.wait_ge(acc_read[parity], base_b)
                for j in range(upb):
                    pe.wait_ge(lo_done, base_u + (j + 1))
                    for kk in range(2):
                        k = 2 * j + kk
                        mm = products([acc[parity][:, m, :] for m in range(M)], k, k == 2 * upb - 1, hi, lo,
                                      (slot0 + j) % SLOTS, kk, NB, NB, k == 0)
                    mm.then_inc(unit_used, 1)
                    if j == 3 and midway is not None:
                        midway()

            def tail(name, hi, lo, width):
                for j in range(4):
                    pe.wait_ge(lo_done, UNIT0[name] + j + 1)
                    for kk in range(4):
                        k = 4 * j + kk
                        mm = products([aux4[2 + m][:, 0:width] for m in range(M)], k, k == KT - 1, hi, lo, j, kk,
                                      width, width, k == 0)
                    mm.then_inc(unit_used, 1)

            def transposes(src, dst, n):
                for t in range(n):
                    for m in range(M):
                        mm = nc.tensor.transpose(dst[:, t * SEQ + m * P:t * SEQ + (m + 1) * P],
                                                 src(m, t), ident)
                return mm

            def x_block(n_done, src):
                transposes(src, aux[0], 4).then_inc(xt_ready, 1)

            def body(name, i, lo_b, n_body, hi, lo, midways, fresh=()):
                for b in range(n_body):
                    upb = UPB[name]
                    gemm_block(name, i * (n_body * upb) + (UNIT0[name] + b * upb),
                               i * (n_body // 2) + (BLOCK0[name] + b) // 2, hi, lo, b * upb, b % 2,
                               midways[b], fresh=b in fresh)

            xs_tile = lambda m, t: xs[:, m, t * P:(t + 1) * P]
            prod_tile = lambda m, t: prod[:, m, t * P:(t + 1) * P]

            def residual_phase(name, hi, lo, transposed):
                done = 4 * (NORM_OF[name] - 1)

                def xt(i, b):
                    def f():
                        pe.wait_ge(acc_read[1 - b], i + (BLOCK0[name] // 2 + b))
                        pe.wait_ge(xlo_done, i * 2 + (done + b + 3))
                        transposes(xs_tile, aux[0], 4).then_inc(xt_ready, 1)
                    return f if transposed else None
                body(name, 0, 0, 2, hi, lo, [None, xt(0, 1)])
                with pe.Fori(1, 2) as i:
                    body(name, i, 0, 2, hi, lo, [xt(i, 0), xt(i, 1)])
                if transposed:
                    xt(2, 0)()

            def ffn(name, down, n0):
                def tr(i):
                    def f():
                        pe.wait_ge(acc_read[1], i + BLOCK0[name] // 2)
                        if n0 or not isinstance(i, int) or i > 1:
                            pe.wait_ge(flo_done, i + (n0 - 1))
                        transposes(prod_tile, aux[1], 4).then_inc(ft_ready, 1)
                    return f
                body(name, 0, 0, 2, hT_hi, hT_lo, [None, None])
                body(name, 1, 0, 2, hT_hi, hT_lo, [tr(1), None])
                with pe.Fori(2, FF // NB) as i:
                    body(name, i, 0, 2, hT_hi, hT_lo, [tr(i), None])
                tr(FF // NB)()
                pe.wait_ge(flo_done, n0 + FF // NB)


            def l0(name):
                pe.wait_ge(l0_step, L0_AT[name])

            def l0_mixer():
                for b in range(2):
                    pe.wait_ge(acc_read[b], BLOCK0["out0"] // 2)
                l0("log1p")
                for dst, col in ((aux[0], QM), (aux[1], KM)):
                    mm = transposes(lambda m, t: pr[:, m, col + t * P:col + (t + 1) * P], dst, MH)
                mm.then_inc(l0_step, 1)
                for h in range(MH):
                    l0(f"m{h}_rows")
                    rows = d_rows[:, :, :].rearrange("p a b -> p (a b)")
                    nc.tensor.matmul(aux4[0][:, 0:P], C["upto"], rows[:, 0:P], start=True, stop=False)
                    nc.tensor.matmul(aux4[0][:, 0:P], C["ones"], rows[:, 5 * P:], start=False, stop=True)
                    nc.tensor.matmul(aux4[0][:, P:3 * P], C["upto"], rows[:, P:3 * P], start=True, stop=False)
                    nc.tensor.matmul(aux4[0][:, P:3 * P], C["ones"], rows[:, 3 * P:5 * P], start=False, stop=True
                                     ).then_inc(l0_step, 1)
                    l0(f"m{h}_d_exp")
                    nc.tensor.matmul(aux4[2][:, 0:P], qmT[:, h, 0:P], kmT[:, h, 0:P], start=True, stop=True)
                    nc.tensor.matmul(aux4[2][:, P:3 * P], qmT[:, h, P:], kmT[:, h, :], start=True, stop=True
                                     ).then_inc(l0_step, 1)
                    l0(f"m{h}_s_prod")
                    for i in range(3):
                        mm = nc.tensor.transpose(aux4[0][:, i * P:(i + 1) * P], d_sb[:, i * P:(i + 1) * P], ident)
                    mm.then_inc(l0_step, 1)
                    l0(f"m{h}_st_copy")
                    weighted_values(st_sb, VM + h * MDV).then_inc(l0_step, 1)
                for i in range(2 * M):
                    l0(f"rot{i}_mul")
                    for t in range(2 * RH):
                        mm = nc.tensor.transpose(aux[i % 2][:, t * P:(t + 1) * P], rot[:, t // 2, t % 2, :], ident)
                    mm.then_inc(l0_step, 1)
                for h in range(RH):
                    l0("rot3_copy" if h == 0 else f"r{h - 1}_o_copy")
                    for d in range(2):
                        nc.tensor.matmul(aux4[0][:, 0:SEQ], krT[:, 2 * h + d, 0:P], qrT[:, 2 * h + d, :],
                                         start=d == 0, stop=d == 1)
                    for d in range(2):
                        mm = nc.tensor.matmul(aux4[0][:, SEQ:3 * P], krT[:, 2 * h + d, P:], qrT[:, 2 * h + d, P:],
                                              start=d == 0, stop=d == 1)
                    mm.then_inc(l0_step, 1)
                    l0(f"r{h}_s_dec")
                    weighted_values(rs_sb, VR + h * RD).then_inc(l0_step, 1)
                for g in range(4):
                    l0("r_norm" if g == 0 else f"mix{g - 1}_lo")
                    base = (VM if g < 2 else VR) + (g % 2) * 4 * P
                    transposes(lambda m, t: pr[:, m, base + t * P:base + (t + 1) * P], aux[g % 2], 4).then_inc(l0_step, 1)

            def weighted_values(st, col):
                v = [pr[:, m, col:col + 256] for m in range(M)]
                nc.tensor.matmul(aux4[2][:, 0:256], st[:, 0:P], v[0], start=True, stop=True)
                nc.tensor.matmul(aux4[2][:, 256:512], st[:, P:2 * P], v[0], start=True, stop=False)
                return nc.tensor.matmul(aux4[2][:, 256:512], st[:, 2 * P:3 * P], v[1], start=False, stop=True)

            def gdn_gates():
                pe.wait_ge(gate_step, GATE_AT["log1p"])
                la = gate_t[:, 1, :]
                nc.tensor.matmul(aux4[2][:, 0:64], C["upto"], la, start=True, stop=True)
                nc.tensor.matmul(aux4[3][:, 0:64], C["after"], la, start=True, stop=True).then_inc(gate_step, 1)

            def gdn(r):
                def at(name):
                    pe.wait_ge(gdn_step, r * GDN_N + GDN_AT[name])

                def done(mm):
                    mm.then_inc(gdn_step, 1)

                for b in range(4):
                    at("round" if b == 0 else f"c{b - 1}_silu")
                    done(transposes(lambda m, t: qkv[:, m, (4 * b + t) * P:(4 * b + t + 1) * P], aux[0], 4))
                for b in range(2):
                    at(f"n{b}_sq")
                    for i in range(2):
                        mm = nc.tensor.matmul(aux4[i], C["ones"], sq[:, 2 * i:2 * i + 2, :].rearrange("p a b -> p (a b)"),
                                              start=True, stop=True)
                    done(mm)
                for name, prev, src in (("k", "n1_mul", lambda t: qkT[:, 4 + t, :]), ("v0", "k_copy", lambda t: vT[:, t, :]),
                                        ("v1", "v0_copy", lambda t: vT[:, 4 + t, :])):
                    at(prev)
                    for m in range(M):
                        for t in range(4):
                            mm = nc.tensor.transpose(aux[0][:, m * NB + t * P:m * NB + (t + 1) * P],
                                                     src(t)[:, m * P:(m + 1) * P], ident)
                    done(mm)
                prev = "v1_copy"
                for c in range(M):
                    tok = slice(c * P, (c + 1) * P)
                    at(prev)
                    for h in range(HQ):
                        k, q = qkT[:, 4 + h, tok], qkT[:, h, tok]
                        nc.tensor.matmul(aux[0][:, 2 * h * P:(2 * h + 1) * P], k, k, start=True, stop=True)
                        mm = nc.tensor.matmul(aux[0][:, (2 * h + 1) * P:(2 * h + 2) * P], k, q, start=True, stop=True)
                    done(mm)
                    for g in range(2):
                        u = f"k{c}_g{g}_"
                        col = lambda h: slice(h * P, (h + 1) * P)
                        at(u + "lam")
                        nc.tensor.matmul(aux4[0], C["upto"], lam[:, :, :].rearrange("p a b -> p (a b)"), start=True, stop=True)
                        for h in range(4):
                            mm = nc.tensor.matmul(aux4[1][:, col(h)], lam[:, h, :], C["upto"], start=True, stop=True)
                        done(mm)
                        for n in range(len(LEVELS)):
                            at(u + f"l{n}_b")
                            for h in range(4):
                                mm = nc.tensor.matmul(aux4[2][:, col(h)], Bm[:, h, :], TT[:, h, :] if n else ident,
                                                      start=True, stop=True)
                            done(mm)
                            if n:
                                at(u + f"l{n}_q")
                                for h in range(4):
                                    if n < LAST:
                                        nc.tensor.matmul(aux4[0][:, col(h)], Q1[:, h, :], T[:, h, :], start=True, stop=True)
                                    mm = nc.tensor.matmul(aux4[1][:, col(h)], T[:, h, :], Q1[:, h, :], start=True, stop=True)
                                done(mm)
                        if c:
                            at(u + f"l{LAST}_t")
                            for h in range(4):
                                s = St[:, 4 * g + h, :]
                                nc.tensor.matmul(aux4[0][:, col(h)], qkT[:, 4 + 2 * g + h // 2, tok], s, start=True, stop=True)
                                mm = nc.tensor.matmul(aux4[1][:, col(h)], qkT[:, 2 * g + h // 2, tok], s, start=True, stop=True)
                            done(mm)
                        at(u + "res")
                        for h in range(4):
                            mm = nc.tensor.matmul(aux4[2][:, col(h)], TT[:, h, :], Rm[:, h, :], start=True, stop=True)
                        done(mm)
                        at(u + "vn")
                        for h in range(4):
                            if not c:
                                nc.tensor.matmul(aux4[0][:, col(h)], k_tail[:, h, :], Vn[:, h, :], start=True, stop=True)
                            mm = nc.tensor.matmul(aux4[3][:, col(h)], ET[:, h, :], Vn[:, h, :], start=True, stop=True)
                        done(mm)
                    prev = f"k{c}_g1_s_copy"

            pe.wait_ge(x_in, 16)
            pe.wait_ge(consts_in, 16 * 4)
            for n in range(4):
                if n:
                    pe.wait_ge(xlo_done, n)
                transposes(lambda m, t: x[:, m, n * NB + t * P:n * NB + (t + 1) * P], aux[0], 4).then_inc(xt_ready, 1)
            pe.wait_ge(xlo_done, 4)
            body("l0a", 0, 0, 2, hT_hi, hT_lo, [None, None], fresh=(0, 1))
            with pe.Fori(1, 3) as i:
                body("l0a", i, 0, 2, hT_hi, hT_lo, [None, None])
            tail("l0t", hT_hi, hT_lo, 8)
            with pe.Fori(0, 4) as i:
                body("l0b", i, 0, 2, hT_hi, hT_lo, [None, None])

            l0_mixer()
            pe.wait_ge(l0_step, L0_AT["mix3_lo"])
            residual_phase("out0", mixT_hi, mixT_lo, True)
            pe.wait_ge(xlo_done, 8)
            ffn("gu0", "dn0", 0)
            residual_phase("dn0", fT_hi, fT_lo, True)
            pe.wait_ge(xlo_done, 12)
            tail("l1t", hT_hi, hT_lo, 64)
            gdn_gates()
            with pe.Fori(0, ROUNDS) as r:
                body("l1r", r, 0, 6, hT_hi, hT_lo, [None] * 6)
                gdn(r)
            pe.wait_ge(gdn_step, ROUNDS * GDN_N + 1)
            for g in range(8):
                if g >= 2:
                    pe.wait_ge(o_lo, g - 1)
                transposes(lambda m, t: o_all[:, m, (4 * g + t) * P:(4 * g + t + 1) * P], aux[g % 2], 4).then_inc(o_tr, 1)
            pe.wait_ge(o_lo, 8)
            residual_phase("out1", oT_hi, oT_lo, True)
            pe.wait_ge(xlo_done, 16)
            ffn("gu1", "dn1", FF // NB)
            residual_phase("dn1", fT_hi, fT_lo, False)

        @block.scalar
        def _(act):
            def body(name, i, n_body, hook):
                upb = UPB[name]
                for b in range(n_body):
                    for j in range(upb):
                        w = b * upb + j
                        s = w % SLOTS
                        act.wait_ge(raw_in[s], i * (n_body * upb // SLOTS * 16) + 16 * ((UNIT0[name] + w) // SLOTS + 1))
                        if not (isinstance(i, int) and i * n_body * upb + UNIT0[name] + w < SLOTS):
                            act.wait_ge(unit_used, i * (n_body * upb) + (UNIT0[name] + w - SLOTS + 1))
                        nc.scalar.activation(whi[:, s, :], wraw[:, s, :], ACT.Copy).then_inc(hi_done, 1)
                        hook(i, b, j)

            def tail(name, width):
                for j in range(4):
                    act.wait_ge(raw_in[j], 16 * ((UNIT0[name] + j) // SLOTS + 1))
                    act.wait_ge(unit_used, UNIT0[name] + j - SLOTS + 1)
                    nc.scalar.activation(whi[:, j, 0:4 * width], wraw[:, j, 0:4 * width], ACT.Copy).then_inc(hi_done, 1)

            def copy_out(name, n, parity, dst, func=ACT.Copy):
                act.wait_ge(unit_used, n * UPB[name] + (UNIT0[name] + UPB[name]))
                for m in range(M):
                    a = nc.scalar.activation(dst(m), acc[parity][:, m, :], func, scale=rstd[:, m:m + 1])
                return a.then_inc(acc_read[parity], 1)

            def root(norm):
                act.wait_ge(mean_done, norm + 1)
                nc.scalar.activation(rms[:], mean[:], ACT.Sqrt, bias=epsc[:, 0:1], scale=1.0 / D).then_inc(rms_done, 1)
                act.wait_ge(rstd_done, norm + 1)

            def x_block(norm, n, src):
                k = n + 4 * norm
                act.drain()
                for m in range(M):
                    a = nc.scalar.activation(aux[1][:, m * NB:(m + 1) * NB], src(m), ACT.Square,
                                             accum_out=ssq[:, m, bass.ds(n, 1)])
                if norm < 4:
                    act.wait_ge(xt_ready, k + 1)
                    for t in range(4):
                        a = nc.scalar.activation(hT_hi[:, bass.ds(n * 4 + t, 1), :].rearrange("p a b -> p (a b)"),
                                                 aux[0][:, t * SEQ:(t + 1) * SEQ], ACT.Copy,
                                                 scale=gains[:, norm, bass.ds(n * 4 + t, 1)])
                a.then_inc(xhi_done, 1)

            def residual_phase(name):
                norm = NORM_OF[name]

                def hook(i, b, j):
                    if j == 7 and not (b == 0 and isinstance(i, int) and i == 0):
                        n = i * 2 + (b - 1)
                        act.wait_ge(acc_read[1 - b], i + (BLOCK0[name] // 2 + b))
                        x_block(norm, n, lambda m: xs[:, m, :])
                body(name, 0, 2, hook)
                with act.Fori(1, 2) as i:
                    body(name, i, 2, hook)
                act.wait_ge(acc_read[1], BLOCK0[name] // 2 + 2)
                x_block(norm, 3, lambda m: xs[:, m, :])

            def ffn(name, norm, n0):
                def f_hi(i):
                    act.wait_ge(ft_ready, i + n0)
                    nc.scalar.activation(fT_hi[:, bass.ds(i * 4 - 4, 4), :].rearrange("p a b -> p (a b)"), aux[1][:, :], ACT.Copy
                                         ).then_inc(fhi_done, 1)

                def hook(i, b, j):
                    first = isinstance(i, int) and i == 0
                    if first and b == 0 and j == 1:
                        root(norm)
                    if b == 1 and j == 3:
                        if not (first and n0 == 0):
                            act.wait_ge(acc_read[1], i + BLOCK0[name] // 2)
                        copy_out(name, i * 2, 0, lambda m: sg[:, m, :], ACT.Silu)
                    if b == 0 and j == 7 and not first:
                        f_hi(i)
                body(name, 0, 2, hook)
                with act.Fori(1, FF // NB) as i:
                    body(name, i, 2, hook)
                f_hi(FF // NB)

            act.wait_ge(x_in, 16)
            act.wait_ge(consts_in, 16 * 4)
            act.wait_ge(eps_set, 1)
            for n in range(4):
                x_block(0, n, lambda m: x[:, m, n * NB:(n + 1) * NB])

            def hook_a(i, b, j):
                first = isinstance(i, int) and i == 0 and b == 0
                if first and j == 1:
                    root(0)
                if j == 3 and not first:
                    copy_out("l0a", i * 2 + (b - 1), (b + 1) % 2, lambda m: pr[:, m, bass.ds(i * 2 * NB + (b - 1) * NB, NB)])

            def hook_b(i, b, j):
                if j == 3 and not (isinstance(i, int) and i == 0 and b == 0):
                    copy_out("l0b", i * 2 + (b - 1), (b + 1) % 2,
                             lambda m: pr[:, m, bass.ds(i * 2 * NB + (QR + (b - 1) * NB), NB)])
            body("l0a", 0, 2, hook_a)
            with act.Fori(1, 3) as i:
                body("l0a", i, 2, hook_a)
            tail("l0t", 8)
            copy_out("l0a", 5, 1, lambda m: pr[:, m, 5 * NB:6 * NB])
            body("l0b", 0, 2, hook_b)
            with act.Fori(1, 4) as i:
                body("l0b", i, 2, hook_b)
            copy_out("l0b", 7, 1, lambda m: pr[:, m, QR + 7 * NB:QR + 8 * NB])

            def l0(name):
                act.wait_ge(l0_step, L0_AT[name])

            def done(a):
                a.then_inc(l0_step, 1)

            g8 = gate_t[:, 0, 0:16]
            l0("gates")
            done(nc.scalar.activation(g8, g8, ACT.Tanh, scale=1.0 / SOFTCAP))
            l0("cap")
            done(nc.scalar.activation(gate_t[:, 2, 0:8], gate_t[:, 2, 0:8], ACT.Exp, scale=-1.0))
            l0("m_tr")
            nc.scalar.activation(qmT[:, :, :].rearrange("p a b -> p (a b)"), aux[0][:, :], ACT.Copy)
            done(nc.scalar.activation(kmT[:, :, :].rearrange("p a b -> p (a b)"), aux[1][:, :], ACT.Copy))
            for h in range(MH):
                l0(f"m{h}_d_max")
                nc.scalar.activation(p_sb[:, 0:P], d_sb[:, 0:P], ACT.Exp, bias=gate_t[:, 5, 0:1])
                nc.scalar.activation(p_sb[:, P:3 * P], d_sb[:, P:3 * P], ACT.Exp, bias=gate_t[:, 5, 1:2])
                done(nc.scalar.activation(gate_t[:, 5, 2:4], gate_t[:, 5, 0:2], ACT.Exp))
                l0(f"m{h}_st_psum")
                done(nc.scalar.activation(st_sb[:], aux4[0][:, 0:3 * P], ACT.Copy))
            l0(f"m{MH - 1}_num_div")
            for h in range(MH):
                for m in range(M):
                    nc.scalar.activation(aux4[1][:, 0:256], pr[:, m, VM + h * MDV:VM + (h + 1) * MDV], ACT.Square,
                                         accum_out=gate_t[:, 6, h * 2 + m:h * 2 + m + 1])
                    act.drain()
            nc.scalar.activation(gate_t[:, 6, 8:16], gate_t[:, 6, 0:8], ACT.Sqrt, bias=epsc[:, 0:1], scale=1.0 / MDV)
            done(nc.scalar.activation(pr[:, :, OM:OM + 1024], pr[:, :, OM:OM + 1024], ACT.Sigmoid))
            l0("pos")
            done(nc.scalar.activation(cs[:].rearrange("p a b c -> p (a b c)"), ang[:].rearrange("p a b c -> p (a b c)"), ACT.Sin))
            for i in range(2 * M):
                l0(f"rot{i}_tr")
                dst = (qrT, krT)[i // M]
                m = i % M
                done(nc.scalar.activation(dst[:, :, m * P:(m + 1) * P], aux[i % 2][:, :].rearrange("p (a b) -> p a b", b=P), ACT.Copy))
            for h in range(RH):
                l0(f"r{h}_o_psum")
                done(nc.scalar.activation(pr[:, :, VR + h * RD:VR + (h + 1) * RD], aux4[2].rearrange("p (m n) -> p m n", m=M), ACT.Copy))
            act.drain()
            for h in range(RH):
                for m in range(M):
                    nc.scalar.activation(aux4[1][:, 0:256], pr[:, m, VR + h * RD:VR + (h + 1) * RD], ACT.Square,
                                         accum_out=gate_t[:, 6, h * 2 + m:h * 2 + m + 1])
                    act.drain()
            nc.scalar.activation(gate_t[:, 6, 8:16], gate_t[:, 6, 0:8], ACT.Sqrt, bias=epsc[:, 0:1], scale=1.0 / RD)
            done(nc.scalar.activation(pr[:, :, GR:GR + 1024], pr[:, :, GR:GR + 1024], ACT.Silu))
            for g in range(4):
                l0(f"mix{g}_tr")
                done(nc.scalar.activation(mixT_hi[:, 4 * g:4 * g + 4, :].rearrange("p a b -> p (a b)"), aux[g % 2][:, :], ACT.Copy))

            residual_phase("out0")
            ffn("gu0", 1, 0)
            residual_phase("dn0")

            tail("l1t", 64)
            root(2)
            act.wait_ge(l1_const, 16 * 4)
            act.wait_ge(gate_step, GATE_AT["raw"])
            nc.scalar.activation(gate_t[:, 2, :], gate_t[:, 2, :], ACT.Exp, scale=-1.0)
            nc.scalar.activation(gate_t[:, 8, 0:32], gate_t[:, 8, 0:32], ACT.Exp)
            nc.scalar.activation(gate_t[:, 0, :], gate_t[:, 0, :], ACT.Sigmoid).then_inc(gate_step, 1)
            act.wait_ge(gate_step, GATE_AT["sums"])
            nc.scalar.activation(gate_t[:, 4, :], aux4[2][:, 0:64], ACT.Exp)
            nc.scalar.activation(gate_t[:, 5, :], aux4[3][:, 0:64], ACT.Exp).then_inc(gate_step, 1)

            def gdn(r):
                def at(name):
                    act.wait_ge(gdn_step, r * GDN_N + GDN_AT[name])

                def done(a):
                    a.then_inc(gdn_step, 1)

                flat = lambda t: t.rearrange("p a b -> p (a b)")
                for b in range(4):
                    at(f"c{b}_x_tr")
                    dst = (qkT[:, 0:4], qkT[:, 4:8], vT[:, 0:4], vT[:, 4:8])[b]
                    for t in range(4):
                        a = nc.scalar.activation(dst[:, t, :], aux[0][:, t * SEQ:(t + 1) * SEQ], ACT.Copy,
                                                 scale=conv_r[:, 4 * b + t, CW - 1:CW])
                    done(a)
                    at(f"c{b}_conv")
                    done(nc.scalar.activation(flat(dst), flat(dst), ACT.Silu))
                act.drain()
                for b in range(2):
                    if b:
                        at("n0_mul")
                    blk = flat(qkT[:, 4 * b:4 * b + 4, :])
                    done(nc.scalar.activation(flat(sq[:]), blk, ACT.Square))
                    at(f"n{b}_sum")
                    done(nc.scalar.activation(flat(rn[:]), aux[0][:, :], ACT.Sqrt, bias=epsc[:, 1 - b:2 - b],
                                              scale=1.0 if b else float(GD)))
                for name, dst in (("k", flat(k_tok[:])), ("v0", v_tok[:, :, 0:NB]), ("v1", v_tok[:, :, NB:])):
                    at(name + "_tr")
                    src = aux[0][:, :] if name == "k" else aux[0][:, :].rearrange("p (m n) -> p m n", m=M)
                    done(nc.scalar.activation(dst, src, ACT.Copy))
                for c in range(M):
                    for g in range(2):
                        u = f"k{c}_g{g}_"
                        at(u + "d_psum")
                        nc.scalar.activation(flat(EA[:]), aux4[0], ACT.Exp)
                        done(nc.scalar.activation(flat(ET[:]), aux4[1], ACT.Exp))
                        for n in range(1, len(LEVELS)):
                            at(u + f"l{n}_q_psum")
                            done(nc.scalar.activation(flat(Q1[:]), aux4[2], ACT.Copy))
                        at(u + "vn_psum")
                        done(nc.scalar.activation(flat(Vn[:]), aux4[2], ACT.Copy))
                        if not c:
                            at(u + "o")
                            done(nc.scalar.activation(flat(St[:, 4 * g:4 * g + 4, :]), aux4[0], ACT.Copy))
                at("k1_g1_o")
                for m in range(M):
                    a = nc.scalar.activation(flat(o_sq[:, m]), o_all[:, m, bass.ds(r * 1024, 1024)], ACT.Square)
                done(a)
                at("o_sum")
                done(nc.scalar.activation(o_ms[:].rearrange("p a b -> p (a b)"), o_ms[:].rearrange("p a b -> p (a b)"), ACT.Sqrt,
                                          bias=epsc[:, 0:1], scale=1.0 / GD))

            def hook_r(r, b, j):
                if b == 1 and j == 3:
                    act.wait_ge(gdn_step, r * GDN_N + 1)
                if j == 3 and b:
                    round_out(r, b - 1)

            def round_out(r, b):
                if b < 4:
                    copy_out("l1r", r * 6 + b, b % 2, lambda m: qkv[:, m, b * NB:(b + 1) * NB])
                else:
                    copy_out("l1r", r * 6 + b, b % 2, lambda m: zs[:, m, (b - 4) * NB:(b - 3) * NB], ACT.Silu)

            act.wait_ge(xs_copied, 8)
            with act.Fori(0, ROUNDS) as r:
                body("l1r", r, 6, hook_r)
                round_out(r, 5)
                gdn(r)
            for g in range(8):
                act.wait_ge(o_tr, g + 1)
                nc.scalar.activation(oT_hi[:, 4 * g:4 * g + 4, :].rearrange("p a b -> p (a b)"), aux[g % 2][:, :], ACT.Copy
                                     ).then_inc(o_hi, 1)
            residual_phase("out1")
            ffn("gu1", 3, FF // NB)
            residual_phase("dn1")
            root(4)

        @block.vector
        def _(dve):
            V = nc.vector

            def body(name, i, n_body, hook):
                upb = UPB[name]
                for b in range(n_body):
                    for j in range(upb):
                        w = b * upb + j
                        s = w % SLOTS
                        dve.wait_ge(hi_done, i * (n_body * upb) + (UNIT0[name] + w + 1))
                        if not (isinstance(i, int) and i * n_body * upb + UNIT0[name] + w < SLOTS):
                            dve.wait_ge(unit_used, i * (n_body * upb) + (UNIT0[name] + w - SLOTS + 1))
                        V.tensor_tensor(wlo[:, s, :], wraw[:, s, :], whi[:, s, :].bitcast(F32), ALU.subtract).then_inc(lo_done, 1)
                        hook(i, b, j)

            def tail(name, width):
                for j in range(4):
                    dve.wait_ge(hi_done, UNIT0[name] + j + 1)
                    dve.wait_ge(unit_used, UNIT0[name] + j - SLOTS + 1)
                    V.tensor_tensor(wlo[:, j, 0:4 * width], wraw[:, j, 0:4 * width], whi[:, j, 0:4 * width].bitcast(F32),
                                    ALU.subtract).then_inc(lo_done, 1)

            def recip(norm):
                dve.wait_ge(rms_done, norm + 1)
                V.reciprocal(rstd[:], rms[:]).then_inc(rstd_done, 1)
                dve.drain()

            def x_lo(norm, n):
                dve.wait_ge(xhi_done, n + (4 * norm + 1))
                if norm < 4:
                    for t in range(4):
                        a = V.scalar_tensor_tensor(
                            hT_lo[:, bass.ds(n * 4 + t, 1), :].rearrange("p a b -> p (a b)"),
                            aux[0][:, t * SEQ:(t + 1) * SEQ], gains[:, norm, bass.ds(n * 4 + t, 1)],
                            hT_hi[:, bass.ds(n * 4 + t, 1), :].rearrange("p a b -> p (a b)").bitcast(F32),
                            op0=ALU.mult, op1=ALU.subtract)
                    a.then_inc(xlo_done, 1)

            def mean_square():
                V.tensor_reduce(mean[:], ssq[:], AX.X, ALU.add).then_inc(mean_done, 1)

            def residual_phase(name):
                norm = NORM_OF[name]

                def add(n, parity):
                    dve.wait_ge(unit_used, n * UPB[name] + (UNIT0[name] + UPB[name]))
                    if not (norm == 1 and isinstance(n, int) and n == 0):
                        dve.wait_ge(xs_copied, n + 4 * (norm - 1))
                    dve.wait_ge(xhi_done, n + 4 * norm)
                    V.tensor_tensor(xs[:], acc[parity][:, :, :], x[:, :, bass.ds(n * NB, NB)], ALU.add
                                    ).then_inc(acc_read[parity], 1)

                def hook(i, b, j):
                    if b == 0 and isinstance(i, int) and i == 0:
                        return
                    if j == 3:
                        add(i * 2 + (b - 1), (b + 1) % 2)
                    if j == 7:
                        x_lo(norm, i * 2 + (b - 1))
                body(name, 0, 2, hook)
                with dve.Fori(1, 2) as i:
                    body(name, i, 2, hook)
                add(3, 1)
                x_lo(norm, 3)
                mean_square()

            def ffn(name, norm, n0):
                def up(i):
                    dve.wait_ge(acc_read[0], i + BLOCK0[name] // 2)
                    dve.wait_ge(unit_used, i * (2 * UPB[name]) + UNIT0[name])
                    if isinstance(i, int) and i == 1:
                        dve.wait_ge(xs_copied, 4 * norm)
                    else:
                        dve.wait_ge(ft_ready, i + (n0 - 1))
                    for m in range(M):
                        a = V.scalar_tensor_tensor(prod[:, m, :], acc[1][:, m, :], rstd[:, m:m + 1], sg[:, m, :],
                                                   op0=ALU.mult, op1=ALU.mult)
                    a.then_inc(acc_read[1], 1)

                def f_lo(i):
                    dve.wait_ge(fhi_done, i + n0)
                    V.tensor_tensor(fT_lo[:, bass.ds(i * 4 - 4, 4), :].rearrange("p a b -> p (a b)"), aux[1][:, :],
                                    fT_hi[:, bass.ds(i * 4 - 4, 4), :].rearrange("p a b -> p (a b)").bitcast(F32), ALU.subtract
                                    ).then_inc(flo_done, 1)

                def hook(i, b, j):
                    first = isinstance(i, int) and i == 0
                    if first and b == 0 and j == 1:
                        recip(norm)
                    if b == 0 and not first:
                        if j == 3:
                            up(i)
                        if j == 7:
                            f_lo(i)
                body(name, 0, 2, hook)
                body(name, 1, 2, hook)
                with dve.Fori(2, FF // NB) as i:
                    body(name, i, 2, hook)
                up(FF // NB)
                f_lo(FF // NB)

            def log1p(dst, y, w):
                z, z2, p = (gate_t[:, k, 0:w] for k in (5, 6, 7))
                V.tensor_scalar(z, y, 2.0, None, ALU.add)
                dve.drain()
                V.reciprocal(z, z)
                dve.drain()
                V.tensor_tensor(z, z, y, ALU.mult)
                dve.drain()
                V.tensor_tensor(z2, z, z, ALU.mult)
                dve.drain()
                V.tensor_scalar(p, z2, 1.0 / 15, None, ALU.mult)
                for k in (13, 11, 9, 7, 5, 3):
                    dve.drain()
                    V.scalar_tensor_tensor(p, p, 1.0 / k, z2, op0=ALU.add, op1=ALU.mult)
                dve.drain()
                V.scalar_tensor_tensor(p, p, 1.0, z, op0=ALU.add, op1=ALU.mult)
                dve.drain()
                V.tensor_scalar(dst, p, 2.0, None, ALU.mult)
                dve.drain()

            V.memset(epsc[:, 0:1], EPS)
            V.memset(epsc[:, 1:2], GD * EPS).then_inc(eps_set, 1)
            dve.wait_ge(consts_in, 16 * 4)
            for n in range(4):
                x_lo(0, n)
            mean_square()
            nothing = lambda i, b, j: None
            body("l0a", 0, 2, lambda i, b, j: recip(0) if b == 0 and j == 1 else None)
            with dve.Fori(1, 3) as i:
                body("l0a", i, 2, nothing)
            tail("l0t", 8)
            with dve.Fori(0, 4) as i:
                body("l0b", i, 2, nothing)

            def l0(name):
                dve.wait_ge(l0_step, L0_AT[name])

            def done(a):
                a.then_inc(l0_step, 1)

            col = lambda k, a, b: gate_t[:, k, a:b]
            dve.wait_ge(unit_used, UNIT0["l0t"] + 4)
            for m in range(M):
                a = V.scalar_tensor_tensor(col(0, 8 * m, 8 * m + 8), aux4[2 + m][:, 0:8], rstd[:, m:m + 1], col(8, 0, 8),
                                           op0=ALU.mult, op1=ALU.add)
            done(a)
            l0("tanh")
            V.tensor_scalar(col(0, 0, 16), col(0, 0, 16), SOFTCAP, None, ALU.mult)
            dve.drain()
            fg = col(0, 0, 16).rearrange("p (m c) -> p m c", m=M)[:, :, 4:8]
            pair = lambda k: col(k, 0, 8).rearrange("p (m c) -> p m c", m=M)
            done(V.scalar_tensor_tensor(pair(2), fg, -1.0, fg, op0=ALU.mult, op1=ALU.max))
            l0("exp")
            log1p(col(3, 0, 8), col(2, 0, 8), 8)
            done(V.scalar_tensor_tensor(pair(4), fg, 0.0, pair(3), op0=ALU.min, op1=ALU.subtract))
            dve.drain()
            for h in range(MH):
                l0("m_trc" if h == 0 else f"m{h - 1}_num_div")
                lf = [col(4, 4 * m + h, 4 * m + h + 1) for m in range(M)]
                li = [col(0, 8 * m + h, 8 * m + h + 1) for m in range(M)]
                V.tensor_scalar(d_rows[:, 0, :], C["after"], lf[0], None, ALU.mult)
                V.tensor_scalar(d_rows[:, 1, :], C["ones"], lf[1], None, ALU.mult)
                V.tensor_scalar(d_rows[:, 2, :], C["after"], lf[1], None, ALU.mult)
                V.tensor_scalar(d_rows[:, 4, :], ident, li[1], None, ALU.mult)
                V.tensor_scalar(d_rows[:, 5, :], ident, li[0], None, ALU.mult)
                dve.drain()
                done(V.tensor_tensor(d_rows[:, 3, :], d_rows[:, 0, :], d_rows[:, 5, :], ALU.add))
                l0(f"m{h}_d_psum")
                V.tensor_tensor(d_sb[:], aux4[0][:, 0:3 * P], C["neg"], ALU.add)
                dve.drain()
                V.tensor_reduce(col(6, 0, 1), d_sb[:, 0:P], AX.X, ALU.max)
                V.tensor_reduce(col(6, 1, 2), d_sb[:, P:3 * P], AX.X, ALU.max)
                dve.drain()
                done(V.tensor_scalar(col(5, 0, 2), col(6, 0, 2), -1.0, None, ALU.mult))
                l0(f"m{h}_s_psum")
                V.scalar_tensor_tensor(d_sb[:, 0:P], aux4[2][:, 0:P], MDQK ** -0.5, p_sb[:, 0:P],
                                       op0=ALU.mult, op1=ALU.mult, accum_out=col(6, 2, 3))
                V.scalar_tensor_tensor(d_sb[:, P:3 * P], aux4[2][:, P:3 * P], MDQK ** -0.5, p_sb[:, P:3 * P],
                                       op0=ALU.mult, op1=ALU.mult, accum_out=col(6, 3, 4))
                dve.drain()
                V.scalar_tensor_tensor(col(6, 4, 6), col(6, 2, 4), -1.0, col(6, 2, 4), op0=ALU.mult, op1=ALU.max)
                dve.drain()
                V.tensor_tensor(col(6, 4, 6), col(6, 4, 6), col(5, 2, 4), ALU.max)
                dve.drain()
                done(V.reciprocal(col(6, 6, 8), col(6, 4, 6)))
                l0(f"m{h}_num_psum")
                for m in range(M):
                    a = V.tensor_scalar(pr[:, m, VM + h * MDV:VM + (h + 1) * MDV], aux4[2][:, m * 256:(m + 1) * 256],
                                        col(6, 6 + m, 7 + m), None, ALU.mult)
                done(a)

            def head_norm(base, gate_col, row):
                V.reciprocal(col(6, 16, 24), col(6, 8, 16))
                dve.drain()
                for h in range(4):
                    for m in range(M):
                        y = pr[:, m, base + h * 256:base + (h + 1) * 256]
                        s = col(6, 16 + 2 * h + m, 17 + 2 * h + m)
                        other = row[:, h * 256:(h + 1) * 256] if row is not None else pr[:, m, gate_col + h * 256:gate_col + (h + 1) * 256]
                        a = V.scalar_tensor_tensor(y, y, s, other, op0=ALU.mult, op1=ALU.mult)
                if row is not None:
                    dve.drain()
                    a = V.tensor_tensor(pr[:, :, base:base + 1024], pr[:, :, base:base + 1024],
                                        pr[:, :, gate_col:gate_col + 1024], ALU.mult)
                done(a)

            l0("m_sq")
            dve.wait_ge(consts_in, 16 * 5)
            head_norm(VM, OM, mnorm[:])
            V.tensor_copy(col(9, 2, 4), gate_t[:, 9, 0:2].bitcast(I32))
            dve.drain()
            for m in range(M):
                V.tensor_scalar(ang[:, 1, m, :], C["freq"], col(9, 2 + m, 3 + m), None, ALU.mult)
            dve.drain()
            flat2 = lambda t: t.rearrange("p a b -> p (a b)")
            sin_a, cos_a = flat2(ang[:, 1]), flat2(ang[:, 0])
            turns = rot_a[:, 0:2, :].rearrange("p a b -> p (a b)")
            MAGIC = 12582912.0
            V.tensor_scalar(turns, sin_a, 1.0 / (2 * np.pi), None, ALU.mult)
            dve.drain()
            V.tensor_scalar(turns, turns, MAGIC, None, ALU.add)
            dve.drain()
            V.tensor_scalar(turns, turns, -MAGIC, None, ALU.add)
            dve.drain()
            for part in TWO_PI:
                V.scalar_tensor_tensor(sin_a, turns, -part, sin_a, op0=ALU.mult, op1=ALU.add)
                dve.drain()
            V.tensor_scalar(cos_a, sin_a, float(np.pi / 2), None, ALU.add)
            dve.drain()
            V.tensor_scalar(turns, cos_a, float(np.pi), -2 * float(np.pi), ALU.is_gt, ALU.mult)
            dve.drain()
            V.tensor_tensor(cos_a, cos_a, turns, ALU.add)
            dve.drain()
            both = ang[:].rearrange("p a b c -> p (a b c)")
            done(V.tensor_scalar(both, both, PI_BELOW, -PI_BELOW, ALU.min, ALU.max))
            for i in range(2 * M):
                l0("sincos" if i == 0 else f"rot{i - 1}_copy")
                m = i % M
                src = pr[:, m, (QR, KR)[i // M]:(QR, KR)[i // M] + 1024].rearrange("p (h n two) -> p h n two", h=RH, two=2)
                t1, t2 = src[:, :, :, 0], src[:, :, :, 1]
                cos, sin = (cs[:, k, m, :].unsqueeze(1).to_broadcast([P, RH, P]) for k in (0, 1))
                for half, (f1, f2, op) in enumerate(((cos, sin, ALU.subtract), (sin, cos, ALU.add))):
                    V.tensor_tensor(rot_a[:], t1, f1, ALU.mult)
                    V.tensor_tensor(rot_b[:], t2, f2, ALU.mult)
                    dve.drain()
                    a = V.tensor_tensor(rot[:, :, half, :], rot_a[:], rot_b[:], op)
                    if half == 0:
                        dve.drain()
                done(a)
            for h in range(RH):
                l0(f"r{h}_s_psum")
                dec = C["decay"][:, h * 256:(h + 1) * 256]
                V.tensor_tensor(rs_sb[:, 0:256], aux4[0][:, 0:256], dec, ALU.mult)
                done(V.tensor_tensor(rs_sb[:, 256:384], aux4[0][:, 256:384], dec[:, 0:P], ALU.mult))
            l0("r_sq")
            head_norm(VR, GR, None)
            for g in range(4):
                l0(f"mix{g}_hi")
                done(V.tensor_tensor(flat2(mixT_lo[:, 4 * g:4 * g + 4, :]), aux[g % 2][:, :],
                                     flat2(mixT_hi[:, 4 * g:4 * g + 4, :]).bitcast(F32), ALU.subtract))

            residual_phase("out0")
            ffn("gu0", 1, 0)
            residual_phase("dn0")

            tail("l1t", 64)
            recip(2)
            dve.wait_ge(l1_const, 16 * 4)
            dve.wait_ge(unit_used, UNIT0["l1t"] + 4)
            for m in range(M):
                mm = slice(32 * m, 32 * m + 32)
                V.tensor_scalar(gate_t[:, 0, mm], aux4[2 + m][:, 0:32], rstd[:, m:m + 1], None, ALU.mult)
                V.scalar_tensor_tensor(gate_t[:, 1, mm], aux4[2 + m][:, 32:64], rstd[:, m:m + 1], gate_t[:, 8, 32:64],
                                       op0=ALU.mult, op1=ALU.add)
            dve.drain()
            a_pre = gate_t[:, 1, :]
            V.scalar_tensor_tensor(gate_t[:, 2, :], a_pre, -1.0, a_pre, op0=ALU.mult, op1=ALU.max).then_inc(gate_step, 1)
            dve.wait_ge(gate_step, GATE_AT["exp"])
            log1p(gate_t[:, 3, :], gate_t[:, 2, :], 64)
            V.scalar_tensor_tensor(gate_t[:, 3, :], a_pre, 0.0, gate_t[:, 3, :], op0=ALU.max, op1=ALU.add)
            dve.drain()
            for m in range(M):
                mm = slice(32 * m, 32 * m + 32)
                a = V.scalar_tensor_tensor(gate_t[:, 1, mm], gate_t[:, 3, mm], -1.0, gate_t[:, 8, 0:32], op0=ALU.mult, op1=ALU.mult)
            a.then_inc(gate_step, 1)
            dve.wait_ge(gate_step, GATE_AT["sums_exp"])
            V.memset(gate_t[:, 2:4, :], 0.0)
            V.memset(gate_t[:, 6, :], 0.0)
            V.scalar_tensor_tensor(gate_t[:, 7, :], gate_t[:, 0, :], -1.0, gate_t[:, 4, :], op0=ALU.mult, op1=ALU.mult
                                   ).then_inc(gdn_step, 1)
            dve.drain()

            def gdn(r):
                def at(name):
                    dve.wait_ge(gdn_step, r * GDN_N + GDN_AT[name])

                def done(a):
                    a.then_inc(gdn_step, 1)

                V.tensor_copy(gr[:].rearrange("p s m h -> p (s m) h"), gate_t[:, 0:8, :].rearrange("p s (m h) -> p (s m) h", m=M)[:, :, bass.ds(r * HV, HV)])
                V.tensor_copy(conv_r[:, 0:4, :], conv_w[:, bass.ds(r * 4, 4), :])
                V.tensor_copy(conv_r[:, 4:8, :], conv_w[:, bass.ds(r * 4 + 16, 4), :])
                dve.wait_ge(acc_read[0], r * 3 + (BLOCK0["l1r"] // 2 + 3))
                dve.wait_ge(acc_read[1], r * 3 + (BLOCK0["l1r"] // 2 + 3))
                V.tensor_copy(conv_r[:, 8:16, :], conv_w[:, bass.ds(r * 8 + 32, 8), :]).then_inc(gdn_step, 1)
                dve.drain()

                def per_head(slot, c, g):
                    return gr[:, slot, c, 4 * g:4 * g + 4].unsqueeze(2).to_broadcast([P, 4, P])

                def all_heads(t, n=4):
                    return t.unsqueeze(1).to_broadcast([P, n, t.shape[1]])

                heads = lambda t: t.rearrange("p (h n) -> p h n", n=P)
                twice = lambda t: t.rearrange("p (q e) n -> p q e n", e=2)
                for b in range(4):
                    at(f"c{b}_tap3")
                    dst = (qkT[:, 0:4], qkT[:, 4:8], vT[:, 0:4], vT[:, 4:8])[b]
                    for lag in range(1, CW):
                        for t in range(4):
                            a = V.scalar_tensor_tensor(dst[:, t, lag:], aux[0][:, t * SEQ:(t + 1) * SEQ - lag],
                                                       conv_r[:, 4 * b + t, CW - 1 - lag:CW - lag], dst[:, t, lag:],
                                                       op0=ALU.mult, op1=ALU.add)
                        if lag < CW - 1:
                            dve.drain()
                    done(a)
                for b in range(2):
                    at(f"n{b}_sqrt")
                    V.reciprocal(rn[:], rn[:])
                    dve.drain()
                    blk = qkT[:, 4 * b:4 * b + 4, :]
                    done(V.tensor_tensor(blk, blk, rn[:], ALU.mult))
                for c in range(M):
                    at(f"k{c}_kq_psum")
                    done(V.tensor_tensor(kq[:], aux[0][:, :].rearrange("p (h n) -> p h n", h=HQ), all_heads(C["low_up"]), ALU.mult))
                    for g in range(2):
                        u = f"k{c}_g{g}_"
                        if g:
                            at(f"k{c}_g0_" + ("o" if c else "s_copy"))
                        done(V.tensor_tensor(lam[:], all_heads(C["after"]), per_head(1, c, g), ALU.mult))
                        at(u + "d_exp")
                        V.tensor_tensor(EA[:], EA[:], per_head(0, c, g), ALU.mult)
                        pair_of = lambda half: kq[:, 2 * g:2 * g + 2, half * P:(half + 1) * P].unsqueeze(2).to_broadcast([P, 2, 2, P])
                        V.tensor_tensor(twice(ET[:]), twice(ET[:]), pair_of(1), ALU.mult)
                        dve.drain()
                        done(V.tensor_tensor(twice(EA[:]), twice(EA[:]), pair_of(0), ALU.mult))
                        dve.drain()
                        for n in range(len(LEVELS)):
                            if n:
                                at(u + f"l{n - 1}_t")
                            done(V.tensor_tensor(Bm[:], EA[:], all_heads(C["levels"][:, n * P:(n + 1) * P]), ALU.mult))
                            if n == 0:
                                dve.drain()
                                V.tensor_tensor(T[:], all_heads(ident), Bm[:], ALU.subtract)
                                at(u + "l0_q_psum")
                                done(V.tensor_tensor(TT[:], all_heads(ident), heads(aux4[2]), ALU.subtract))
                            else:
                                at(u + f"l{n}_t_psum")
                                if n < LAST:
                                    V.tensor_tensor(T[:], T[:], heads(aux4[0]), ALU.subtract)
                                done(V.tensor_tensor(TT[:], TT[:], heads(aux4[1]), ALU.subtract))
                        bv = heads(v_tok[:, c, g * NB:(g + 1) * NB])
                        if c:
                            at(u + "res_psum")
                            V.tensor_tensor(Rm[:], bv, per_head(0, c, g), ALU.mult)
                            V.tensor_tensor(qs_sb[:], heads(aux4[1]), per_head(4, c, g), ALU.mult)
                            V.tensor_tensor(Bm[:], heads(aux4[0]), per_head(7, c, g), ALU.mult)
                            dve.drain()
                            done(V.tensor_tensor(Rm[:], Rm[:], Bm[:], ALU.add))
                        else:
                            dve.drain()
                            kt2 = heads(k_tok[:, c, g * 256:(g + 1) * 256]).unsqueeze(2).to_broadcast([P, 2, 2, P])
                            et2 = gr[:, 5, c, 4 * g:4 * g + 4].rearrange("p (q e) -> p q e", e=2).unsqueeze(3).to_broadcast([P, 2, 2, P])
                            V.tensor_tensor(twice(k_tail[:]), kt2, et2, ALU.mult)
                            done(V.tensor_tensor(Rm[:], bv, per_head(0, c, g), ALU.mult))
                        at(u + "o_psum")
                        dst = o_all[:, c, bass.ds(r * 1024 + g * NB, NB)]
                        if c:
                            done(V.tensor_tensor(dst, aux4[3], qs_sb[:].rearrange("p a b -> p (a b)"), ALU.add))
                        else:
                            done(V.tensor_copy(dst, aux4[3]))
                at("o_sq")
                done(V.tensor_reduce(o_ms[:], o_sq[:], AX.X, ALU.add))
                at("o_rs")
                V.reciprocal(o_ms[:], o_ms[:])
                dve.drain()
                for m in range(M):
                    o = heads(o_all[:, m, bass.ds(r * 1024, 1024)])
                    V.tensor_tensor(o, o, o_ms[:, m, :].unsqueeze(2).to_broadcast([P, HV, GD]), ALU.mult)
                dve.drain()
                for m in range(M):
                    o = heads(o_all[:, m, bass.ds(r * 1024, 1024)])
                    V.tensor_tensor(o, o, all_heads(gnorm[:], HV), ALU.mult)
                dve.drain()
                for m in range(M):
                    o = o_all[:, m, bass.ds(r * 1024, 1024)]
                    a = V.tensor_tensor(o, o, zs[:, m, :], ALU.mult)
                done(a)

            with dve.Fori(0, ROUNDS) as r:
                body("l1r", r, 6, nothing)
                gdn(r)
            for g in range(8):
                dve.wait_ge(o_hi, g + 1)
                V.tensor_tensor(flat2(oT_lo[:, 4 * g:4 * g + 4, :]), aux[g % 2][:, :], flat2(oT_hi[:, 4 * g:4 * g + 4, :]).bitcast(F32),
                                ALU.subtract).then_inc(o_lo, 1)
            residual_phase("out1")
            ffn("gu1", 3, FF // NB)
            residual_phase("dn1")
            recip(4)
            dve.wait_ge(xs_copied, 16)
            dve.wait_ge(consts_in, 16 * 6)
            for m in range(M):
                V.scalar_tensor_tensor(x[:, m, :], x[:, m, :], rstd[:, m:m + 1], fgain[:], op0=ALU.mult, op1=ALU.mult
                                       ).then_inc(epi_step, 1)


WEIGHTS = ["x", "l0_w_in", "l0_gate_bias", "l0_mlstm_norm", "l0_w_out", "l0_w_gate", "l0_w_up", "l0_w_down",
           "l1_w_in", "l1_a_log", "l1_dt_bias", "l1_gdn_norm", "l1_w_out", "l1_w_gate", "l1_w_up", "l1_w_down",
           "final_norm"]


def layout(inputs):
    arrays = {f"in_{name}": np.ascontiguousarray(inputs[name]) for name in WEIGHTS}
    gains = [np.asarray(inputs[n]).reshape(KT, P).T for n in ("l0_norm_mix", "l0_norm_ffn", "l1_norm_mix", "l1_norm_ffn")]
    arrays["in_gains"] = np.ascontiguousarray(np.concatenate(gains, 1))
    conv = np.asarray(inputs["l1_conv_w"]).reshape(CW, -1, P)
    arrays["in_conv"] = np.ascontiguousarray(conv.transpose(2, 1, 0).reshape(P, -1))
    arrays["in_positions"] = np.ascontiguousarray(np.asarray(inputs["positions"]).reshape(M, P).T)
    arrays["in_shape_constants"] = shape_constants()
    return arrays


def kernel(**inputs):
    import concourse.bacc as bacc
    from concourse.bass_utils import run_bass_kernel_spmd

    nc = bacc.Bacc("TRN2", target_bir_lowering=False, num_devices=1)
    arrays = layout(inputs)
    aps = {name[3:]: nc.dram_tensor(name, a.shape, mybir.dt.from_np(a.dtype), kind="ExternalInput").ap()
           for name, a in arrays.items()}
    out = nc.dram_tensor("out_y", (SEQ, D), F32, kind="ExternalOutput").ap()
    build(nc, aps, out)
    r = run_bass_kernel_spmd(nc, [arrays], core_ids=[0])
    return r.results[0]["out_y"].reshape(1, SEQ, D)
```

```python
from contextlib import ExitStack

import numpy as np

import concourse.bass as bass
from concourse import mybir

F32 = mybir.dt.float32
F32R = mybir.dt.float32r
I32 = mybir.dt.int32
ALU = mybir.AluOpType
ACT = mybir.ActivationFunctionType
AX = mybir.AxisListType

P = 128
SEQ, D = 256, 2048
M = SEQ // P
KT = D // P
FF = -(-8 * D // (3 * 256)) * 256
FKT = FF // P
NB = 512
EPS = 1e-6
SLOTS = 4
MH, MDQK, MDV = 4, 128, 256
RH, RD = 4, 256
QKH, VH, GD = 16, 32, 128
CW = 4
ROUNDS = 4
HQ, HV = QKH // ROUNDS, VH // ROUNDS
SOFTCAP = 15.0
NEG = -1e30
TWO_PI = [6.28125, np.floor((2 * np.pi - 6.28125) * 2 ** 20) / 2 ** 20]
TWO_PI = [float(v) for v in TWO_PI + [2 * np.pi - sum(TWO_PI)]]
PI_BELOW = 3.1415925

QR, KR, QM, KM, VR, VM, OM, GR, L0W = 0, 1024, 2048, 2560, 3072, 4096, 5120, 6144, 7168
L0_GATES = 3072
L0_COLS = [3080, 3592, 4104, 4616, 0, 512, 5128, 5640, 1024, 1536, 2048, 2560, 6152, 6664]
L1_GATES = 12288

LEVELS = [1, 2, 4, 8, 16, 32, 64]
CONST_PARTS = [("ident", 128), ("upto", 128), ("after", 128), ("ones", 128), ("neg", 384),
               ("low_up", 256), ("levels", 128 * len(LEVELS)), ("decay", RH * 256), ("freq", 128)]
CONST_AT = {}
_n = 0
for _name, _w in CONST_PARTS:
    CONST_AT[_name] = (_n, _n + _w)
    _n += _w
CONST_W = _n


def shape_constants():
    a, b = np.arange(P)[:, None], np.arange(P)[None, :]
    c = np.zeros((P, CONST_W), np.float32)

    def put(name, v):
        lo, hi = CONST_AT[name]
        c[:, lo:hi] = v

    put("ident", a == b)
    put("upto", a <= b)
    put("after", a > b)
    put("ones", 1.0)
    neg = np.where(a >= b, 0.0, NEG)
    put("neg", np.concatenate([neg, np.zeros((P, P)), neg], 1))
    put("low_up", np.concatenate([a > b, a <= b], 1))
    put("levels", np.concatenate([((a // (2 * n)) == (b // (2 * n))) & ((a // n) % 2 == 1) & ((b // n) % 2 == 0)
                                  for n in LEVELS], 1))
    t = np.arange(SEQ)[None, :]
    rel = np.where(t >= a, t - a, 0).astype(np.float32)
    dec = []
    for h in range(RH):
        log_gamma = np.log(np.float32(1.0) - np.float32(2.0) ** np.float32(-5.0 - h))
        dec.append(np.where(t >= a, np.exp(rel * log_gamma), 0.0) * RD ** -0.5)
    put("decay", np.concatenate(dec, 1))
    put("freq", (np.float32(10000.0) ** (-np.arange(0, RD, 2, dtype=np.float32) / np.float32(RD)))[None, :])
    return c


PHASES = [("l0a", KT // 2, 4), ("l0b", KT // 2, 2), ("l0t", 4, 0), ("l0c", KT // 2, 8), ("out0", KT // 2, 4), ("gu0", KT // 2, 2 * FF // NB),
          ("dn0", FKT // 2, 4), ("l1t", 4, 0), ("l1q", KT // 2, 4), ("l1r", KT // 2, 12), ("l1z", KT // 2, 8), ("out1", KT, 4),
          ("gu1", KT // 2, 2 * FF // NB), ("dn1", FKT // 2, 4)]
UNIT0, BLOCK0, UPB = {}, {}, {}
_u = _b = 0
for _name, _upb, _nb in PHASES:
    UNIT0[_name], BLOCK0[_name], UPB[_name] = _u, _b, _upb
    _u += _upb * max(_nb, 1)
    _b += _nb
UNIT_END, BLOCK_END = _u, _b

MLSTM_HEAD = ["rows", "d_psum", "d_max", "d_exp", "s_psum", "s_prod", "st_psum", "st_copy", "num_psum", "num_div"]
L0_STEPS = (["pos", "sincos"]
            + [f"rot{i}_{s}" for i in range(2 * M) for s in ("mul", "tr", "copy")]
            + ["gates", "tanh", "cap", "exp", "log1p", "m_tr", "m_trc"]
            + [f"r{h}_{s}" for h in range(RH) for s in ("s_psum", "s_dec", "o_psum", "o_copy")]
            + [f"m{h}_{s}" for h in range(MH) for s in MLSTM_HEAD]
            + ["m_sq", "m_norm"]
            + [f"mix{g}_{s}" for g in range(2) for s in ("tr", "hi", "lo")]
            + ["r_sq", "r_norm"]
            + [f"mix{g}_{s}" for g in range(2, 4) for s in ("tr", "hi", "lo")])
L0_AT = {s: i + 1 for i, s in enumerate(L0_STEPS)}

AHEAD = 2
L0_SLOTS = [0, 1, 2, 3, 4, 20, 21] + list(range(40, 48)) + list(range(53, 69)) + [72, 73, 74]

GATES_AT = 6
O_SLOTS = [55, 58, 61]

GDN_GATE_STEPS = ["raw", "exp", "log1p", "sums", "sums_exp"]
GATE_AT = {s: i + 1 for i, s in enumerate(GDN_GATE_STEPS)}
CONV_BLOCK = ["x_tr", "tap3", "conv", "silu"]
LAST = len(LEVELS) - 1


def level_steps(n):
    return ["q_psum"] + (["q", "t_psum"] if n else []) + ["t"]


GDN_STEPS = (["round"] + [f"c{b}_{s}" for b in range(4) for s in CONV_BLOCK]
             + [f"n{b}_{s}" for b in range(2) for s in ("sq", "sum", "sqrt", "mul")]
             + ["k_tr", "k_copy", "v0_tr", "v0_copy", "v1_tr", "v1_copy", "o_sq", "o_sum", "o_rs", "o_norm"])
GROUP_STEPS = [f"t{c}_{s}" for c in range(M) for s in
               ["lam", "d_psum", "d_exp", "kq_psum", "a"]
               + [f"l{n}_{s}" for n in range(len(LEVELS)) for s in level_steps(n)]
               + (["res_psum"] if c else []) + ["res", "vn_psum", "vn", "o_psum", "o"]
               + ([] if c else ["s_copy"])]
GROUP_AT = {s: i + 1 for i, s in enumerate(GROUP_STEPS)}
GROUP_N = len(GROUP_STEPS)
GDN_AT = {s: i + 2 for i, s in enumerate(GDN_STEPS)}
GDN_N = len(GDN_STEPS)


def build(nc, A, out):
    with ExitStack() as ctx:
        def sb(name, shape, dt=F32):
            return ctx.enter_context(nc.sbuf_tensor(name, shape, dt))

        def sem(name):
            return ctx.enter_context(nc.semaphore(name))

        wraw = sb("wraw", [P, SLOTS, 2 * NB])
        whi = sb("whi", [P, SLOTS, 2 * NB], F32R)
        wlo = sb("wlo", [P, SLOTS, 2 * NB], F32R)
        x = sb("x", [P, M, D])
        xs = sb("xs", [P, M, NB])
        hT_at = nc.sbuf_base
        hT_hi = sb("hT_hi", [P, KT, SEQ], F32R)
        hT_lo = sb("hT_lo", [P, KT, SEQ], F32R)
        const = sb("const", [P, CONST_W])
        gains = sb("gains", [P, 4, KT])
        ssq = sb("ssq", [P, M, 4])
        mean = sb("mean", [P, M])
        rms = sb("rms", [P, M])
        rstd = sb("rstd", [P, M])
        epsc = sb("epsc", [P, 2])
        gate_t = sb("gate_t", [P, 10, 64])
        C = {name: const[:, lo:hi] for name, (lo, hi) in CONST_AT.items()}
        ident = C["ident"]

        arena0 = (nc.sbuf_base + 63) // 64 * 64
        arena_end = arena0
        names = iter(range(1000))

        def at(offset, shape, dt=F32):
            nonlocal arena_end
            size = 4 * int(np.prod(shape[1:]))
            arena_end = max(arena_end, arena0 + offset + size)
            return nc.alloc_sbuf_tensor_at(f"arena{next(names)}", shape, dt, offset=arena0 + offset)

        KB = 1024
        pr = at(0, [P, M, L0W])
        mixT_hi = at(56 * KB, [P, KT, SEQ], F32R)
        mixT_lo = at(72 * KB, [P, KT, SEQ], F32R)
        rot = at(56 * KB, [P, RH, 2, P])
        rot_a = at(60 * KB, [P, RH, P])
        rot_b = at(62 * KB, [P, RH, P])
        qmT = at(56 * KB, [P, MH, SEQ])
        kmT = at(60 * KB, [P, MH, SEQ])
        qrT = at(64 * KB, [P, 2 * RH, SEQ])
        krT = at(72 * KB, [P, 2 * RH, SEQ])
        cs = at(80 * KB, [P, 2, M, P])
        ang = at(82 * KB, [P, 2, M, P])
        d_rows = at(80 * KB, [P, 6, P])
        d_sb = at(83 * KB, [P, 384])
        p_sb = at(84 * KB + 512, [P, 384])
        st_sb = at(86 * KB, [P, 384])
        rs_sb = at(86 * KB, [P, 384])
        mnorm = at(87 * KB + 512, [P, MH * MDV])
        fT_hi = at(0, [P, FKT, SEQ], F32R)
        fT_lo = at(44 * KB, [P, FKT, SEQ], F32R)
        sg = at(88 * KB, [P, M, NB])
        prod = xs
        qkv = at(0, [P, M, 2048])
        k_tok = at(16 * KB, [P, M, 512])
        v_tok = at(20 * KB, [P, M, 1024])
        qkT = at(28 * KB, [P, 8, SEQ])
        zs = [at((36 if n < 2 * (ROUNDS - 1) else 64) * KB, [P, M, NB]) for n in range(2 * ROUNDS)]
        kq = [at((76 + 2 * g) * KB, [P, 2, 2 * P]) for g in range(2)]
        vT = at(48 * KB, [P, 8, SEQ])
        sq = at(56 * KB, [P, 4, SEQ])
        rn = at(60 * KB, [P, 4, SEQ])
        EA, ET, T, TT, Q1, B0, B1 = ([at((48 + 14 * g + 2 * k) * KB, [P, 4, P]) for g in range(2)] for k in range(7))
        Bm = [[B0[g], B1[g]] for g in range(2)]
        lam, Rm, Vn, k_tail, qs_sb = B0, T, Q1, B0, B1
        o_sq = at(48 * KB, [P, M, HV, GD])
        St = xs[:, :, :].rearrange("p m (h n) -> p (m h) n", n=P)
        conv_w = at(80 * KB, [P, 64, CW])
        gnorm = at(81 * KB, [P, GD])
        conv_r = at(81 * KB + 512, [P, 16, CW])
        gr = at(82 * KB, [P, 8, M, HV])
        o_ms = at(82 * KB + 512, [P, M, HV])
        o_r = at(84 * KB, [P, M, HV * GD])
        o_z = [at(0, [P, M, HV * GD]), at(8 * KB, [P, M, HV * GD]), at(40 * KB, [P, M, HV * GD]), o_r]
        o_dram = nc.dram_tensor("o_rounds", (SEQ, VH * GD), F32, kind="Internal").ap()
        O_ORDER = [0, 2, 1, 3]
        oT_hi = at(0, [P, 2 * KT, SEQ], F32R)
        oT_lo = at(32 * KB, [P, 2 * KT, SEQ], F32R)
        fgain = nc.alloc_sbuf_tensor_at("fgain", [P, D], F32, offset=hT_at)
        assert arena_end <= nc.sbuf_usable_end, (arena_end, nc.sbuf_usable_end)

        acc = [ctx.enter_context(nc.psum_tensor(f"acc{i}", [P, M, NB], F32)) for i in range(2)]
        aux = [ctx.enter_context(nc.psum_tensor(f"aux{i}", [P, 2 * NB], F32)) for i in range(2)]
        aux4 = [aux[i // 2][:, (i % 2) * NB:(i % 2 + 1) * NB] for i in range(4)]

        raw_in = [sem(f"raw_in{i}") for i in range(SLOTS)]
        hi_done = sem("hi_done")
        lo_done = sem("lo_done")
        unit_used = sem("unit_used")
        acc_read = [sem(f"acc_read{i}") for i in range(2)]
        consts_in = sem("consts_in")
        x_in = sem("x_in")
        eps_set = sem("eps_set")
        xs_copied = sem("xs_copied")
        xt_ready = sem("xt_ready")
        xhi_done = sem("xhi_done")
        xlo_done = sem("xlo_done")
        mean_done = sem("mean_done")
        rms_done = sem("rms_done")
        rstd_done = sem("rstd_done")
        tail_ready = sem("tail_ready")
        tail_read = sem("tail_read")
        ft_ready = sem("ft_ready")
        fhi_done = sem("fhi_done")
        flo_done = sem("flo_done")
        l0_step = sem("l0_step")
        gate_step = sem("gate_step")
        gdn_step = sem("gdn_step")
        group_step = [sem(f"group_step{g}") for g in range(2)]
        level_part = [sem(f"level_part{g}") for g in range(2)]
        o_stored = sem("o_stored")
        o_loaded = [sem(f"o_loaded{r}") for r in range(ROUNDS - 1)]
        gated = sem("gated")
        o_tr = sem("o_tr")
        o_hi = sem("o_hi")
        o_lo = sem("o_lo")
        epi_step = sem("epi_step")
        l1_const = sem("l1_const")
        out_done = sem("out_done")

        def col_block(w, col):
            return w.rearrange("(k p) n -> p k n", p=P)[:, :, bass.ds(col, NB)]

        NORM_OF = {"out0": 1, "dn0": 2, "out1": 3, "dn1": 4}

        def l0_slots(mixer, w):
            if w in L0_SLOTS:
                next(mixer)

        block = ctx.enter_context(nc.Block())

        @block.sync
        def _(sp):
            def unit(w, u, j, col):
                sp.wait_ge(lo_done, u - (SLOTS - 1))
                sp.dma_start(wraw[:, j % SLOTS, :].rearrange("p (k n) -> p k n", k=2),
                             col_block(w, col)[:, 2 * j:2 * j + 2, :]).then_inc(raw_in[j % SLOTS], 16)

            def first_units(w, col, n):
                for j in range(n):
                    sp.dma_start(wraw[:, j, :].rearrange("p (k n) -> p k n", k=2),
                                 col_block(w, col)[:, 2 * j:2 * j + 2, :]).then_inc(raw_in[j], 16)

            def phase(name, n_body, lo, hi, cols):
                upb = UPB[name]
                with sp.Fori(lo, hi) as i:
                    for b, (wt, col) in enumerate(cols(i)):
                        for j in range(upb):
                            u = UNIT0[name] + (i * n_body + b) * upb + j
                            sp.wait_ge(lo_done, u - (SLOTS - 1))
                            s = (b * upb + j) % SLOTS
                            sp.dma_start(wraw[:, s, :].rearrange("p (k n) -> p k n", k=2),
                                         col_block(wt, col)[:, 2 * j:2 * j + 2, :]).then_inc(raw_in[s], 16)

            def tail(name, w, col, width):
                for j in range(4):
                    sp.wait_ge(lo_done, UNIT0[name] + j - (SLOTS - 1))
                    sp.dma_start(wraw[:, j, 0:4 * width].rearrange("p (k n) -> p k n", k=4),
                                 w.rearrange("(k p) n -> p k n", p=P)[:, 4 * j:4 * j + 4, col:col + width]
                                 ).then_inc(raw_in[j], 16)

            sp.dma_start(x[:], A["x"].rearrange("a (m p) n -> p (a m) n", p=P)).then_inc(x_in, 16)
            sp.dma_start(const[:], A["shape_constants"]).then_inc(consts_in, 16)
            sp.dma_start(gains[:], A["gains"].rearrange("p (n k) -> p n k", n=4)).then_inc(consts_in, 16)
            sp.dma_start(gate_t[:, 9, 0:2].bitcast(I32), A["positions"]
                         ).then_inc(consts_in, 16)
            sp.dma_start(gate_t[:, 8, 0:8], A["l0_gate_bias"].rearrange("(a n) -> a n", a=1).to_broadcast([P, 8])
                         ).then_inc(consts_in, 16)
            sp.dma_start(mnorm[:], A["l0_mlstm_norm"].rearrange("(a n) -> a n", a=1).to_broadcast([P, MH * MDV])
                         ).then_inc(consts_in, 16)
            w0, w1 = A["l0_w_in"], A["l1_w_in"]
            first_units(w0, L0_COLS[0], SLOTS)
            for j in range(SLOTS, 2 * UPB["l0a"]):
                unit(w0, j, j % UPB["l0a"], L0_COLS[j // UPB["l0a"]])
            phase("l0a", 2, 1, 2, lambda i: [(w0, i * 2 * NB + L0_COLS[b]) for b in range(2)])
            phase("l0b", 2, 0, 1, lambda i: [(w0, i * 2 * NB + L0_COLS[4 + b]) for b in range(2)])
            tail("l0t", w0, L0_GATES, 8)
            for n in range(4):
                for b in range(2):
                    for j in range(UPB["l0c"]):
                        unit(w0, UNIT0["l0c"] + (2 * n + b) * UPB["l0c"] + j, j, L0_COLS[6 + 2 * n + b])
            phase("out0", 2, 0, 2, lambda i: [(A["l0_w_out"], i * 2 * NB + b * NB) for b in range(2)])
            phase("gu0", 2, 0, FF // NB, lambda i: [(A["l0_w_gate"], i * NB), (A["l0_w_up"], i * NB)])
            phase("dn0", 2, 0, 2, lambda i: [(A["l0_w_down"], i * 2 * NB + b * NB) for b in range(2)])
            tail("l1t", A["l1_w_in"], L1_GATES, 64)
            sp.wait_ge(unit_used, UNIT0["l1t"])
            sp.dma_start(gnorm[:], A["l1_gdn_norm"].rearrange("(a n) -> a n", a=1).to_broadcast([P, GD])
                         ).then_inc(l1_const, 16)
            sp.dma_start(conv_w[:], A["conv"].rearrange("p (c w) -> p c w", w=CW)).then_inc(l1_const, 16)
            for n, g in enumerate(("l1_a_log", "l1_dt_bias")):
                sp.dma_start(gate_t[:, 8, 32 * n:32 * n + 32], A[g].rearrange("(a n) -> a n", a=1).to_broadcast([P, 32])
                             ).then_inc(l1_const, 16)
            zcol, qkvcol = 8192, [0, 2048, 4096, 4096 + NB]
            phase("l1q", 4, 0, 1, lambda i: [(w1, i * NB + c) for c in qkvcol])
            phase("l1r", 4, 0, ROUNDS - 1, lambda i: [(w1, i * NB + c + NB) for c in qkvcol[:2]]
                  + [(w1, i * 2 * NB + c + 2 * NB) for c in qkvcol[2:]])
            phase("l1z", 2, 0, 4, lambda i: [(w1, i * 2 * NB + zcol + b * NB) for b in range(2)])
            phase("out1", 2, 0, 2, lambda i: [(A["l1_w_out"], i * 2 * NB + b * NB) for b in range(2)])
            phase("gu1", 2, 0, FF // NB, lambda i: [(A["l1_w_gate"], i * NB), (A["l1_w_up"], i * NB)])
            sp.wait_ge(unit_used, UNIT0["dn1"])
            sp.dma_start(fgain[:], A["final_norm"].rearrange("(a n) -> a n", a=1).to_broadcast([P, D])
                         ).then_inc(consts_in, 16)
            phase("dn1", 2, 0, 2, lambda i: [(A["l1_w_down"], i * 2 * NB + b * NB) for b in range(2)])
            for m in range(M):
                sp.wait_ge(epi_step, m + 1)
                sp.dma_start(out[m * P:(m + 1) * P, :], x[:, m, :]).then_inc(out_done, 16)
            sp.wait_ge(out_done, 16 * M)

        @block.gpsimd
        def _(pool):
            def keep_x(name):
                with pool.Fori(0, 2) as i:
                    for b in range(2):
                        pool.wait_ge(acc_read[b], i + (BLOCK0[name] // 2 + 1))
                        nc.gpsimd.tensor_copy(x[:, :, bass.ds(i * 2 * NB + b * NB, NB)], xs[:]).then_inc(xs_copied, 1)

            def level_parts(r):
                for c in range(M):
                    for n in range(len(LEVELS)):
                        mask = C["levels"][:, n * P:(n + 1) * P].unsqueeze(1).to_broadcast([P, 4, P])
                        for g in range(2):
                            if n == 0:
                                pool.wait_ge(group_step[g], r * GROUP_N + GROUP_AT[f"t{c}_a"])
                            elif n >= 2:
                                pool.wait_ge(group_step[g], r * GROUP_N + GROUP_AT[f"t{c}_l{n - 2}_q_psum" if n > 2 else f"t{c}_l0_t"])
                            nc.gpsimd.tensor_tensor(Bm[g][n % 2][:], EA[g][:], mask, ALU.mult).then_inc(level_part[g], 1)

            keep_x("out0")
            keep_x("dn0")
            with pool.Fori(0, ROUNDS - 1) as r:
                level_parts(r)
                pool.wait_ge(gdn_step, r * GDN_N + GDN_AT["o_norm"])
                pool.dma_start(o_dram[:, bass.ds(r * HV * GD, HV * GD)].rearrange("(m p) n -> p m n", p=P), o_r[:]
                               ).then_inc(o_stored, 16)
                pool.wait_ge(o_stored, r * 16 + 16)
            level_parts(ROUNDS - 1)
            keep_x("out1")
            keep_x("dn1")

        @block.tensor
        def _(pe):
            def products(pair, k, k_last, hi, lo, slot, kk, width, stride, first):
                for m in range(M):
                    tok = slice(m * P, (m + 1) * P)
                    o = pair[m]
                    a, b = hi[:, k, tok], lo[:, k, tok]
                    wh = whi[:, slot, kk * stride:kk * stride + width]
                    wl = wlo[:, slot, kk * stride:kk * stride + width]
                    nc.tensor.matmul(o, a, wh, start=first, stop=False)
                    nc.tensor.matmul(o, a, wl, start=False, stop=False)
                    mm = nc.tensor.matmul(o, b, wh, start=False, stop=k_last)
                return mm

            def gemm_block(name, base_u, base_b, hi, lo, slot0, parity, midway=None, fresh=False, between=None):
                upb = UPB[name]
                if not fresh:
                    pe.wait_ge(acc_read[parity], base_b)
                for j in range(upb):
                    pe.wait_ge(lo_done, base_u + (j + 1))
                    for kk in range(2):
                        k = 2 * j + kk
                        mm = products([acc[parity][:, m, :] for m in range(M)], k, k == 2 * upb - 1, hi, lo,
                                      (slot0 + j) % SLOTS, kk, NB, NB, k == 0)
                    mm.then_inc(unit_used, 1)
                    if j == 3 and midway is not None:
                        midway()
                    if between is not None:
                        between(slot0 + j)

            def tail(name, hi, lo, width):
                for j in range(4):
                    pe.wait_ge(lo_done, UNIT0[name] + j + 1)
                    for kk in range(4):
                        k = 4 * j + kk
                        mm = products([aux4[2 + m][:, 0:width] for m in range(M)], k, k == KT - 1, hi, lo, j, kk,
                                      width, width, k == 0)
                    mm.then_inc(unit_used, 1)

            def transposes(src, dst, n):
                for t in range(n):
                    for m in range(M):
                        mm = nc.tensor.transpose(dst[:, t * SEQ + m * P:t * SEQ + (m + 1) * P],
                                                 src(m, t), ident)
                return mm

            def x_block(n_done, src):
                transposes(src, aux[0], 4).then_inc(xt_ready, 1)

            def body(name, i, lo_b, n_body, hi, lo, midways, fresh=(), between=None):
                for b in range(n_body):
                    upb = UPB[name]
                    gemm_block(name, i * (n_body * upb) + (UNIT0[name] + b * upb),
                               i * (n_body // 2) + (BLOCK0[name] + b) // 2, hi, lo, b * upb, b % 2,
                               midways[b], b in fresh, between)

            xs_tile = lambda m, t: xs[:, m, t * P:(t + 1) * P]
            prod_tile = lambda m, t: prod[:, m, t * P:(t + 1) * P]

            def residual_phase(name, hi, lo, transposed):
                done = 4 * (NORM_OF[name] - 1)

                def xt(i, b):
                    def f():
                        pe.wait_ge(acc_read[1 - b], i + (BLOCK0[name] // 2 + b))
                        pe.wait_ge(xlo_done, i * 2 + (done + b + 3))
                        transposes(xs_tile, aux[0], 4).then_inc(xt_ready, 1)
                    return f if transposed else None
                body(name, 0, 0, 2, hi, lo, [None, xt(0, 1)])
                with pe.Fori(1, 2) as i:
                    body(name, i, 0, 2, hi, lo, [xt(i, 0), xt(i, 1)])
                if transposed:
                    xt(2, 0)()

            def ffn(name, down, n0):
                def tr(i):
                    def f():
                        pe.wait_ge(acc_read[1], i + BLOCK0[name] // 2)
                        if n0 or not isinstance(i, int) or i > 1:
                            pe.wait_ge(flo_done, i + (n0 - 1))
                        transposes(prod_tile, aux[1], 4).then_inc(ft_ready, 1)
                    return f
                body(name, 0, 0, 2, hT_hi, hT_lo, [None, None])
                body(name, 1, 0, 2, hT_hi, hT_lo, [tr(1), None])
                with pe.Fori(2, FF // NB) as i:
                    body(name, i, 0, 2, hT_hi, hT_lo, [tr(i), None])
                tr(FF // NB)()
                pe.wait_ge(flo_done, n0 + FF // NB)


            def l0(name):
                pe.wait_ge(l0_step, L0_AT[name])

            def projected(blocks):
                for b in range(2):
                    pe.wait_ge(acc_read[b], blocks // 2)

            def l0_mixer():
                for i in range(2 * M):
                    yield
                    l0(f"rot{i}_mul")
                    for t in range(2 * RH):
                        mm = nc.tensor.transpose(aux[i % 2][:, t * P:(t + 1) * P], rot[:, t // 2, t % 2, :], ident)
                    mm.then_inc(l0_step, 1)
                yield
                yield
                projected(6)
                l0("log1p")
                for dst, col in ((aux[0], QM), (aux[1], KM)):
                    mm = transposes(lambda m, t: pr[:, m, col + t * P:col + (t + 1) * P], dst, MH)
                mm.then_inc(l0_step, 1)
                for h in range(RH):
                    yield
                    l0("m_trc" if h == 0 else f"r{h - 1}_o_copy")
                    for d in range(2):
                        nc.tensor.matmul(aux4[0][:, 0:SEQ], krT[:, 2 * h + d, 0:P], qrT[:, 2 * h + d, :],
                                         start=d == 0, stop=d == 1)
                    for d in range(2):
                        mm = nc.tensor.matmul(aux4[0][:, SEQ:3 * P], krT[:, 2 * h + d, P:], qrT[:, 2 * h + d, P:],
                                              start=d == 0, stop=d == 1)
                    mm.then_inc(l0_step, 1)
                    yield
                    l0(f"r{h}_s_dec")
                    projected(8)
                    weighted_values(rs_sb, VR + h * RD).then_inc(l0_step, 1)
                for h in range(MH):
                    yield
                    l0(f"m{h}_rows")
                    rows = d_rows[:, :, :].rearrange("p a b -> p (a b)")
                    nc.tensor.matmul(aux4[0][:, 0:P], C["upto"], rows[:, 0:P], start=True, stop=False)
                    nc.tensor.matmul(aux4[0][:, 0:P], C["ones"], rows[:, 5 * P:], start=False, stop=True)
                    nc.tensor.matmul(aux4[0][:, P:3 * P], C["upto"], rows[:, P:3 * P], start=True, stop=False)
                    nc.tensor.matmul(aux4[0][:, P:3 * P], C["ones"], rows[:, 3 * P:5 * P], start=False, stop=True
                                     ).then_inc(l0_step, 1)
                    yield
                    l0(f"m{h}_d_exp")
                    nc.tensor.matmul(aux4[2][:, 0:P], qmT[:, h, 0:P], kmT[:, h, 0:P], start=True, stop=True)
                    nc.tensor.matmul(aux4[2][:, P:3 * P], qmT[:, h, P:], kmT[:, h, :], start=True, stop=True
                                     ).then_inc(l0_step, 1)
                    yield
                    l0(f"m{h}_s_prod")
                    for i in range(3):
                        mm = nc.tensor.transpose(aux4[0][:, i * P:(i + 1) * P], d_sb[:, i * P:(i + 1) * P], ident)
                    mm.then_inc(l0_step, 1)
                    yield
                    l0(f"m{h}_st_copy")
                    projected(10)
                    weighted_values(st_sb, VM + h * MDV).then_inc(l0_step, 1)
                yield
                for g in range(4):
                    if g == 2:
                        yield
                    yield
                    l0(("m_norm", "mix0_lo", "r_norm", "mix2_lo")[g])
                    base = (VM if g < 2 else VR) + (g % 2) * 4 * P
                    transposes(lambda m, t: pr[:, m, base + t * P:base + (t + 1) * P], aux[g % 2], 4).then_inc(l0_step, 1)

            def weighted_values(st, col):
                v = [pr[:, m, col:col + 256] for m in range(M)]
                nc.tensor.matmul(aux4[2][:, 0:256], st[:, 0:P], v[0], start=True, stop=True)
                nc.tensor.matmul(aux4[2][:, 256:512], st[:, P:2 * P], v[0], start=True, stop=False)
                return nc.tensor.matmul(aux4[2][:, 256:512], st[:, 2 * P:3 * P], v[1], start=False, stop=True)

            def gdn_gates():
                pe.wait_ge(gate_step, GATE_AT["log1p"])
                la = gate_t[:, 1, :]
                nc.tensor.matmul(aux4[2][:, 0:64], C["upto"], la, start=True, stop=True)
                nc.tensor.matmul(aux4[3][:, 0:64], C["after"], la, start=True, stop=True).then_inc(gate_step, 1)

            def gdn(r):
                def at(name):
                    pe.wait_ge(gdn_step, r * GDN_N + GDN_AT[name])

                def done(mm):
                    mm.then_inc(gdn_step, 1)

                for b in range(4):
                    if b:
                        yield
                    at("round" if b == 0 else f"c{b - 1}_silu")
                    done(transposes(lambda m, t: qkv[:, m, (4 * b + t) * P:(4 * b + t + 1) * P], aux[0], 4))
                for b in range(2):
                    yield
                    at(f"n{b}_sq")
                    for i in range(2):
                        mm = nc.tensor.matmul(aux4[i], C["ones"], sq[:, 2 * i:2 * i + 2, :].rearrange("p a b -> p (a b)"),
                                              start=True, stop=True)
                    done(mm)
                for name, prev, src in (("k", "n1_mul", lambda t: qkT[:, 4 + t, :]), ("v0", "k_copy", lambda t: vT[:, t, :]),
                                        ("v1", "v0_copy", lambda t: vT[:, 4 + t, :])):
                    yield
                    at(prev)
                    for m in range(M):
                        for t in range(4):
                            mm = nc.tensor.transpose(aux[0][:, m * NB + t * P:m * NB + (t + 1) * P],
                                                     src(t)[:, m * P:(m + 1) * P], ident)
                    done(mm)

                def gat(g, name):
                    pe.wait_ge(group_step[g], r * GROUP_N + GROUP_AT[name])

                def gdone(g, mm):
                    mm.then_inc(group_step[g], 1)

                col = lambda h: slice(h * P, (h + 1) * P)
                half = lambda g, k: aux[g][:, k * NB:(k + 1) * NB]
                for c in range(M):
                    tok = slice(c * P, (c + 1) * P)
                    u = f"t{c}_"
                    yield
                    for g in range(2):
                        gat(g, u + "lam")
                        gdone(g, nc.tensor.matmul(half(g, 0), C["upto"], lam[g][:, :, :].rearrange("p a b -> p (a b)"),
                                                  start=True, stop=True))
                    yield
                    for g in range(2):
                        gat(g, u + "d_exp")
                        for h in range(2):
                            k, q = qkT[:, 4 + 2 * g + h, tok], qkT[:, 2 * g + h, tok]
                            nc.tensor.matmul(half(g, 0)[:, col(2 * h)], k, k, start=True, stop=True)
                            nc.tensor.matmul(half(g, 0)[:, col(2 * h + 1)], k, q, start=True, stop=True)
                        for h in range(4):
                            mm = nc.tensor.transpose(half(g, 1)[:, col(h)], EA[g][:, h, :], ident)
                        gdone(g, mm)
                    for n in range(len(LEVELS)):
                        yield
                        for g in range(2):
                            pe.wait_ge(level_part[g], r * (M * len(LEVELS)) + (c * len(LEVELS) + n + 1))
                            gat(g, u + (f"l{n - 1}_t" if n else "a"))
                            for h in range(4):
                                if n:
                                    mm = nc.tensor.matmul(half(g, 0)[:, col(h)], Bm[g][n % 2][:, h, :], TT[g][:, h, :],
                                                          start=True, stop=True)
                                else:
                                    mm = nc.tensor.transpose(half(g, 0)[:, col(h)], Bm[g][0][:, h, :], ident)
                            gdone(g, mm)
                        if n:
                            yield
                            for g in range(2):
                                gat(g, u + f"l{n}_q")
                                for h in range(4):
                                    if n < LAST:
                                        nc.tensor.matmul(half(g, 0)[:, col(h)], Q1[g][:, h, :], T[g][:, h, :], start=True, stop=True)
                                    mm = nc.tensor.matmul(half(g, 1)[:, col(h)], T[g][:, h, :], Q1[g][:, h, :], start=True, stop=True)
                                gdone(g, mm)
                    if c:
                        yield
                        for g in range(2):
                            gat(g, u + f"l{LAST}_t")
                            for h in range(4):
                                s = St[:, 4 * g + h, :]
                                nc.tensor.matmul(half(g, 0)[:, col(h)], qkT[:, 4 + 2 * g + h // 2, tok], s, start=True, stop=True)
                                mm = nc.tensor.matmul(half(g, 1)[:, col(h)], qkT[:, 2 * g + h // 2, tok], s, start=True, stop=True)
                            gdone(g, mm)
                    yield
                    for g in range(2):
                        gat(g, u + "res")
                        for h in range(4):
                            mm = nc.tensor.matmul(half(g, 0)[:, col(h)], TT[g][:, h, :], Rm[g][:, h, :], start=True, stop=True)
                        gdone(g, mm)
                    yield
                    for g in range(2):
                        gat(g, u + "vn")
                        for h in range(4):
                            if not c:
                                nc.tensor.matmul(half(g, 0)[:, col(h)], k_tail[g][:, h, :], Vn[g][:, h, :], start=True, stop=True)
                            mm = nc.tensor.matmul(half(g, 1)[:, col(h)], ET[g][:, h, :], Vn[g][:, h, :], start=True, stop=True)
                        gdone(g, mm)
                yield

            pe.wait_ge(x_in, 16)
            pe.wait_ge(consts_in, 16 * 5)
            for n in range(4):
                if n:
                    pe.wait_ge(xlo_done, n)
                transposes(lambda m, t: x[:, m, n * NB + t * P:n * NB + (t + 1) * P], aux[0], 4).then_inc(xt_ready, 1)
            pe.wait_ge(xlo_done, 4)
            body("l0a", 0, 0, 2, hT_hi, hT_lo, [None, None], fresh=(0, 1))
            body("l0a", 1, 0, 2, hT_hi, hT_lo, [None, None])
            mixer = l0_mixer()
            body("l0b", 0, 0, 2, hT_hi, hT_lo, [None, None], between=lambda w: l0_slots(mixer, w))
            l0("rot3_copy")
            tail("l0t", hT_hi, hT_lo, 8)
            body("l0c", 0, 0, 8, hT_hi, hT_lo, [None] * 8, between=lambda w: l0_slots(mixer, w + 20))
            for _ in mixer:
                pass
            l0("mix3_lo")
            residual_phase("out0", mixT_hi, mixT_lo, True)
            pe.wait_ge(xlo_done, 8)
            ffn("gu0", "dn0", 0)
            residual_phase("dn0", fT_hi, fT_lo, True)
            pe.wait_ge(xlo_done, 12)
            tail("l1t", hT_hi, hT_lo, 64)
            body("l1q", 0, 0, 4, hT_hi, hT_lo, [None] * 4, between=lambda w: gdn_gates() if w == GATES_AT else None)
            pe.wait_ge(gate_step, GATE_AT["sums_exp"])
            with pe.Fori(0, ROUNDS - 1) as r:
                mixer = gdn(r)
                body("l1r", r, 0, 4, hT_hi, hT_lo, [None] * 4, between=lambda w: next(mixer, None))
                for _ in mixer:
                    pass

            def o_transposes(n):
                r = O_ORDER[n]
                pe.wait_ge(gated, 2 * r + 2)
                if n:
                    pe.wait_ge(o_lo, 2 * n)
                for g in range(2):
                    transposes(lambda m, t: o_z[r][:, m, (4 * g + t) * P:(4 * g + t + 1) * P], aux[g], 4).then_inc(o_tr, 1)

            def after_unit(w):
                next(mixer, None)
                if w in O_SLOTS:
                    if w == O_SLOTS[0]:
                        pe.wait_ge(gdn_step, (ROUNDS - 1) * GDN_N + GDN_AT["o_norm"])
                    o_transposes(O_SLOTS.index(w))
            mixer = gdn(ROUNDS - 1)
            body("l1z", 0, 0, 8, hT_hi, hT_lo, [None] * 8, between=after_unit)
            o_transposes(3)
            pe.wait_ge(o_lo, 8)
            residual_phase("out1", oT_hi, oT_lo, True)
            pe.wait_ge(xlo_done, 16)
            ffn("gu1", "dn1", FF // NB)
            residual_phase("dn1", fT_hi, fT_lo, False)

        @block.scalar
        def _(act):
            def body(name, i, n_body, hook):
                upb = UPB[name]
                for b in range(n_body):
                    for j in range(upb):
                        w = b * upb + j
                        s = w % SLOTS
                        act.wait_ge(raw_in[s], i * (n_body * upb // SLOTS * 16) + 16 * ((UNIT0[name] + w) // SLOTS + 1))
                        if not (isinstance(i, int) and i * n_body * upb + UNIT0[name] + w < SLOTS):
                            act.wait_ge(unit_used, i * (n_body * upb) + (UNIT0[name] + w - SLOTS + 1))
                        nc.scalar.activation(whi[:, s, :], wraw[:, s, :], ACT.Copy).then_inc(hi_done, 1)
                        hook(i, b, j)

            def tail(name, width):
                for j in range(4):
                    act.wait_ge(raw_in[j], 16 * ((UNIT0[name] + j) // SLOTS + 1))
                    act.wait_ge(unit_used, UNIT0[name] + j - SLOTS + 1)
                    nc.scalar.activation(whi[:, j, 0:4 * width], wraw[:, j, 0:4 * width], ACT.Copy).then_inc(hi_done, 1)

            def copy_out(name, n, parity, dst, func=ACT.Copy):
                act.wait_ge(unit_used, n * UPB[name] + (UNIT0[name] + UPB[name]))
                for m in range(M):
                    a = nc.scalar.activation(dst(m), acc[parity][:, m, :], func, scale=rstd[:, m:m + 1])
                return a.then_inc(acc_read[parity], 1)

            def root(norm):
                act.wait_ge(mean_done, norm + 1)
                nc.scalar.activation(rms[:], mean[:], ACT.Sqrt, bias=epsc[:, 0:1], scale=1.0 / D).then_inc(rms_done, 1)
                act.wait_ge(rstd_done, norm + 1)

            def x_block(norm, n, src):
                k = n + 4 * norm
                for m in range(M):
                    a = nc.scalar.activation(aux[1][:, m * NB:(m + 1) * NB], src(m), ACT.Square,
                                             accum_out=ssq[:, m, bass.ds(n, 1)])
                if norm < 4:
                    act.wait_ge(xt_ready, k + 1)
                    for t in range(4):
                        a = nc.scalar.activation(hT_hi[:, bass.ds(n * 4 + t, 1), :].rearrange("p a b -> p (a b)"),
                                                 aux[0][:, t * SEQ:(t + 1) * SEQ], ACT.Copy,
                                                 scale=gains[:, norm, bass.ds(n * 4 + t, 1)])
                a.then_inc(xhi_done, 1)

            def residual_phase(name):
                norm = NORM_OF[name]

                def hook(i, b, j):
                    if j == 7 and not (b == 0 and isinstance(i, int) and i == 0):
                        n = i * 2 + (b - 1)
                        act.drain()
                        act.wait_ge(acc_read[1 - b], i + (BLOCK0[name] // 2 + b))
                        x_block(norm, n, lambda m: xs[:, m, :])
                body(name, 0, 2, hook)
                with act.Fori(1, 2) as i:
                    body(name, i, 2, hook)
                act.drain()
                act.wait_ge(acc_read[1], BLOCK0[name] // 2 + 2)
                x_block(norm, 3, lambda m: xs[:, m, :])

            def ffn(name, norm, n0):
                def f_hi(i):
                    act.wait_ge(ft_ready, i + n0)
                    nc.scalar.activation(fT_hi[:, bass.ds(i * 4 - 4, 4), :].rearrange("p a b -> p (a b)"), aux[1][:, :], ACT.Copy
                                         ).then_inc(fhi_done, 1)

                def hook(i, b, j):
                    first = isinstance(i, int) and i == 0
                    if first and b == 0 and j == 1:
                        root(norm)
                    if b == 1 and j == 3:
                        if not (first and n0 == 0):
                            act.wait_ge(acc_read[1], i + BLOCK0[name] // 2)
                        copy_out(name, i * 2, 0, lambda m: sg[:, m, :], ACT.Silu)
                    if b == 0 and j == 7 and not first:
                        f_hi(i)
                body(name, 0, 2, hook)
                with act.Fori(1, FF // NB) as i:
                    body(name, i, 2, hook)
                f_hi(FF // NB)

            act.wait_ge(x_in, 16)
            act.wait_ge(consts_in, 16 * 5)
            act.wait_ge(eps_set, 1)
            for n in range(4):
                act.drain()
                x_block(0, n, lambda m: x[:, m, n * NB:(n + 1) * NB])

            def l0(name):
                act.wait_ge(l0_step, L0_AT[name])

            def done(a):
                a.then_inc(l0_step, 1)

            def head_squares(base, h, to):
                for m in range(M):
                    nc.scalar.activation(aux4[1][:, m * 256:(m + 1) * 256], pr[:, m, base + h * 256:base + (h + 1) * 256],
                                         ACT.Square, accum_out=gate_t[:, 9, to + h * 2 + m:to + h * 2 + m + 1])

            def head_rms(at):
                act.drain()
                return nc.scalar.activation(gate_t[:, 9, 8:16], gate_t[:, 9, at:at + 8], ACT.Sqrt, bias=epsc[:, 0:1], scale=1.0 / 256)

            def l0_mixer():
                l0("pos")
                done(nc.scalar.activation(cs[:].rearrange("p a b c -> p (a b c)"), ang[:].rearrange("p a b c -> p (a b c)"), ACT.Sin))
                for i in range(2 * M):
                    yield
                    l0(f"rot{i}_tr")
                    dst = (qrT, krT)[i // M]
                    m = i % M
                    done(nc.scalar.activation(dst[:, :, m * P:(m + 1) * P], aux[i % 2][:, :].rearrange("p (a b) -> p a b", b=P), ACT.Copy))
                yield
                g8 = gate_t[:, 0, 0:16]
                l0("gates")
                done(nc.scalar.activation(g8, g8, ACT.Tanh, scale=1.0 / SOFTCAP))
                l0("cap")
                done(nc.scalar.activation(gate_t[:, 2, 0:8], gate_t[:, 2, 0:8], ACT.Exp, scale=-1.0))
                yield
                l0("m_tr")
                nc.scalar.activation(qmT[:, :, :].rearrange("p a b -> p (a b)"), aux[0][:, :], ACT.Copy)
                done(nc.scalar.activation(kmT[:, :, :].rearrange("p a b -> p (a b)"), aux[1][:, :], ACT.Copy))
                for h in range(RH):
                    yield
                    yield
                    l0(f"r{h}_o_psum")
                    done(nc.scalar.activation(pr[:, :, VR + h * RD:VR + (h + 1) * RD], aux4[2].rearrange("p (m n) -> p m n", m=M), ACT.Copy))
                    act.drain()
                    head_squares(VR, h, 24)
                for h in range(MH):
                    yield
                    l0(f"m{h}_d_max")
                    if h:
                        act.drain()
                        head_squares(VM, h - 1, 16)
                    nc.scalar.activation(p_sb[:, 0:P], d_sb[:, 0:P], ACT.Exp, bias=gate_t[:, 5, 0:1])
                    nc.scalar.activation(p_sb[:, P:3 * P], d_sb[:, P:3 * P], ACT.Exp, bias=gate_t[:, 5, 1:2])
                    done(nc.scalar.activation(gate_t[:, 5, 2:4], gate_t[:, 5, 0:2], ACT.Exp))
                    yield
                    yield
                    l0(f"m{h}_st_psum")
                    done(nc.scalar.activation(st_sb[:], aux4[0][:, 0:3 * P], ACT.Copy))
                    yield
                yield
                l0(f"m{MH - 1}_num_div")
                head_squares(VM, MH - 1, 16)
                head_rms(16)
                done(nc.scalar.activation(pr[:, :, OM:OM + 1024], pr[:, :, OM:OM + 1024], ACT.Sigmoid))
                for g in range(4):
                    if g == 2:
                        yield
                        l0("mix1_lo")
                        head_rms(24)
                        done(nc.scalar.activation(pr[:, :, GR:GR + 1024], pr[:, :, GR:GR + 1024], ACT.Silu))
                    yield
                    l0(f"mix{g}_tr")
                    done(nc.scalar.activation(mixT_hi[:, 4 * g:4 * g + 4, :].rearrange("p a b -> p (a b)"), aux[g % 2][:, :], ACT.Copy))

            def pr_out(name, i, b):
                first = {"l0a": QR, "l0b": QM, "l0c": VR}[name]
                copy_out(name, i * 2 + (b - 1), (b + 1) % 2, lambda m: pr[:, m, bass.ds(i * 2 * NB + (first + (b - 1) * NB), NB)])

            def hook_a(i, b, j):
                first = isinstance(i, int) and i == 0 and b == 0
                if first and j == 1:
                    root(0)
                if j == 3 and not first:
                    pr_out("l0a", i, b)

            def hook_b(i, b, j):
                if j == 3:
                    pr_out("l0a" if b == 0 else "l0b", 1 if b == 0 else 0, 2 if b == 0 else 1)
                l0_slots(mixer, b * UPB["l0b"] + j - AHEAD)

            def hook_c(i, b, j):
                if j == 3:
                    pr_out("l0b" if b == 0 else "l0c", 0, 2 if b == 0 else b)
                l0_slots(mixer, 20 + b * UPB["l0c"] + j - AHEAD)

            body("l0a", 0, 2, hook_a)
            body("l0a", 1, 2, hook_a)
            mixer = l0_mixer()
            body("l0b", 0, 2, hook_b)
            tail("l0t", 8)
            body("l0c", 0, 8, hook_c)
            pr_out("l0c", 0, 8)
            act.drain()
            for _ in mixer:
                pass

            residual_phase("out0")
            ffn("gu0", 1, 0)
            residual_phase("dn0")

            tail("l1t", 64)
            root(2)
            def gdn_gates():
                act.wait_ge(l1_const, 16 * 4)
                act.wait_ge(gate_step, GATE_AT["raw"])
                nc.scalar.activation(gate_t[:, 2, :], gate_t[:, 2, :], ACT.Exp, scale=-1.0)
                nc.scalar.activation(gate_t[:, 8, 0:32], gate_t[:, 8, 0:32], ACT.Exp)
                nc.scalar.activation(gate_t[:, 0, :], gate_t[:, 0, :], ACT.Sigmoid).then_inc(gate_step, 1)
                act.wait_ge(gate_step, GATE_AT["sums"])
                nc.scalar.activation(gate_t[:, 4, :], aux4[2][:, 0:64], ACT.Exp)
                nc.scalar.activation(gate_t[:, 5, :], aux4[3][:, 0:64], ACT.Exp).then_inc(gate_step, 1)

            def gdn(r):
                def at(name):
                    act.wait_ge(gdn_step, r * GDN_N + GDN_AT[name])

                def done(a):
                    a.then_inc(gdn_step, 1)

                def gat(g, name):
                    act.wait_ge(group_step[g], r * GROUP_N + GROUP_AT[name])

                flat = lambda t: t.rearrange("p a b -> p (a b)")
                for b in range(4):
                    if b:
                        yield
                    at(f"c{b}_x_tr")
                    dst = (qkT[:, 0:4], qkT[:, 4:8], vT[:, 0:4], vT[:, 4:8])[b]
                    for t in range(4):
                        a = nc.scalar.activation(dst[:, t, :], aux[0][:, t * SEQ:(t + 1) * SEQ], ACT.Copy,
                                                 scale=conv_r[:, 4 * b + t, CW - 1:CW])
                    done(a)
                    at(f"c{b}_conv")
                    done(nc.scalar.activation(flat(dst), flat(dst), ACT.Silu))
                act.drain()
                for b in range(2):
                    if b:
                        at("n0_mul")
                    blk = flat(qkT[:, 4 * b:4 * b + 4, :])
                    done(nc.scalar.activation(flat(sq[:]), blk, ACT.Square))
                    yield
                    at(f"n{b}_sum")
                    done(nc.scalar.activation(flat(rn[:]), aux[0][:, :], ACT.Sqrt, bias=epsc[:, 1 - b:2 - b],
                                              scale=1.0 if b else float(GD)))
                for name, dst in (("k", flat(k_tok[:])), ("v0", v_tok[:, :, 0:NB]), ("v1", v_tok[:, :, NB:])):
                    yield
                    at(name + "_tr")
                    src = aux[0][:, :] if name == "k" else aux[0][:, :].rearrange("p (m n) -> p m n", m=M)
                    done(nc.scalar.activation(dst, src, ACT.Copy))
                for c in range(M):
                    u = f"t{c}_"
                    yield
                    for g in range(2):
                        gat(g, u + "d_psum")
                        nc.scalar.activation(flat(EA[g][:]), aux[g][:, 0:NB], ACT.Exp).then_inc(group_step[g], 1)
                    yield
                    for n in range(len(LEVELS)):
                        yield
                        if n:
                            for g in range(2):
                                gat(g, u + f"l{n}_q_psum")
                                nc.scalar.activation(flat(Q1[g][:]), aux[g][:, 0:NB], ACT.Copy).then_inc(group_step[g], 1)
                            yield
                    if c:
                        yield
                    yield
                    for g in range(2):
                        gat(g, u + "vn_psum")
                        nc.scalar.activation(flat(Vn[g][:]), aux[g][:, 0:NB], ACT.Copy).then_inc(group_step[g], 1)
                    yield
                    if not c:
                        for g in range(2):
                            gat(g, u + "o")
                            nc.scalar.activation(flat(St[:, 4 * g:4 * g + 4, :]), aux[g][:, 0:NB], ACT.Copy).then_inc(group_step[g], 1)
                yield
                for g in range(2):
                    gat(g, "t1_o")
                done(nc.scalar.activation(o_sq[:].rearrange("p m h n -> p (m h n)"), flat(o_r[:]), ACT.Square))
                at("o_sum")
                done(nc.scalar.activation(flat(o_ms[:]), flat(o_ms[:]), ACT.Sqrt, bias=epsc[:, 0:1], scale=1.0 / GD))

            def qkv_out(name, n, b, q):
                copy_out(name, n, b % 2, lambda m: qkv[:, m, q * NB:(q + 1) * NB])

            def z_out(n):
                if n:
                    act.wait_ge(gated, n)
                copy_out("l1z", n, n % 2, lambda m: zs[n][:, m, :], ACT.Silu)

            def hook_q(i, b, j):
                if j == 3 and b:
                    qkv_out("l1q", b - 1, b - 1, b - 1)
                if b * UPB["l1q"] + j == GATES_AT + AHEAD:
                    gdn_gates()

            def hook_r(r, b, j):
                if j == 3 and b:
                    qkv_out("l1r", r * 4 + (b - 1), b - 1, b - 1)
                if b * UPB["l1r"] + j >= AHEAD:
                    next(mixer, None)

            def o_split(n):
                act.wait_ge(o_tr, 2 * n + 2)
                for g in range(2):
                    t = O_ORDER[n] * HV + 4 * g
                    nc.scalar.activation(oT_hi[:, t:t + 4, :].rearrange("p a b -> p (a b)"), aux[g][:, :], ACT.Copy
                                         ).then_inc(o_hi, 1)

            def hook_z(i, b, j):
                w = b * UPB["l1z"] + j
                if j == 3 and b:
                    z_out(b - 1)
                if w >= AHEAD:
                    next(mixer, None)
                if w == 6 + AHEAD:
                    act.wait_ge(gdn_step, (ROUNDS - 1) * GDN_N + GDN_AT["c3_x_tr"])
                    act.wait_ge(o_stored, 16 * (ROUNDS - 1))
                    for r in range(ROUNDS - 1):
                        act.dma_start(o_z[r][:], o_dram[:, r * HV * GD:(r + 1) * HV * GD].rearrange("(m p) n -> p m n", p=P)
                                      ).then_inc(o_loaded[r], 16)
                if w - AHEAD in O_SLOTS:
                    o_split(O_SLOTS.index(w - AHEAD))

            act.wait_ge(xs_copied, 8)
            body("l1q", 0, 4, hook_q)
            qkv_out("l1q", 3, 3, 3)
            with act.Fori(0, ROUNDS - 1) as r:
                mixer = gdn(r)
                body("l1r", r, 4, hook_r)
                for _ in mixer:
                    pass
                qkv_out("l1r", r * 4 + 3, 3, 3)
            mixer = gdn(ROUNDS - 1)
            body("l1z", 0, 8, hook_z)
            z_out(7)
            o_split(3)
            residual_phase("out1")
            ffn("gu1", 3, FF // NB)
            residual_phase("dn1")
            root(4)

        @block.vector
        def _(dve):
            V = nc.vector

            def body(name, i, n_body, hook):
                upb = UPB[name]
                for b in range(n_body):
                    for j in range(upb):
                        w = b * upb + j
                        s = w % SLOTS
                        dve.wait_ge(hi_done, i * (n_body * upb) + (UNIT0[name] + w + 1))
                        if not (isinstance(i, int) and i * n_body * upb + UNIT0[name] + w < SLOTS):
                            dve.wait_ge(unit_used, i * (n_body * upb) + (UNIT0[name] + w - SLOTS + 1))
                        V.tensor_tensor(wlo[:, s, :], wraw[:, s, :], whi[:, s, :].bitcast(F32), ALU.subtract).then_inc(lo_done, 1)
                        hook(i, b, j)

            def tail(name, width):
                for j in range(4):
                    dve.wait_ge(hi_done, UNIT0[name] + j + 1)
                    dve.wait_ge(unit_used, UNIT0[name] + j - SLOTS + 1)
                    V.tensor_tensor(wlo[:, j, 0:4 * width], wraw[:, j, 0:4 * width], whi[:, j, 0:4 * width].bitcast(F32),
                                    ALU.subtract).then_inc(lo_done, 1)

            def recip(norm):
                dve.wait_ge(rms_done, norm + 1)
                V.reciprocal(rstd[:], rms[:]).then_inc(rstd_done, 1)
                dve.drain()

            def x_lo(norm, n):
                dve.wait_ge(xhi_done, n + (4 * norm + 1))
                if norm < 4:
                    for t in range(4):
                        a = V.scalar_tensor_tensor(
                            hT_lo[:, bass.ds(n * 4 + t, 1), :].rearrange("p a b -> p (a b)"),
                            aux[0][:, t * SEQ:(t + 1) * SEQ], gains[:, norm, bass.ds(n * 4 + t, 1)],
                            hT_hi[:, bass.ds(n * 4 + t, 1), :].rearrange("p a b -> p (a b)").bitcast(F32),
                            op0=ALU.mult, op1=ALU.subtract)
                    a.then_inc(xlo_done, 1)

            def mean_square():
                V.tensor_reduce(mean[:], ssq[:], AX.X, ALU.add).then_inc(mean_done, 1)

            def residual_phase(name):
                norm = NORM_OF[name]

                def add(n, parity):
                    dve.wait_ge(unit_used, n * UPB[name] + (UNIT0[name] + UPB[name]))
                    if not (norm == 1 and isinstance(n, int) and n == 0):
                        dve.wait_ge(xs_copied, n + 4 * (norm - 1))
                    dve.wait_ge(xhi_done, n + 4 * norm)
                    V.tensor_tensor(xs[:], acc[parity][:, :, :], x[:, :, bass.ds(n * NB, NB)], ALU.add
                                    ).then_inc(acc_read[parity], 1)

                def hook(i, b, j):
                    if b == 0 and isinstance(i, int) and i == 0:
                        return
                    if j == 3:
                        add(i * 2 + (b - 1), (b + 1) % 2)
                    if j == 7:
                        x_lo(norm, i * 2 + (b - 1))
                body(name, 0, 2, hook)
                with dve.Fori(1, 2) as i:
                    body(name, i, 2, hook)
                add(3, 1)
                x_lo(norm, 3)
                mean_square()

            def ffn(name, norm, n0):
                def up(i):
                    dve.wait_ge(acc_read[0], i + BLOCK0[name] // 2)
                    dve.wait_ge(unit_used, i * (2 * UPB[name]) + UNIT0[name])
                    if isinstance(i, int) and i == 1:
                        dve.wait_ge(xs_copied, 4 * norm)
                    else:
                        dve.wait_ge(ft_ready, i + (n0 - 1))
                    for m in range(M):
                        a = V.scalar_tensor_tensor(prod[:, m, :], acc[1][:, m, :], rstd[:, m:m + 1], sg[:, m, :],
                                                   op0=ALU.mult, op1=ALU.mult)
                    a.then_inc(acc_read[1], 1)

                def f_lo(i):
                    dve.wait_ge(fhi_done, i + n0)
                    V.tensor_tensor(fT_lo[:, bass.ds(i * 4 - 4, 4), :].rearrange("p a b -> p (a b)"), aux[1][:, :],
                                    fT_hi[:, bass.ds(i * 4 - 4, 4), :].rearrange("p a b -> p (a b)").bitcast(F32), ALU.subtract
                                    ).then_inc(flo_done, 1)

                def hook(i, b, j):
                    first = isinstance(i, int) and i == 0
                    if first and b == 0 and j == 1:
                        recip(norm)
                    if b == 0 and not first:
                        if j == 3:
                            up(i)
                        if j == 7:
                            f_lo(i)
                body(name, 0, 2, hook)
                body(name, 1, 2, hook)
                with dve.Fori(2, FF // NB) as i:
                    body(name, i, 2, hook)
                up(FF // NB)
                f_lo(FF // NB)

            def log1p(dst, y, w):
                z, z2, p = (gate_t[:, k, 0:w] for k in (5, 6, 7))
                V.tensor_scalar(z, y, 2.0, None, ALU.add)
                dve.drain()
                V.reciprocal(z, z)
                dve.drain()
                V.tensor_tensor(z, z, y, ALU.mult)
                dve.drain()
                V.tensor_tensor(z2, z, z, ALU.mult)
                dve.drain()
                V.tensor_scalar(p, z2, 1.0 / 15, None, ALU.mult)
                for k in (13, 11, 9, 7, 5, 3):
                    dve.drain()
                    V.scalar_tensor_tensor(p, p, 1.0 / k, z2, op0=ALU.add, op1=ALU.mult)
                dve.drain()
                V.scalar_tensor_tensor(p, p, 1.0, z, op0=ALU.add, op1=ALU.mult)
                dve.drain()
                V.tensor_scalar(dst, p, 2.0, None, ALU.mult)
                dve.drain()

            V.memset(epsc[:, 0:1], EPS)
            V.memset(epsc[:, 1:2], GD * EPS).then_inc(eps_set, 1)
            dve.wait_ge(consts_in, 16 * 5)
            for n in range(4):
                x_lo(0, n)
            mean_square()
            nothing = lambda i, b, j: None
            flat2 = lambda t: t.rearrange("p a b -> p (a b)")
            col = lambda k, a, b: gate_t[:, k, a:b]

            def l0(name):
                dve.wait_ge(l0_step, L0_AT[name])

            def done(a):
                a.then_inc(l0_step, 1)

            def projected(blocks):
                for b in range(2):
                    dve.wait_ge(acc_read[b], blocks // 2)

            def head_norm(base, gate_col, row):
                V.reciprocal(col(6, 16, 24), col(9, 8, 16))
                dve.drain()
                for h in range(4):
                    for m in range(M):
                        y = pr[:, m, base + h * 256:base + (h + 1) * 256]
                        s = col(6, 16 + 2 * h + m, 17 + 2 * h + m)
                        other = row[:, h * 256:(h + 1) * 256] if row is not None else pr[:, m, gate_col + h * 256:gate_col + (h + 1) * 256]
                        a = V.scalar_tensor_tensor(y, y, s, other, op0=ALU.mult, op1=ALU.mult)
                if row is not None:
                    dve.drain()
                    a = V.tensor_tensor(pr[:, :, base:base + 1024], pr[:, :, base:base + 1024],
                                        pr[:, :, gate_col:gate_col + 1024], ALU.mult)
                done(a)

            def rows(h):
                lf = [col(4, 4 * m + h, 4 * m + h + 1) for m in range(M)]
                li = [col(0, 8 * m + h, 8 * m + h + 1) for m in range(M)]
                V.tensor_scalar(d_rows[:, 0, :], C["after"], lf[0], None, ALU.mult)
                V.tensor_scalar(d_rows[:, 1, :], C["ones"], lf[1], None, ALU.mult)
                V.tensor_scalar(d_rows[:, 2, :], C["after"], lf[1], None, ALU.mult)
                V.tensor_scalar(d_rows[:, 4, :], ident, li[1], None, ALU.mult)
                V.tensor_scalar(d_rows[:, 5, :], ident, li[0], None, ALU.mult)
                dve.drain()
                done(V.tensor_tensor(d_rows[:, 3, :], d_rows[:, 0, :], d_rows[:, 5, :], ALU.add))

            def rotate(i):
                m = i % M
                src = pr[:, m, (QR, KR)[i // M]:(QR, KR)[i // M] + 1024].rearrange("p (h n two) -> p h n two", h=RH, two=2)
                t1, t2 = src[:, :, :, 0], src[:, :, :, 1]
                cos, sin = (cs[:, k, m, :].unsqueeze(1).to_broadcast([P, RH, P]) for k in (0, 1))
                for half, (f1, f2, op) in enumerate(((cos, sin, ALU.subtract), (sin, cos, ALU.add))):
                    V.tensor_tensor(rot_a[:], t1, f1, ALU.mult)
                    V.tensor_tensor(rot_b[:], t2, f2, ALU.mult)
                    dve.drain()
                    a = V.tensor_tensor(rot[:, :, half, :], rot_a[:], rot_b[:], op)
                    if half == 0:
                        dve.drain()
                done(a)

            def l0_mixer():
                V.tensor_copy(col(9, 2, 4), gate_t[:, 9, 0:2].bitcast(I32))
                dve.drain()
                for m in range(M):
                    V.tensor_scalar(ang[:, 1, m, :], C["freq"], col(9, 2 + m, 3 + m), None, ALU.mult)
                dve.drain()
                sin_a, cos_a = flat2(ang[:, 1]), flat2(ang[:, 0])
                turns = rot_a[:, 0:2, :].rearrange("p a b -> p (a b)")
                MAGIC = 12582912.0
                V.tensor_scalar(turns, sin_a, 1.0 / (2 * np.pi), None, ALU.mult)
                dve.drain()
                V.tensor_scalar(turns, turns, MAGIC, None, ALU.add)
                dve.drain()
                V.tensor_scalar(turns, turns, -MAGIC, None, ALU.add)
                dve.drain()
                for part in TWO_PI:
                    V.scalar_tensor_tensor(sin_a, turns, -part, sin_a, op0=ALU.mult, op1=ALU.add)
                    dve.drain()
                V.tensor_scalar(cos_a, sin_a, float(np.pi / 2), None, ALU.add)
                dve.drain()
                V.tensor_scalar(turns, cos_a, float(np.pi), -2 * float(np.pi), ALU.is_gt, ALU.mult)
                dve.drain()
                V.tensor_tensor(cos_a, cos_a, turns, ALU.add)
                dve.drain()
                both = ang[:].rearrange("p a b c -> p (a b c)")
                done(V.tensor_scalar(both, both, PI_BELOW, -PI_BELOW, ALU.min, ALU.max))
                l0("sincos")
                projected(2)
                rotate(0)
                for i in range(2 * M):
                    yield
                    if i < 2 * M - 1:
                        l0(f"rot{i}_copy")
                        projected(2 if i == 0 else 4)
                        rotate(i + 1)
                yield
                l0("rot3_copy")
                dve.wait_ge(unit_used, UNIT0["l0t"] + 4)
                for m in range(M):
                    a = V.scalar_tensor_tensor(col(0, 8 * m, 8 * m + 8), aux4[2 + m][:, 0:8], rstd[:, m:m + 1], col(8, 0, 8),
                                               op0=ALU.mult, op1=ALU.add)
                done(a)
                l0("tanh")
                V.tensor_scalar(col(0, 0, 16), col(0, 0, 16), SOFTCAP, None, ALU.mult)
                dve.drain()
                fg = col(0, 0, 16).rearrange("p (m c) -> p m c", m=M)[:, :, 4:8]
                pair = lambda k: col(k, 0, 8).rearrange("p (m c) -> p m c", m=M)
                done(V.scalar_tensor_tensor(pair(2), fg, -1.0, fg, op0=ALU.mult, op1=ALU.max))
                l0("exp")
                log1p(col(3, 0, 8), col(2, 0, 8), 8)
                done(V.scalar_tensor_tensor(pair(4), fg, 0.0, pair(3), op0=ALU.min, op1=ALU.subtract))
                dve.drain()
                yield
                for h in range(RH):
                    yield
                    l0(f"r{h}_s_psum")
                    dec = C["decay"][:, h * 256:(h + 1) * 256]
                    V.tensor_tensor(rs_sb[:, 0:256], aux4[0][:, 0:256], dec, ALU.mult)
                    done(V.tensor_tensor(rs_sb[:, 256:384], aux4[0][:, 256:384], dec[:, 0:P], ALU.mult))
                    yield
                for h in range(MH):
                    l0("r3_o_copy" if h == 0 else f"m{h - 1}_num_div")
                    rows(h)
                    yield
                    l0(f"m{h}_d_psum")
                    V.tensor_tensor(d_sb[:], aux4[0][:, 0:3 * P], C["neg"], ALU.add)
                    dve.drain()
                    V.tensor_reduce(col(6, 0, 1), d_sb[:, 0:P], AX.X, ALU.max)
                    V.tensor_reduce(col(6, 1, 2), d_sb[:, P:3 * P], AX.X, ALU.max)
                    dve.drain()
                    done(V.tensor_scalar(col(5, 0, 2), col(6, 0, 2), -1.0, None, ALU.mult))
                    yield
                    l0(f"m{h}_s_psum")
                    V.scalar_tensor_tensor(d_sb[:, 0:P], aux4[2][:, 0:P], MDQK ** -0.5, p_sb[:, 0:P],
                                           op0=ALU.mult, op1=ALU.mult, accum_out=col(6, 2, 3))
                    V.scalar_tensor_tensor(d_sb[:, P:3 * P], aux4[2][:, P:3 * P], MDQK ** -0.5, p_sb[:, P:3 * P],
                                           op0=ALU.mult, op1=ALU.mult, accum_out=col(6, 3, 4))
                    dve.drain()
                    V.scalar_tensor_tensor(col(6, 4, 6), col(6, 2, 4), -1.0, col(6, 2, 4), op0=ALU.mult, op1=ALU.max)
                    dve.drain()
                    V.tensor_tensor(col(6, 4, 6), col(6, 4, 6), col(5, 2, 4), ALU.max)
                    dve.drain()
                    done(V.reciprocal(col(6, 6, 8), col(6, 4, 6)))
                    yield
                    yield
                    l0(f"m{h}_num_psum")
                    for m in range(M):
                        a = V.tensor_scalar(pr[:, m, VM + h * MDV:VM + (h + 1) * MDV], aux4[2][:, m * 256:(m + 1) * 256],
                                            col(6, 6 + m, 7 + m), None, ALU.mult)
                    done(a)
                yield
                l0("m_sq")
                dve.wait_ge(consts_in, 16 * 5)
                head_norm(VM, OM, mnorm[:])
                for g in range(4):
                    if g == 2:
                        yield
                        l0("r_sq")
                        head_norm(VR, GR, None)
                    yield
                    l0(f"mix{g}_hi")
                    done(V.tensor_tensor(flat2(mixT_lo[:, 4 * g:4 * g + 4, :]), aux[g % 2][:, :],
                                         flat2(mixT_hi[:, 4 * g:4 * g + 4, :]).bitcast(F32), ALU.subtract))

            body("l0a", 0, 2, lambda i, b, j: recip(0) if b == 0 and j == 1 else None)
            body("l0a", 1, 2, nothing)
            mixer = l0_mixer()
            body("l0b", 0, 2, lambda i, b, j: l0_slots(mixer, b * UPB["l0b"] + j - AHEAD))
            tail("l0t", 8)
            body("l0c", 0, 8, lambda i, b, j: l0_slots(mixer, 20 + b * UPB["l0c"] + j - AHEAD))
            for _ in mixer:
                pass

            residual_phase("out0")
            ffn("gu0", 1, 0)
            residual_phase("dn0")

            tail("l1t", 64)
            recip(2)
            def gdn_gates():
                dve.wait_ge(l1_const, 16 * 4)
                dve.wait_ge(unit_used, UNIT0["l1t"] + 4)
                for m in range(M):
                    mm = slice(32 * m, 32 * m + 32)
                    V.tensor_scalar(gate_t[:, 0, mm], aux4[2 + m][:, 0:32], rstd[:, m:m + 1], None, ALU.mult)
                    V.scalar_tensor_tensor(gate_t[:, 1, mm], aux4[2 + m][:, 32:64], rstd[:, m:m + 1], gate_t[:, 8, 32:64],
                                           op0=ALU.mult, op1=ALU.add)
                dve.drain()
                a_pre = gate_t[:, 1, :]
                V.scalar_tensor_tensor(gate_t[:, 2, :], a_pre, -1.0, a_pre, op0=ALU.mult, op1=ALU.max).then_inc(gate_step, 1)
                dve.wait_ge(gate_step, GATE_AT["exp"])
                log1p(gate_t[:, 3, :], gate_t[:, 2, :], 64)
                V.scalar_tensor_tensor(gate_t[:, 3, :], a_pre, 0.0, gate_t[:, 3, :], op0=ALU.max, op1=ALU.add)
                dve.drain()
                for m in range(M):
                    mm = slice(32 * m, 32 * m + 32)
                    a = V.scalar_tensor_tensor(gate_t[:, 1, mm], gate_t[:, 3, mm], -1.0, gate_t[:, 8, 0:32], op0=ALU.mult, op1=ALU.mult)
                a.then_inc(gate_step, 1)
                dve.wait_ge(gate_step, GATE_AT["sums_exp"])
                V.memset(gate_t[:, 2:4, :], 0.0)
                V.memset(gate_t[:, 6, :], 0.0)
                V.scalar_tensor_tensor(gate_t[:, 7, :], gate_t[:, 0, :], -1.0, gate_t[:, 4, :], op0=ALU.mult, op1=ALU.mult
                                       ).then_inc(gdn_step, 1)
                dve.drain()

            def gdn(r):
                def at(name):
                    dve.wait_ge(gdn_step, r * GDN_N + GDN_AT[name])

                def done(a):
                    a.then_inc(gdn_step, 1)

                dve.wait_ge(acc_read[0], r * 2 + BLOCK0["l1r"] // 2)
                dve.wait_ge(acc_read[1], r * 2 + BLOCK0["l1r"] // 2)
                per_round = gate_t[:, 0:8, :].rearrange("p s (m h) -> p (s m) h", m=M)
                V.tensor_copy(gr[:].rearrange("p s m h -> p (s m) h"), per_round[:, :, bass.ds(r * HV, HV)])
                V.tensor_copy(conv_r[:, 0:4, :], conv_w[:, bass.ds(r * 4, 4), :])
                V.tensor_copy(conv_r[:, 4:8, :], conv_w[:, bass.ds(r * 4 + 16, 4), :])
                done(V.tensor_copy(conv_r[:, 8:16, :], conv_w[:, bass.ds(r * 8 + 32, 8), :]))
                dve.drain()

                def per_head(slot, c, g):
                    return gr[:, slot, c, 4 * g:4 * g + 4].unsqueeze(2).to_broadcast([P, 4, P])

                def all_heads(t, n=4):
                    return t.unsqueeze(1).to_broadcast([P, n, t.shape[1]])

                heads = lambda t: t.rearrange("p (h n) -> p h n", n=P)
                twice = lambda t: t.rearrange("p (q e) n -> p q e n", e=2)
                for b in range(4):
                    if b:
                        yield
                    at(f"c{b}_tap3")
                    dst = (qkT[:, 0:4], qkT[:, 4:8], vT[:, 0:4], vT[:, 4:8])[b]
                    for lag in range(1, CW):
                        for t in range(4):
                            a = V.scalar_tensor_tensor(dst[:, t, lag:], aux[0][:, t * SEQ:(t + 1) * SEQ - lag],
                                                       conv_r[:, 4 * b + t, CW - 1 - lag:CW - lag], dst[:, t, lag:],
                                                       op0=ALU.mult, op1=ALU.add)
                        if lag < CW - 1:
                            dve.drain()
                    done(a)
                for b in range(2):
                    yield
                    at(f"n{b}_sqrt")
                    V.reciprocal(rn[:], rn[:])
                    dve.drain()
                    blk = qkT[:, 4 * b:4 * b + 4, :]
                    done(V.tensor_tensor(blk, blk, rn[:], ALU.mult))
                yield
                yield
                yield

                def gat(g, name):
                    dve.wait_ge(group_step[g], r * GROUP_N + GROUP_AT[name])

                def gdone(g, a):
                    a.then_inc(group_step[g], 1)

                at("v1_copy")
                for c in range(M):
                    u = f"t{c}_"
                    for g in range(2):
                        if c:
                            gat(g, "t0_s_copy")
                        gdone(g, V.tensor_tensor(lam[g][:], all_heads(C["after"]), per_head(1, c, g), ALU.mult))
                    yield
                    yield
                    for g in range(2):
                        gat(g, u + "kq_psum")
                        V.tensor_tensor(kq[g][:], aux[g][:, 0:NB].rearrange("p (h n) -> p h n", h=2),
                                        all_heads(C["low_up"], 2), ALU.mult)
                        V.tensor_tensor(EA[g][:], EA[g][:], per_head(0, c, g), ALU.mult)
                        pair_of = lambda half: kq[g][:, :, half * P:(half + 1) * P].unsqueeze(2).to_broadcast([P, 2, 2, P])
                        dve.drain()
                        V.tensor_tensor(twice(ET[g][:]), twice(heads(aux[g][:, NB:])), pair_of(1), ALU.mult)
                        gdone(g, V.tensor_tensor(twice(EA[g][:]), twice(EA[g][:]), pair_of(0), ALU.mult))
                    for n in range(len(LEVELS)):
                        yield
                        if n == 0:
                            for g in range(2):
                                gat(g, u + "l0_q_psum")
                                V.tensor_tensor(T[g][:], all_heads(ident), Bm[g][0][:], ALU.subtract)
                                gdone(g, V.tensor_tensor(TT[g][:], all_heads(ident), heads(aux[g][:, 0:NB]), ALU.subtract))
                        else:
                            yield
                            for g in range(2):
                                gat(g, u + f"l{n}_t_psum")
                                if n < LAST:
                                    V.tensor_tensor(T[g][:], T[g][:], heads(aux[g][:, 0:NB]), ALU.subtract)
                                gdone(g, V.tensor_tensor(TT[g][:], TT[g][:], heads(aux[g][:, NB:]), ALU.subtract))
                    if c:
                        yield
                    for g in range(2):
                        bv = heads(v_tok[:, c, g * NB:(g + 1) * NB])
                        if c:
                            gat(g, u + "res_psum")
                            V.tensor_tensor(Rm[g][:], bv, per_head(0, c, g), ALU.mult)
                            V.tensor_tensor(qs_sb[g][:], heads(aux[g][:, NB:]), per_head(4, c, g), ALU.mult)
                            V.tensor_tensor(B0[g][:], heads(aux[g][:, 0:NB]), per_head(7, c, g), ALU.mult)
                            dve.drain()
                            gdone(g, V.tensor_tensor(Rm[g][:], Rm[g][:], B0[g][:], ALU.add))
                        else:
                            kt2 = heads(k_tok[:, c, g * 256:(g + 1) * 256]).unsqueeze(2).to_broadcast([P, 2, 2, P])
                            et2 = gr[:, 5, c, 4 * g:4 * g + 4].rearrange("p (q e) -> p q e", e=2).unsqueeze(3).to_broadcast([P, 2, 2, P])
                            V.tensor_tensor(twice(k_tail[g][:]), kt2, et2, ALU.mult)
                            gdone(g, V.tensor_tensor(Rm[g][:], bv, per_head(0, c, g), ALU.mult))
                    yield
                    yield
                    for g in range(2):
                        gat(g, u + "o_psum")
                        dst = o_r[:, c, g * NB:(g + 1) * NB]
                        if c:
                            gdone(g, V.tensor_tensor(dst, aux[g][:, NB:], flat2(qs_sb[g][:]), ALU.add))
                        else:
                            gdone(g, V.tensor_copy(dst, aux[g][:, NB:]))
                yield
                at("o_sq")
                done(V.tensor_reduce(o_ms[:], o_sq[:], AX.X, ALU.add))
                at("o_rs")
                V.reciprocal(o_ms[:], o_ms[:])
                dve.drain()
                o = o_r[:].rearrange("p m (h n) -> p (m h) n", n=GD)
                V.tensor_tensor(o, o, o_ms[:].rearrange("p m h -> p (m h)").unsqueeze(2).to_broadcast([P, M * HV, GD]), ALU.mult)
                dve.drain()
                done(V.tensor_tensor(o, o, all_heads(gnorm[:], M * HV), ALU.mult))

            def hook_r(r, b, j):
                if b * UPB["l1r"] + j >= AHEAD:
                    next(mixer, None)

            def gate(n):
                if n == 6:
                    dve.drain()
                elif n % 2 == 0:
                    dve.wait_ge(o_loaded[n // 2], 16)
                dve.wait_ge(acc_read[n % 2], BLOCK0["l1z"] // 2 + n // 2 + 1)
                o = o_z[n // 2][:, :, n % 2 * NB:(n % 2 + 1) * NB]
                V.tensor_tensor(o, o, zs[n][:], ALU.mult).then_inc(gated, 1)

            def o_split(n):
                for g in range(2):
                    t = O_ORDER[n] * HV + 4 * g
                    dve.wait_ge(o_hi, 2 * n + g + 1)
                    V.tensor_tensor(flat2(oT_lo[:, t:t + 4, :]), aux[g][:, :], flat2(oT_hi[:, t:t + 4, :]).bitcast(F32),
                                    ALU.subtract).then_inc(o_lo, 1)

            def hook_z(i, b, j):
                w = b * UPB["l1z"] + j
                if j == 5 and b:
                    gate(b - 1)
                if w >= AHEAD:
                    next(mixer, None)
                if w - AHEAD in O_SLOTS:
                    o_split(O_SLOTS.index(w - AHEAD))

            body("l1q", 0, 4, lambda i, b, j: gdn_gates() if b * UPB["l1q"] + j == GATES_AT + AHEAD else None)
            with dve.Fori(0, ROUNDS - 1) as r:
                mixer = gdn(r)
                body("l1r", r, 4, hook_r)
                for _ in mixer:
                    pass
            mixer = gdn(ROUNDS - 1)
            body("l1z", 0, 8, hook_z)
            gate(7)
            o_split(3)
            residual_phase("out1")
            ffn("gu1", 3, FF // NB)
            residual_phase("dn1")
            recip(4)
            dve.wait_ge(xs_copied, 16)
            dve.wait_ge(consts_in, 16 * 6)
            for m in range(M):
                V.scalar_tensor_tensor(x[:, m, :], x[:, m, :], rstd[:, m:m + 1], fgain[:], op0=ALU.mult, op1=ALU.mult
                                       ).then_inc(epi_step, 1)


WEIGHTS = ["x", "l0_w_in", "l0_gate_bias", "l0_mlstm_norm", "l0_w_out", "l0_w_gate", "l0_w_up", "l0_w_down",
           "l1_w_in", "l1_a_log", "l1_dt_bias", "l1_gdn_norm", "l1_w_out", "l1_w_gate", "l1_w_up", "l1_w_down",
           "final_norm"]


def layout(inputs):
    arrays = {f"in_{name}": np.ascontiguousarray(inputs[name]) for name in WEIGHTS}
    gains = [np.asarray(inputs[n]).reshape(KT, P).T for n in ("l0_norm_mix", "l0_norm_ffn", "l1_norm_mix", "l1_norm_ffn")]
    arrays["in_gains"] = np.ascontiguousarray(np.concatenate(gains, 1))
    conv = np.asarray(inputs["l1_conv_w"]).reshape(CW, -1, P)
    arrays["in_conv"] = np.ascontiguousarray(conv.transpose(2, 1, 0).reshape(P, -1))
    arrays["in_positions"] = np.ascontiguousarray(np.asarray(inputs["positions"]).reshape(M, P).T)
    arrays["in_shape_constants"] = shape_constants()
    return arrays


def kernel(**inputs):
    import concourse.bacc as bacc
    from concourse.bass_utils import run_bass_kernel_spmd

    nc = bacc.Bacc("TRN2", target_bir_lowering=False, num_devices=1)
    arrays = layout(inputs)
    aps = {name[3:]: nc.dram_tensor(name, a.shape, mybir.dt.from_np(a.dtype), kind="ExternalInput").ap()
           for name, a in arrays.items()}
    out = nc.dram_tensor("out_y", (SEQ, D), F32, kind="ExternalOutput").ap()
    build(nc, aps, out)
    r = run_bass_kernel_spmd(nc, [arrays], core_ids=[0])
    return r.results[0]["out_y"].reshape(1, SEQ, D)
```

```python
from contextlib import ExitStack

import numpy as np

import concourse.bass as bass
from concourse import mybir

F32 = mybir.dt.float32
F32R = mybir.dt.float32r
I32 = mybir.dt.int32
ALU = mybir.AluOpType
ACT = mybir.ActivationFunctionType
AX = mybir.AxisListType

P = 128
SEQ, D = 256, 2048
M = SEQ // P
KT = D // P
FF = -(-8 * D // (3 * 256)) * 256
FKT = FF // P
NB = 512
EPS = 1e-6
SLOTS = 4
MH, MDQK, MDV = 4, 128, 256
RH, RD = 4, 256
QKH, VH, GD = 16, 32, 128
CW = 4
ROUNDS = 4
HQ, HV = QKH // ROUNDS, VH // ROUNDS
SOFTCAP = 15.0
NEG = -1e30
TWO_PI = [6.28125, np.floor((2 * np.pi - 6.28125) * 2 ** 20) / 2 ** 20]
TWO_PI = [float(v) for v in TWO_PI + [2 * np.pi - sum(TWO_PI)]]
PI_BELOW = 3.1415925

QR, KR, QM, KM, VR, VM, OM, GR, L0W = 0, 1024, 2048, 2560, 3072, 4096, 5120, 6144, 7168
L0_GATES = 3072
L0_COLS = [3080, 3592, 4104, 4616, 0, 512, 5128, 5640, 1024, 1536, 2048, 2560, 6152, 6664]
L1_GATES = 12288
GW = (8, 64)

LEVELS = [1, 2, 4, 8, 16, 32, 64]
CONST_PARTS = [("ident", 128), ("upto", 128), ("after", 128), ("ones", 128), ("neg", 384),
               ("low_up", 256), ("levels", 128 * len(LEVELS)), ("decay", RH * 256), ("freq", 128)]
CONST_AT = {}
_n = 0
for _name, _w in CONST_PARTS:
    CONST_AT[_name] = (_n, _n + _w)
    _n += _w
CONST_W = _n


def shape_constants():
    a, b = np.arange(P)[:, None], np.arange(P)[None, :]
    c = np.zeros((P, CONST_W), np.float32)

    def put(name, v):
        lo, hi = CONST_AT[name]
        c[:, lo:hi] = v

    put("ident", a == b)
    put("upto", a <= b)
    put("after", a > b)
    put("ones", 1.0)
    neg = np.where(a >= b, 0.0, NEG)
    put("neg", np.concatenate([neg, np.zeros((P, P)), neg], 1))
    put("low_up", np.concatenate([a > b, a <= b], 1))
    put("levels", np.concatenate([((a // (2 * n)) == (b // (2 * n))) & ((a // n) % 2 == 1) & ((b // n) % 2 == 0)
                                  for n in LEVELS], 1))
    t = np.arange(SEQ)[None, :]
    rel = np.where(t >= a, t - a, 0).astype(np.float32)
    dec = []
    for h in range(RH):
        log_gamma = np.log(np.float32(1.0) - np.float32(2.0) ** np.float32(-5.0 - h))
        dec.append(np.where(t >= a, np.exp(rel * log_gamma), 0.0) * RD ** -0.5)
    put("decay", np.concatenate(dec, 1))
    put("freq", (np.float32(10000.0) ** (-np.arange(0, RD, 2, dtype=np.float32) / np.float32(RD)))[None, :])
    return c


PHASES = [("l0a", KT // 2, 4), ("l0b", KT // 2, 2), ("l0c", KT // 2, 8), ("out0", KT // 2, 4), ("gu0", KT // 2, 2 * FF // NB),
          ("dn0", FKT // 2, 4), ("l1p", KT // 2, 2), ("l1q", KT // 2, 2), ("l1r", KT // 2, 12), ("l1z", KT // 2, 8), ("out1", KT, 4),
          ("gu1", KT // 2, 2 * FF // NB), ("dn1", FKT // 2, 4)]
UNIT0, BLOCK0, UPB = {}, {}, {}
_u = _b = 0
for _name, _upb, _nb in PHASES:
    UNIT0[_name], BLOCK0[_name], UPB[_name] = _u, _b, _upb
    _u += _upb * _nb
    _b += _nb
UNIT_END, BLOCK_END = _u, _b

MLSTM_HEAD = ["rows", "d_psum", "d_max", "d_exp", "s_psum", "s_prod", "st_psum", "st_copy", "num_psum", "num_div"]
L0_STEPS = (["pos", "sincos"]
            + [f"rot{i}_{s}" for i in range(2 * M) for s in ("mul", "tr", "copy")]
            + ["gates", "tanh", "cap", "exp", "log1p", "m_tr", "m_trc"]
            + [f"r{h}_{s}" for h in range(RH) for s in ("s_psum", "s_dec", "o_psum", "o_copy")]
            + [f"m{h}_{s}" for h in range(MH) for s in MLSTM_HEAD]
            + ["m_sq", "m_norm"]
            + [f"mix{g}_{s}" for g in range(2) for s in ("tr", "hi", "lo")]
            + ["r_sq", "r_norm"]
            + [f"mix{g}_{s}" for g in range(2, 4) for s in ("tr", "hi", "lo")])
L0_AT = {s: i + 1 for i, s in enumerate(L0_STEPS)}

AHEAD = 2
L0_SLOTS = ([0, 3, 5, 7, 9, 16, 17, 33, 35, 37, 39, 41, 43, 45, 47]
            + [49, 50, 51, 53, 54, 55, 56, 57, 59, 60, 61, 62, 64, 65, 66, 67, 71, 73, 75])

GATES_AT = 10
O_SLOTS = [55, 58, 61]

GDN_GATE_STEPS = ["raw", "exp", "log1p", "sums", "sums_exp"]
GATE_AT = {s: i + 1 for i, s in enumerate(GDN_GATE_STEPS)}
LAST = len(LEVELS) - 1


def level_steps(n):
    return ["q_psum"] + (["q", "t_psum"] if n else []) + ["t"]


GDN_STEPS = ["round"] + [f"o{c}_{s}" for c in range(M) for s in ("sq", "sum", "rs", "norm")]
NORM_STEPS = ["sums", "roots", "recips", "k_row", "k_mul", "q_row", "q_mul"]
NORM_AT = {s: i + 1 for i, s in enumerate(NORM_STEPS)}
POOL_UNITS = range(AHEAD, AHEAD + 8)
GROUP_STEPS = [f"t{c}_{s}" for c in range(M) for s in
               ["lam", "d_psum", "d_exp", "kq_psum", "a"]
               + [f"l{n}_{s}" for n in range(len(LEVELS)) for s in level_steps(n)]
               + (["res_psum"] if c else []) + ["res", "vn_psum", "vn", "o_psum", "o"]
               + ([] if c else ["s_copy"])]
GROUP_AT = {s: i + 1 for i, s in enumerate(GROUP_STEPS)}
GROUP_N = len(GROUP_STEPS)
GDN_AT = {s: i + 2 for i, s in enumerate(GDN_STEPS)}
GDN_N = len(GDN_STEPS)


def build(nc, A, out):
    with ExitStack() as ctx:
        def sb(name, shape, dt=F32):
            return ctx.enter_context(nc.sbuf_tensor(name, shape, dt))

        def sem(name):
            return ctx.enter_context(nc.semaphore(name))

        wraw = sb("wraw", [P, SLOTS, 2 * NB])
        whi = sb("whi", [P, SLOTS, 2 * NB], F32R)
        wlo = sb("wlo", [P, SLOTS, 2 * NB], F32R)
        x = sb("x", [P, M, D])
        xs = sb("xs", [P, M, NB])
        hT_at = nc.sbuf_base
        hT_hi = sb("hT_hi", [P, KT, SEQ], F32R)
        hT_lo = sb("hT_lo", [P, KT, SEQ], F32R)
        const = sb("const", [P, CONST_W])
        gains = sb("gains", [P, 4, KT])
        ssq = sb("ssq", [P, M, 4])
        mean = sb("mean", [P, M])
        rms = sb("rms", [P, M])
        rstd = sb("rstd", [P, M])
        epsc = sb("epsc", [P, 2])
        gate_t = sb("gate_t", [P, 10, 64])
        C = {name: const[:, lo:hi] for name, (lo, hi) in CONST_AT.items()}
        ident = C["ident"]

        arena0 = (nc.sbuf_base + 63) // 64 * 64
        arena_end = arena0
        names = iter(range(1000))

        def at(offset, shape, dt=F32):
            nonlocal arena_end
            offset = int(offset)
            size = 4 * int(np.prod(shape[1:]))
            arena_end = max(arena_end, arena0 + offset + size)
            return nc.alloc_sbuf_tensor_at(f"arena{next(names)}", shape, dt, offset=arena0 + offset)

        KB = 1024
        gw_raw, gw_hi, gw_lo = ([at((84.5 + 0.5 * i) * KB, [P, KT * GW[0]], dt), at((20 + 4 * i) * KB, [P, KT * GW[1]], dt)]
                                for i, dt in enumerate((F32, F32R, F32R)))
        gates_T = [at(86 * KB, [P, SEQ]), at(32 * KB, [P, SEQ])]
        pr = at(0, [P, M, L0W])
        mixT_hi = at(56 * KB, [P, KT, SEQ], F32R)
        mixT_lo = at(72 * KB, [P, KT, SEQ], F32R)
        rot = at(56 * KB, [P, RH, 2, P])
        rot_a = at(60 * KB, [P, RH, P])
        rot_b = at(62 * KB, [P, RH, P])
        qmT = at(56 * KB, [P, MH, SEQ])
        kmT = at(60 * KB, [P, MH, SEQ])
        qrT = at(64 * KB, [P, 2 * RH, SEQ])
        krT = at(72 * KB, [P, 2 * RH, SEQ])
        cs = at(80 * KB, [P, 2, M, P])
        ang = at(82 * KB, [P, 2, M, P])
        d_rows = at(80 * KB, [P, 6, P])
        d_sb = at(83 * KB, [P, 384])
        p_sb = at(84 * KB + 512, [P, 384])
        st_sb = at(86 * KB, [P, 384])
        rs_sb = at(86 * KB, [P, 384])
        mnorm = at(87 * KB + 512, [P, MH * MDV])
        fT_hi = at(0, [P, FKT, SEQ], F32R)
        fT_lo = at(44 * KB, [P, FKT, SEQ], F32R)
        sg = at(88 * KB, [P, M, NB])
        prod = xs
        qkv = at(0, [P, M, 2048])
        k_tok = at(16 * KB, [P, M, 512])
        v_tok = at(20 * KB, [P, M, 1024])
        qkT = at(28 * KB, [P, 8, SEQ])
        zs = [at((36 if n < 2 * (ROUNDS - 1) else 64) * KB, [P, M, NB]) for n in range(2 * ROUNDS)]
        kq = [at((76 + 2 * g) * KB, [P, 2, 2 * P]) for g in range(2)]
        vT = at(48 * KB, [P, 8, SEQ])
        sq = [at((56 + 8 * b) * KB, [P, 4, SEQ]) for b in range(2)]
        EA, ET, T, TT, Q1, B0, B1 = ([at((48 + 14 * g + 2 * k) * KB, [P, 4, P]) for g in range(2)] for k in range(7))
        Bm = [[B0[g], B1[g]] for g in range(2)]
        lam, Rm, Vn, k_tail, qs_sb = B0, T, Q1, B0, B1
        St = xs[:, :, :].rearrange("p m (h n) -> p (m h) n", n=P)
        conv_w = at(80 * KB, [P, 64, CW])
        gnorm = at(81 * KB, [P, GD])
        conv_r = at(81 * KB + 512, [P, 16, CW])
        gr = at(82 * KB, [P, 8, M, HV])
        o_ms = at(82 * KB + 512, [P, M, HV])
        qk_rms = at(82 * KB + 640, [P, 2, 8])
        o_r = at(84 * KB, [P, M, HV * GD])
        o_z = [at(0, [P, M, HV * GD]), at(8 * KB, [P, M, HV * GD]), at(40 * KB, [P, M, HV * GD]), o_r]
        o_dram = nc.dram_tensor("o_rounds", (SEQ, VH * GD), F32, kind="Internal").ap()
        O_ORDER = [0, 2, 1, 3]
        oT_hi = at(0, [P, 2 * KT, SEQ], F32R)
        oT_lo = at(32 * KB, [P, 2 * KT, SEQ], F32R)
        fgain = nc.alloc_sbuf_tensor_at("fgain", [P, D], F32, offset=hT_at)
        assert arena_end <= nc.sbuf_usable_end, (arena_end, nc.sbuf_usable_end)

        acc = [ctx.enter_context(nc.psum_tensor(f"acc{i}", [P, M, NB], F32)) for i in range(2)]
        aux = [ctx.enter_context(nc.psum_tensor(f"aux{i}", [P, 2 * NB], F32)) for i in range(2)]
        first_xt = [aux[0]] + [acc[i][:].rearrange("p m n -> p (m n)") for i in (1, 0)] + [aux[0]]
        aux4 = [aux[i // 2][:, (i % 2) * NB:(i % 2 + 1) * NB] for i in range(4)]

        raw_in = [sem(f"raw_in{i}") for i in range(SLOTS)]
        hi_done = sem("hi_done")
        lo_done = sem("lo_done")
        unit_used = sem("unit_used")
        acc_read = [sem(f"acc_read{i}") for i in range(2)]
        consts_in = sem("consts_in")
        first_in = sem("first_in")
        x_in = [sem(f"x_in{n}") for n in range(4)]
        eps_set = sem("eps_set")
        xs_copied = sem("xs_copied")
        xt_ready = sem("xt_ready")
        xhi_done = sem("xhi_done")
        xlo_done = sem("xlo_done")
        mean_done = sem("mean_done")
        rms_done = sem("rms_done")
        rstd_done = sem("rstd_done")
        gw_in = sem("gw_in")
        gw_hi_done = sem("gw_hi_done")
        gw_lo_done = sem("gw_lo_done")
        gw_used = sem("gw_used")
        gates_out = sem("gates_out")
        gates_tr = sem("gates_tr")
        ft_ready = sem("ft_ready")
        fhi_done = sem("fhi_done")
        flo_done = sem("flo_done")
        l0_step = sem("l0_step")
        gate_step = sem("gate_step")
        gdn_step = sem("gdn_step")
        conv_tr = sem("conv_tr")
        conv_tap = sem("conv_tap")
        conv_sum = sem("conv_sum")
        conv_silu = sem("conv_silu")
        norm_sq = sem("norm_sq")
        norm_step = sem("norm_step")
        tok_tr = sem("tok_tr")
        tok_copy = sem("tok_copy")
        group_step = [sem(f"group_step{g}") for g in range(2)]
        level_part = [sem(f"level_part{g}") for g in range(2)]
        o_stored = sem("o_stored")
        o_loaded = [sem(f"o_loaded{r}") for r in range(ROUNDS - 1)]
        gated = sem("gated")
        o_tr = sem("o_tr")
        o_hi = sem("o_hi")
        o_lo = sem("o_lo")
        epi_step = sem("epi_step")
        l1_const = sem("l1_const")
        out_done = sem("out_done")

        def col_block(w, col):
            return w.rearrange("(k p) n -> p k n", p=P)[:, :, bass.ds(col, NB)]

        NORM_OF = {"out0": 1, "dn0": 2, "out1": 3, "dn1": 4}

        def l0_slots(mixer, w):
            if w in L0_SLOTS:
                next(mixer)

        block = ctx.enter_context(nc.Block())

        @block.sync
        def _(sp):
            def unit(w, u, j, col):
                sp.wait_ge(lo_done, u - (SLOTS - 1))
                sp.dma_start(wraw[:, j % SLOTS, :].rearrange("p (k n) -> p k n", k=2),
                             col_block(w, col)[:, 2 * j:2 * j + 2, :]).then_inc(raw_in[j % SLOTS], 16)

            def first_units(w, col, n):
                for j in range(n):
                    sp.dma_start(wraw[:, j, :].rearrange("p (k n) -> p k n", k=2),
                                 col_block(w, col)[:, 2 * j:2 * j + 2, :]).then_inc(raw_in[j], 16)

            def phase(name, n_body, lo, hi, cols):
                upb = UPB[name]
                with sp.Fori(lo, hi) as i:
                    for b, (wt, col) in enumerate(cols(i)):
                        for j in range(upb):
                            u = UNIT0[name] + (i * n_body + b) * upb + j
                            sp.wait_ge(lo_done, u - (SLOTS - 1))
                            s = (b * upb + j) % SLOTS
                            sp.dma_start(wraw[:, s, :].rearrange("p (k n) -> p k n", k=2),
                                         col_block(wt, col)[:, 2 * j:2 * j + 2, :]).then_inc(raw_in[s], 16)

            def gate_columns(w, col, layer):
                sp.dma_start(gw_raw[layer][:].rearrange("p (k n) -> p k n", k=KT),
                             w.rearrange("(k p) n -> p k n", p=P)[:, :, col:col + GW[layer]]).then_inc(gw_in, 16)

            sp.dma_start(const[:, 0:P], A["shape_constants"][:, 0:P]).then_inc(first_in, 16)
            sp.dma_start(gains[:], A["gains"].rearrange("p (n k) -> p n k", n=4)).then_inc(first_in, 16)
            for n in range(4):
                sp.dma_start(x[:, :, n * NB:(n + 1) * NB], A["x"].rearrange("a (m p) n -> p (a m) n", p=P)[:, :, n * NB:(n + 1) * NB]
                             ).then_inc(x_in[n], 16)
            w0, w1 = A["l0_w_in"], A["l1_w_in"]
            first_units(w0, L0_COLS[0], SLOTS)
            sp.dma_start(const[:, P:], A["shape_constants"][:, P:]).then_inc(consts_in, 16)
            sp.dma_start(gate_t[:, 9, 0:2].bitcast(I32), A["positions"]
                         ).then_inc(consts_in, 16)
            sp.dma_start(gate_t[:, 8, 0:8], A["l0_gate_bias"].rearrange("(a n) -> a n", a=1).to_broadcast([P, 8])
                         ).then_inc(consts_in, 16)
            sp.dma_start(mnorm[:], A["l0_mlstm_norm"].rearrange("(a n) -> a n", a=1).to_broadcast([P, MH * MDV])
                         ).then_inc(consts_in, 16)
            gate_columns(w0, L0_GATES, 0)
            for j in range(SLOTS, 2 * UPB["l0a"]):
                unit(w0, j, j % UPB["l0a"], L0_COLS[j // UPB["l0a"]])
            phase("l0a", 2, 1, 2, lambda i: [(w0, i * 2 * NB + L0_COLS[b]) for b in range(2)])
            phase("l0b", 2, 0, 1, lambda i: [(w0, i * 2 * NB + L0_COLS[4 + b]) for b in range(2)])
            for n in range(4):
                for b in range(2):
                    for j in range(UPB["l0c"]):
                        unit(w0, UNIT0["l0c"] + (2 * n + b) * UPB["l0c"] + j, j, L0_COLS[6 + 2 * n + b])
            phase("out0", 2, 0, 2, lambda i: [(A["l0_w_out"], i * 2 * NB + b * NB) for b in range(2)])
            phase("gu0", 2, 0, FF // NB, lambda i: [(A["l0_w_gate"], i * NB), (A["l0_w_up"], i * NB)])
            phase("dn0", 2, 0, 2, lambda i: [(A["l0_w_down"], i * 2 * NB + b * NB) for b in range(2)])
            zcol, qkvcol = 8192, [0, 2048, 4096, 4096 + NB]
            phase("l1p", 2, 0, 1, lambda i: [(w1, i * NB + c) for c in qkvcol[:2]])
            sp.wait_ge(unit_used, UNIT0["l1p"])
            gate_columns(w1, L1_GATES, 1)
            sp.dma_start(gnorm[:], A["l1_gdn_norm"].rearrange("(a n) -> a n", a=1).to_broadcast([P, GD])
                         ).then_inc(l1_const, 16)
            sp.dma_start(conv_w[:], A["conv"].rearrange("p (c w) -> p c w", w=CW)).then_inc(l1_const, 16)
            for n, g in enumerate(("l1_a_log", "l1_dt_bias")):
                sp.dma_start(gate_t[:, 8, 32 * n:32 * n + 32], A[g].rearrange("(a n) -> a n", a=1).to_broadcast([P, 32])
                             ).then_inc(l1_const, 16)
            phase("l1q", 2, 0, 1, lambda i: [(w1, i * NB + c) for c in qkvcol[2:]])
            phase("l1r", 4, 0, ROUNDS - 1, lambda i: [(w1, i * NB + c + NB) for c in qkvcol[:2]]
                  + [(w1, i * 2 * NB + c + 2 * NB) for c in qkvcol[2:]])
            phase("l1z", 2, 0, 4, lambda i: [(w1, i * 2 * NB + zcol + b * NB) for b in range(2)])
            phase("out1", 2, 0, 2, lambda i: [(A["l1_w_out"], i * 2 * NB + b * NB) for b in range(2)])
            phase("gu1", 2, 0, FF // NB, lambda i: [(A["l1_w_gate"], i * NB), (A["l1_w_up"], i * NB)])
            sp.wait_ge(unit_used, UNIT0["dn1"])
            sp.dma_start(fgain[:], A["final_norm"].rearrange("(a n) -> a n", a=1).to_broadcast([P, D])
                         ).then_inc(consts_in, 16)
            phase("dn1", 2, 0, 2, lambda i: [(A["l1_w_down"], i * 2 * NB + b * NB) for b in range(2)])
            for m in range(M):
                sp.wait_ge(epi_step, m + 1)
                sp.dma_start(out[m * P:(m + 1) * P, :], x[:, m, :]).then_inc(out_done, 16)
            sp.wait_ge(out_done, 16 * M)

        @block.gpsimd
        def _(pool):
            def keep_x(name):
                with pool.Fori(0, 2) as i:
                    for b in range(2):
                        pool.wait_ge(acc_read[b], i + (BLOCK0[name] // 2 + 1))
                        nc.gpsimd.tensor_copy(x[:, :, bass.ds(i * 2 * NB + b * NB, NB)], xs[:]).then_inc(xs_copied, 1)

            def squares_and_lo_parts(r):
                u0 = r * (4 * UPB["l1r"]) + UNIT0["l1r"]
                for w in POOL_UNITS:
                    s = w % SLOTS
                    if w == POOL_UNITS[0]:
                        pool.wait_ge(lo_done, u0 + w)
                    pool.wait_ge(hi_done, u0 + (w + 1))
                    pool.wait_ge(unit_used, u0 + (w - SLOTS + 1))
                    nc.gpsimd.tensor_tensor(wlo[:, s, :], wraw[:, s, :], whi[:, s, :].bitcast(F32), ALU.subtract
                                            ).then_inc(lo_done, 1)
                    b = w - POOL_UNITS[0] - 2
                    if b in (0, 1):
                        pool.wait_ge(conv_silu, r * 4 + (b + 1))
                        y = qkT[:, 4 * b:4 * b + 4, :]
                        nc.gpsimd.tensor_tensor(sq[b][:], y, y, ALU.mult).then_inc(norm_sq, 1)

            def level_parts(r):
                for c in range(M):
                    for n in range(len(LEVELS)):
                        mask = C["levels"][:, n * P:(n + 1) * P].unsqueeze(1).to_broadcast([P, 4, P])
                        for g in range(2):
                            if n == 0:
                                pool.wait_ge(group_step[g], r * GROUP_N + GROUP_AT[f"t{c}_a"])
                            elif n >= 2:
                                pool.wait_ge(group_step[g], r * GROUP_N + GROUP_AT[f"t{c}_l{n - 2}_q_psum" if n > 2 else f"t{c}_l0_t"])
                            nc.gpsimd.tensor_tensor(Bm[g][n % 2][:], EA[g][:], mask, ALU.mult).then_inc(level_part[g], 1)

            keep_x("out0")
            keep_x("dn0")
            squares_and_lo_parts(0)
            with pool.Fori(0, ROUNDS - 1) as r:
                level_parts(r)
                pool.wait_ge(gdn_step, r * GDN_N + GDN_AT[f"o{M - 1}_norm"])
                pool.dma_start(o_dram[:, bass.ds(r * HV * GD, HV * GD)].rearrange("(m p) n -> p m n", p=P), o_r[:]
                               ).then_inc(o_stored, 16)
                squares_and_lo_parts(r + 1)
                pool.wait_ge(o_stored, r * 16 + 16)
            level_parts(ROUNDS - 1)
            keep_x("out1")
            keep_x("dn1")

        @block.tensor
        def _(pe):
            def products(pair, k, k_last, hi, lo, slot, kk, width, stride, first):
                for m in range(M):
                    tok = slice(m * P, (m + 1) * P)
                    o = pair[m]
                    a, b = hi[:, k, tok], lo[:, k, tok]
                    wh = whi[:, slot, kk * stride:kk * stride + width]
                    wl = wlo[:, slot, kk * stride:kk * stride + width]
                    nc.tensor.matmul(o, a, wh, start=first, stop=False)
                    nc.tensor.matmul(o, a, wl, start=False, stop=False)
                    mm = nc.tensor.matmul(o, b, wh, start=False, stop=k_last)
                return mm

            def gemm_block(name, base_u, base_b, hi, lo, slot0, parity, midway=None, fresh=False, between=None):
                upb = UPB[name]
                if not fresh:
                    pe.wait_ge(acc_read[parity], base_b)
                for j in range(upb):
                    pe.wait_ge(lo_done, base_u + (j + 1))
                    for kk in range(2):
                        k = 2 * j + kk
                        mm = products([acc[parity][:, m, :] for m in range(M)], k, k == 2 * upb - 1, hi, lo,
                                      (slot0 + j) % SLOTS, kk, NB, NB, k == 0)
                    mm.then_inc(unit_used, 1)
                    if j == 3 and midway is not None:
                        midway()
                    if between is not None:
                        between(slot0 + j)

            def gate_products(layer):
                pe.wait_ge(gw_lo_done, layer + 1)
                w = GW[layer]
                o = aux4[2][0:w, 0:SEQ]
                for k in range(KT):
                    w_hi, w_lo = (g[layer][:, k * w:(k + 1) * w] for g in (gw_hi, gw_lo))
                    nc.tensor.matmul(o, w_hi, hT_hi[:, k, :], start=k == 0, stop=False)
                    nc.tensor.matmul(o, w_lo, hT_hi[:, k, :], start=False, stop=False)
                    mm = nc.tensor.matmul(o, w_hi, hT_lo[:, k, :], start=False, stop=k == KT - 1)
                mm.then_inc(gw_used, 1)

            def gate_transposes(layer):
                pe.wait_ge(gates_out, layer + 1)
                w = GW[layer]
                for m in range(M):
                    mm = nc.tensor.transpose(aux4[2 + m][:, 0:w], gates_T[layer][0:w, m * P:(m + 1) * P], ident[0:w, 0:w])
                mm.then_inc(gates_tr, 1)

            def transposes(src, dst, n):
                for t in range(n):
                    for m in range(M):
                        mm = nc.tensor.transpose(dst[:, t * SEQ + m * P:t * SEQ + (m + 1) * P],
                                                 src(m, t), ident)
                return mm

            def body(name, i, n_body, hi, lo, midways, fresh=(), between=None):
                for b in range(n_body):
                    upb = UPB[name]
                    gemm_block(name, i * (n_body * upb) + (UNIT0[name] + b * upb),
                               i * (n_body // 2) + (BLOCK0[name] + b) // 2, hi, lo, b * upb, b % 2,
                               midways[b], b in fresh, between)

            xs_tile = lambda m, t: xs[:, m, t * P:(t + 1) * P]
            prod_tile = lambda m, t: prod[:, m, t * P:(t + 1) * P]

            def residual_phase(name, hi, lo, transposed):
                done = 4 * (NORM_OF[name] - 1)

                def xt(i, b):
                    def f():
                        pe.wait_ge(acc_read[1 - b], i + (BLOCK0[name] // 2 + b))
                        pe.wait_ge(xlo_done, i * 2 + (done + b + 3))
                        transposes(xs_tile, aux[0], 4).then_inc(xt_ready, 1)
                    return f if transposed else None
                body(name, 0, 2, hi, lo, [None, xt(0, 1)])
                with pe.Fori(1, 2) as i:
                    body(name, i, 2, hi, lo, [xt(i, 0), xt(i, 1)])
                if transposed:
                    pe.wait_ge(xlo_done, done + 4 + 3)

            def last_x_block(name):
                def between(w):
                    if w == 1:
                        pe.wait_ge(acc_read[1], BLOCK0[name] // 2 + 2)
                        transposes(xs_tile, aux[0], 4).then_inc(xt_ready, 1)
                    if w == 5:
                        pe.wait_ge(xlo_done, 4 * (NORM_OF[name] + 1))
                return between

            def ffn(name, after, n0):
                def tr(i):
                    def f():
                        pe.wait_ge(acc_read[1], i + BLOCK0[name] // 2)
                        if n0 or not isinstance(i, int) or i > 1:
                            pe.wait_ge(flo_done, i + (n0 - 1))
                        transposes(prod_tile, aux[1], 4).then_inc(ft_ready, 1)
                    return f
                body(name, 0, 2, hT_hi, hT_lo, [None, None], between=last_x_block(after))
                body(name, 1, 2, hT_hi, hT_lo, [tr(1), None])
                with pe.Fori(2, FF // NB) as i:
                    body(name, i, 2, hT_hi, hT_lo, [tr(i), None])
                tr(FF // NB)()
                pe.wait_ge(flo_done, n0 + FF // NB)


            def l0(name):
                pe.wait_ge(l0_step, L0_AT[name])

            def projected(blocks):
                for b in range(2):
                    pe.wait_ge(acc_read[b], blocks // 2)

            def l0_mixer():
                pe.wait_ge(consts_in, 16 * 4)
                for i in range(2 * M):
                    yield
                    l0(f"rot{i}_mul")
                    for t in range(2 * RH):
                        mm = nc.tensor.transpose(aux[i % 2][:, t * P:(t + 1) * P], rot[:, t // 2, t % 2, :], ident)
                    mm.then_inc(l0_step, 1)
                yield
                yield
                projected(6)
                l0("log1p")
                for dst, col in ((aux[0], QM), (aux[1], KM)):
                    mm = transposes(lambda m, t: pr[:, m, col + t * P:col + (t + 1) * P], dst, MH)
                mm.then_inc(l0_step, 1)
                for h in range(RH):
                    yield
                    l0("m_trc" if h == 0 else f"r{h - 1}_o_copy")
                    for d in range(2):
                        nc.tensor.matmul(aux4[0][:, 0:SEQ], krT[:, 2 * h + d, 0:P], qrT[:, 2 * h + d, :],
                                         start=d == 0, stop=d == 1)
                    for d in range(2):
                        mm = nc.tensor.matmul(aux4[0][:, SEQ:3 * P], krT[:, 2 * h + d, P:], qrT[:, 2 * h + d, P:],
                                              start=d == 0, stop=d == 1)
                    mm.then_inc(l0_step, 1)
                    yield
                    l0(f"r{h}_s_dec")
                    projected(8)
                    weighted_values(rs_sb, VR + h * RD).then_inc(l0_step, 1)
                for h in range(MH):
                    yield
                    l0(f"m{h}_rows")
                    rows = d_rows[:, :, :].rearrange("p a b -> p (a b)")
                    nc.tensor.matmul(aux4[0][:, 0:P], C["upto"], rows[:, 0:P], start=True, stop=False)
                    nc.tensor.matmul(aux4[0][:, 0:P], C["ones"], rows[:, 5 * P:], start=False, stop=True)
                    nc.tensor.matmul(aux4[0][:, P:3 * P], C["upto"], rows[:, P:3 * P], start=True, stop=False)
                    nc.tensor.matmul(aux4[0][:, P:3 * P], C["ones"], rows[:, 3 * P:5 * P], start=False, stop=True
                                     ).then_inc(l0_step, 1)
                    yield
                    l0(f"m{h}_d_exp")
                    nc.tensor.matmul(aux4[2][:, 0:P], qmT[:, h, 0:P], kmT[:, h, 0:P], start=True, stop=True)
                    nc.tensor.matmul(aux4[2][:, P:3 * P], qmT[:, h, P:], kmT[:, h, :], start=True, stop=True
                                     ).then_inc(l0_step, 1)
                    yield
                    l0(f"m{h}_s_prod")
                    for i in range(3):
                        mm = nc.tensor.transpose(aux4[0][:, i * P:(i + 1) * P], d_sb[:, i * P:(i + 1) * P], ident)
                    mm.then_inc(l0_step, 1)
                    yield
                    l0(f"m{h}_st_copy")
                    projected(10)
                    weighted_values(st_sb, VM + h * MDV).then_inc(l0_step, 1)
                yield
                for g in range(4):
                    if g == 2:
                        yield
                    yield
                    l0(("m_norm", "mix0_lo", "r_norm", "mix2_lo")[g])
                    base = (VM if g < 2 else VR) + (g % 2) * 4 * P
                    transposes(lambda m, t: pr[:, m, base + t * P:base + (t + 1) * P], aux[g % 2], 4).then_inc(l0_step, 1)

            def weighted_values(st, col):
                v = [pr[:, m, col:col + 256] for m in range(M)]
                nc.tensor.matmul(aux4[2][:, 0:256], st[:, 0:P], v[0], start=True, stop=True)
                nc.tensor.matmul(aux4[2][:, 256:512], st[:, P:2 * P], v[0], start=True, stop=False)
                return nc.tensor.matmul(aux4[2][:, 256:512], st[:, 2 * P:3 * P], v[1], start=False, stop=True)

            def gdn_gates():
                pe.wait_ge(gate_step, GATE_AT["log1p"])
                la = gate_t[:, 1, :]
                nc.tensor.matmul(aux4[2][:, 0:64], C["upto"], la, start=True, stop=True)
                nc.tensor.matmul(aux4[3][:, 0:64], C["after"], la, start=True, stop=True).then_inc(gate_step, 1)

            def gdn(r):
                def at(name):
                    pe.wait_ge(gdn_step, r * GDN_N + GDN_AT[name])

                def done(mm):
                    mm.then_inc(gdn_step, 1)

                for b in range(4):
                    if b:
                        yield
                    if b == 0:
                        at("round")
                    if b >= 2:
                        pe.wait_ge(conv_sum, r * 4 + (b - 1))
                    transposes(lambda m, t: qkv[:, m, (4 * b + t) * P:(4 * b + t + 1) * P], aux[b % 2], 4).then_inc(conv_tr, 1)

                def norm(name):
                    pe.wait_ge(norm_step, r * len(NORM_STEPS) + NORM_AT[name])

                def sums(b):
                    pe.wait_ge(norm_sq, r * 2 + (b + 1))
                    for i in range(8):
                        mm = nc.tensor.matmul(aux[0][:, 8 * b + i:8 * b + i + 1], sq[b][:, i // M, i % M * P:(i % M + 1) * P],
                                              C["ones"][:, 0:1], start=True, stop=True)
                    return mm

                def row(b, to):
                    for i in range(8):
                        mm = nc.tensor.matmul(to[:, i * P:(i + 1) * P], qk_rms[:, b, i:i + 1].to_broadcast([P, P]), ident,
                                              start=True, stop=True)
                    mm.then_inc(norm_step, 1)

                def token_major(src, to):
                    for m in range(M):
                        for t in range(4):
                            mm = nc.tensor.transpose(to[:, m * NB + t * P:m * NB + (t + 1) * P],
                                                     src[:, t, m * P:(m + 1) * P], ident)
                    mm.then_inc(tok_tr, 1)
                yield
                pe.wait_ge(conv_sum, r * 4 + 3)
                sums(0)
                sums(1).then_inc(norm_step, 1)
                yield
                pe.wait_ge(conv_silu, r * 4 + 3)
                pe.wait_ge(conv_sum, r * 4 + 4)
                token_major(vT[:, 0:4], aux[1])
                yield
                norm("recips")
                row(1, aux[0])
                yield
                pe.wait_ge(conv_silu, r * 4 + 4)
                pe.wait_ge(tok_copy, r * 3 + 1)
                token_major(vT[:, 4:8], aux[1])
                yield
                norm("k_mul")
                token_major(qkT[:, 4:8], aux[0])
                pe.wait_ge(tok_copy, r * 3 + 2)
                row(0, aux[1])

                def gat(g, name):
                    pe.wait_ge(group_step[g], r * GROUP_N + GROUP_AT[name])

                def gdone(g, mm):
                    mm.then_inc(group_step[g], 1)

                col = lambda h: slice(h * P, (h + 1) * P)
                half = lambda g, k: aux[g][:, k * NB:(k + 1) * NB]
                for c in range(M):
                    tok = slice(c * P, (c + 1) * P)
                    u = f"t{c}_"
                    yield
                    if c == 0:
                        pe.wait_ge(tok_copy, r * 3 + 3)
                        norm("q_mul")
                    for g in range(2):
                        gat(g, u + "lam")
                        gdone(g, nc.tensor.matmul(half(g, 0), C["upto"], lam[g][:, :, :].rearrange("p a b -> p (a b)"),
                                                  start=True, stop=True))
                    yield
                    for g in range(2):
                        gat(g, u + "d_exp")
                        for h in range(2):
                            k, q = qkT[:, 4 + 2 * g + h, tok], qkT[:, 2 * g + h, tok]
                            nc.tensor.matmul(half(g, 0)[:, col(2 * h)], k, k, start=True, stop=True)
                            nc.tensor.matmul(half(g, 0)[:, col(2 * h + 1)], k, q, start=True, stop=True)
                        for h in range(4):
                            mm = nc.tensor.transpose(half(g, 1)[:, col(h)], EA[g][:, h, :], ident)
                        gdone(g, mm)
                    for n in range(len(LEVELS)):
                        yield
                        for g in range(2):
                            pe.wait_ge(level_part[g], r * (M * len(LEVELS)) + (c * len(LEVELS) + n + 1))
                            gat(g, u + (f"l{n - 1}_t" if n else "a"))
                            for h in range(4):
                                if n:
                                    mm = nc.tensor.matmul(half(g, 0)[:, col(h)], Bm[g][n % 2][:, h, :], TT[g][:, h, :],
                                                          start=True, stop=True)
                                else:
                                    mm = nc.tensor.transpose(half(g, 0)[:, col(h)], Bm[g][0][:, h, :], ident)
                            gdone(g, mm)
                        if n:
                            yield
                            for g in range(2):
                                gat(g, u + f"l{n}_q")
                                for h in range(4):
                                    if n < LAST:
                                        nc.tensor.matmul(half(g, 0)[:, col(h)], Q1[g][:, h, :], T[g][:, h, :], start=True, stop=True)
                                    mm = nc.tensor.matmul(half(g, 1)[:, col(h)], T[g][:, h, :], Q1[g][:, h, :], start=True, stop=True)
                                gdone(g, mm)
                    if c:
                        yield
                        for g in range(2):
                            gat(g, u + f"l{LAST}_t")
                            for h in range(4):
                                s = St[:, 4 * g + h, :]
                                nc.tensor.matmul(half(g, 0)[:, col(h)], qkT[:, 4 + 2 * g + h // 2, tok], s, start=True, stop=True)
                                mm = nc.tensor.matmul(half(g, 1)[:, col(h)], qkT[:, 2 * g + h // 2, tok], s, start=True, stop=True)
                            gdone(g, mm)
                    yield
                    for g in range(2):
                        gat(g, u + "res")
                        for h in range(4):
                            mm = nc.tensor.matmul(half(g, 0)[:, col(h)], TT[g][:, h, :], Rm[g][:, h, :], start=True, stop=True)
                        gdone(g, mm)
                    yield
                    for g in range(2):
                        gat(g, u + "vn")
                        for h in range(4):
                            if not c:
                                nc.tensor.matmul(half(g, 0)[:, col(h)], k_tail[g][:, h, :], Vn[g][:, h, :], start=True, stop=True)
                            mm = nc.tensor.matmul(half(g, 1)[:, col(h)], ET[g][:, h, :], Vn[g][:, h, :], start=True, stop=True)
                        gdone(g, mm)
                yield

            pe.wait_ge(first_in, 16 * 2)
            for n in range(4):
                pe.wait_ge(x_in[n], 16)
                if n == 3:
                    pe.wait_ge(xlo_done, 1)
                transposes(lambda m, t: x[:, m, n * NB + t * P:n * NB + (t + 1) * P], first_xt[n], 4).then_inc(xt_ready, 1)
            pe.wait_ge(xlo_done, 3)
            body("l0a", 0, 2, hT_hi, hT_lo, [None, None], fresh=(0, 1),
                 between=lambda w: pe.wait_ge(xlo_done, 4) if w == 5 else None)
            body("l0a", 1, 2, hT_hi, hT_lo, [None, None])
            gate_products(0)
            mixer = l0_mixer()
            pe.wait_ge(gates_out, 1)
            body("l0b", 0, 2, hT_hi, hT_lo, [None, None], between=lambda w: l0_slots(mixer, w))
            l0("rot3_copy")
            gate_transposes(0)
            body("l0c", 0, 8, hT_hi, hT_lo, [None] * 8, between=lambda w: l0_slots(mixer, w + 16))
            for _ in mixer:
                pass
            l0("mix3_lo")
            residual_phase("out0", mixT_hi, mixT_lo, True)
            ffn("gu0", "out0", 0)
            residual_phase("dn0", fT_hi, fT_lo, True)
            def between_q(w):
                if w == 2:
                    gate_products(1)
                if w == 4:
                    gate_transposes(1)
                if w == GATES_AT:
                    gdn_gates()
            body("l1p", 0, 2, hT_hi, hT_lo, [None] * 2, between=last_x_block("dn0"))
            body("l1q", 0, 2, hT_hi, hT_lo, [None] * 2, between=between_q)
            pe.wait_ge(gate_step, GATE_AT["sums_exp"])
            with pe.Fori(0, ROUNDS - 1) as r:
                mixer = gdn(r)
                body("l1r", r, 4, hT_hi, hT_lo, [None] * 4, between=lambda w: next(mixer, None))
                for _ in mixer:
                    pass

            def o_transposes(n):
                r = O_ORDER[n]
                pe.wait_ge(gated, 2 * r + 2)
                if n:
                    pe.wait_ge(o_lo, 2 * n)
                for g in range(2):
                    transposes(lambda m, t: o_z[r][:, m, (4 * g + t) * P:(4 * g + t + 1) * P], aux[g], 4).then_inc(o_tr, 1)

            def after_unit(w):
                next(mixer, None)
                if w in O_SLOTS:
                    if w == O_SLOTS[0]:
                        pe.wait_ge(gdn_step, (ROUNDS - 1) * GDN_N + GDN_AT[f"o{M - 1}_norm"])
                    o_transposes(O_SLOTS.index(w))
            mixer = gdn(ROUNDS - 1)
            body("l1z", 0, 8, hT_hi, hT_lo, [None] * 8, between=after_unit)
            o_transposes(3)
            pe.wait_ge(o_lo, 8)
            residual_phase("out1", oT_hi, oT_lo, True)
            ffn("gu1", "out1", FF // NB)
            residual_phase("dn1", fT_hi, fT_lo, False)

        @block.scalar
        def _(act):
            def body(name, i, n_body, hook):
                upb = UPB[name]
                for b in range(n_body):
                    for j in range(upb):
                        w = b * upb + j
                        s = w % SLOTS
                        act.wait_ge(raw_in[s], i * (n_body * upb // SLOTS * 16) + 16 * ((UNIT0[name] + w) // SLOTS + 1))
                        if not (isinstance(i, int) and i * n_body * upb + UNIT0[name] + w < SLOTS):
                            act.wait_ge(unit_used, i * (n_body * upb) + (UNIT0[name] + w - SLOTS + 1))
                        nc.scalar.activation(whi[:, s, :], wraw[:, s, :], ACT.Copy).then_inc(hi_done, 1)
                        hook(i, b, j)

            def gate_hi(layer):
                act.wait_ge(gw_in, 16 * (layer + 1))
                nc.scalar.activation(gw_hi[layer][:], gw_raw[layer][:], ACT.Copy).then_inc(gw_hi_done, 1)

            def gates_copy(layer):
                act.wait_ge(gw_used, layer + 1)
                w = GW[layer]
                nc.scalar.activation(gates_T[layer][0:w, :], aux4[2][0:w, 0:SEQ], ACT.Copy).then_inc(gates_out, 1)

            def copy_out(name, n, parity, dst, func=ACT.Copy):
                act.wait_ge(unit_used, n * UPB[name] + (UNIT0[name] + UPB[name]))
                for m in range(M):
                    a = nc.scalar.activation(dst(m), acc[parity][:, m, :], func, scale=rstd[:, m:m + 1])
                return a.then_inc(acc_read[parity], 1)

            def root(norm):
                act.wait_ge(mean_done, norm + 1)
                nc.scalar.activation(rms[:], mean[:], ACT.Sqrt, bias=epsc[:, 0:1], scale=1.0 / D).then_inc(rms_done, 1)
                act.wait_ge(rstd_done, norm + 1)

            def x_block(norm, n, src):
                k = n + 4 * norm
                for m in range(M):
                    a = nc.scalar.activation(aux[1][:, m * NB:(m + 1) * NB], src(m), ACT.Square,
                                             accum_out=ssq[:, m, bass.ds(n, 1)])
                if norm < 4:
                    act.wait_ge(xt_ready, k + 1)
                    xt = aux[0] if norm else first_xt[n]
                    for t in range(4):
                        a = nc.scalar.activation(hT_hi[:, bass.ds(n * 4 + t, 1), :].rearrange("p a b -> p (a b)"),
                                                 xt[:, t * SEQ:(t + 1) * SEQ], ACT.Copy,
                                                 scale=gains[:, norm, bass.ds(n * 4 + t, 1)])
                a.then_inc(xhi_done, 1)

            def residual_phase(name):
                norm = NORM_OF[name]

                def hook(i, b, j):
                    if j == 7 and not (b == 0 and isinstance(i, int) and i == 0):
                        n = i * 2 + (b - 1)
                        act.drain()
                        act.wait_ge(acc_read[1 - b], i + (BLOCK0[name] // 2 + b))
                        x_block(norm, n, lambda m: xs[:, m, :])
                body(name, 0, 2, hook)
                with act.Fori(1, 2) as i:
                    body(name, i, 2, hook)

            def last_x_block(name):
                act.drain()
                act.wait_ge(acc_read[1], BLOCK0[name] // 2 + 2)
                x_block(NORM_OF[name], 3, lambda m: xs[:, m, :])

            def ffn(name, after, n0):
                def f_hi(i):
                    act.wait_ge(ft_ready, i + n0)
                    nc.scalar.activation(fT_hi[:, bass.ds(i * 4 - 4, 4), :].rearrange("p a b -> p (a b)"), aux[1][:, :], ACT.Copy
                                         ).then_inc(fhi_done, 1)

                def hook(i, b, j):
                    first = isinstance(i, int) and i == 0
                    if first and b == 0 and j == 3:
                        last_x_block(after)
                    if first and b == 0 and j == 4:
                        root(NORM_OF[after])
                    if b == 1 and j == 3:
                        if not (first and n0 == 0):
                            act.wait_ge(acc_read[1], i + BLOCK0[name] // 2)
                        copy_out(name, i * 2, 0, lambda m: sg[:, m, :], ACT.Silu)
                    if b == 0 and j == 7 and not first:
                        f_hi(i)
                body(name, 0, 2, hook)
                with act.Fori(1, FF // NB) as i:
                    body(name, i, 2, hook)
                f_hi(FF // NB)

            act.wait_ge(first_in, 16 * 2)
            act.wait_ge(eps_set, 1)
            for n in range(4):
                act.drain()
                act.wait_ge(x_in[n], 16)
                x_block(0, n, lambda m: x[:, m, n * NB:(n + 1) * NB])

            def l0(name):
                act.wait_ge(l0_step, L0_AT[name])

            def done(a):
                a.then_inc(l0_step, 1)

            def head_squares(base, h, to):
                for m in range(M):
                    nc.scalar.activation(aux4[1][:, m * 256:(m + 1) * 256], pr[:, m, base + h * 256:base + (h + 1) * 256],
                                         ACT.Square, accum_out=gate_t[:, 9, to + h * 2 + m:to + h * 2 + m + 1])

            def head_rms(at):
                act.drain()
                return nc.scalar.activation(gate_t[:, 9, 8:16], gate_t[:, 9, at:at + 8], ACT.Sqrt, bias=epsc[:, 0:1], scale=1.0 / 256)

            def l0_mixer():
                l0("pos")
                done(nc.scalar.activation(cs[:].rearrange("p a b c -> p (a b c)"), ang[:].rearrange("p a b c -> p (a b c)"), ACT.Sin))
                for i in range(2 * M):
                    yield
                    l0(f"rot{i}_tr")
                    dst = (qrT, krT)[i // M]
                    m = i % M
                    done(nc.scalar.activation(dst[:, :, m * P:(m + 1) * P], aux[i % 2][:, :].rearrange("p (a b) -> p a b", b=P), ACT.Copy))
                yield
                g8 = gate_t[:, 0, 0:16]
                l0("gates")
                done(nc.scalar.activation(g8, g8, ACT.Tanh, scale=1.0 / SOFTCAP))
                l0("cap")
                done(nc.scalar.activation(gate_t[:, 2, 0:8], gate_t[:, 2, 0:8], ACT.Exp, scale=-1.0))
                yield
                l0("m_tr")
                nc.scalar.activation(qmT[:, :, :].rearrange("p a b -> p (a b)"), aux[0][:, :], ACT.Copy)
                done(nc.scalar.activation(kmT[:, :, :].rearrange("p a b -> p (a b)"), aux[1][:, :], ACT.Copy))
                for h in range(RH):
                    yield
                    yield
                    l0(f"r{h}_o_psum")
                    done(nc.scalar.activation(pr[:, :, VR + h * RD:VR + (h + 1) * RD], aux4[2].rearrange("p (m n) -> p m n", m=M), ACT.Copy))
                    act.drain()
                    head_squares(VR, h, 24)
                for h in range(MH):
                    yield
                    l0(f"m{h}_d_max")
                    if h:
                        act.drain()
                        head_squares(VM, h - 1, 16)
                    nc.scalar.activation(p_sb[:, 0:P], d_sb[:, 0:P], ACT.Exp, bias=gate_t[:, 5, 0:1])
                    nc.scalar.activation(p_sb[:, P:3 * P], d_sb[:, P:3 * P], ACT.Exp, bias=gate_t[:, 5, 1:2])
                    done(nc.scalar.activation(gate_t[:, 5, 2:4], gate_t[:, 5, 0:2], ACT.Exp))
                    yield
                    yield
                    l0(f"m{h}_st_psum")
                    done(nc.scalar.activation(st_sb[:], aux4[0][:, 0:3 * P], ACT.Copy))
                    yield
                yield
                l0(f"m{MH - 1}_num_div")
                head_squares(VM, MH - 1, 16)
                head_rms(16)
                done(nc.scalar.activation(pr[:, :, OM:OM + 1024], pr[:, :, OM:OM + 1024], ACT.Sigmoid))
                for g in range(4):
                    if g == 2:
                        yield
                        l0("mix1_lo")
                        head_rms(24)
                        done(nc.scalar.activation(pr[:, :, GR:GR + 1024], pr[:, :, GR:GR + 1024], ACT.Silu))
                    yield
                    l0(f"mix{g}_tr")
                    done(nc.scalar.activation(mixT_hi[:, 4 * g:4 * g + 4, :].rearrange("p a b -> p (a b)"), aux[g % 2][:, :], ACT.Copy))

            def pr_out(name, i, b):
                first = {"l0a": QR, "l0b": QM, "l0c": VR}[name]
                copy_out(name, i * 2 + (b - 1), (b + 1) % 2, lambda m: pr[:, m, bass.ds(i * 2 * NB + (first + (b - 1) * NB), NB)])

            def hook_a(i, b, j):
                first = isinstance(i, int) and i == 0 and b == 0
                if first and j == 1:
                    root(0)
                if j == 3 and not first:
                    pr_out("l0a", i, b)

            def hook_b(i, b, j):
                if b == 0 and j == 1:
                    gates_copy(0)
                if j == 3:
                    pr_out("l0a" if b == 0 else "l0b", 1 if b == 0 else 0, 2 if b == 0 else 1)
                l0_slots(mixer, b * UPB["l0b"] + j - AHEAD)

            def hook_c(i, b, j):
                if j == 3:
                    pr_out("l0b" if b == 0 else "l0c", 0, 2 if b == 0 else b)
                l0_slots(mixer, 16 + b * UPB["l0c"] + j - AHEAD)

            body("l0a", 0, 2, hook_a)
            gate_hi(0)
            body("l0a", 1, 2, hook_a)
            mixer = l0_mixer()
            body("l0b", 0, 2, hook_b)
            body("l0c", 0, 8, hook_c)
            pr_out("l0c", 0, 8)
            act.drain()
            for _ in mixer:
                pass

            residual_phase("out0")
            ffn("gu0", "out0", 0)
            residual_phase("dn0")

            def gdn_gates():
                act.wait_ge(l1_const, 16 * 4)
                act.wait_ge(gate_step, GATE_AT["raw"])
                nc.scalar.activation(gate_t[:, 2, :], gate_t[:, 2, :], ACT.Exp, scale=-1.0)
                nc.scalar.activation(gate_t[:, 8, 0:32], gate_t[:, 8, 0:32], ACT.Exp)
                nc.scalar.activation(gate_t[:, 0, :], gate_t[:, 0, :], ACT.Sigmoid).then_inc(gate_step, 1)
                yield
                act.wait_ge(gate_step, GATE_AT["sums"])
                nc.scalar.activation(gate_t[:, 4, :], aux4[2][:, 0:64], ACT.Exp)
                nc.scalar.activation(gate_t[:, 5, :], aux4[3][:, 0:64], ACT.Exp).then_inc(gate_step, 1)

            def gdn(r):
                def at(name):
                    act.wait_ge(gdn_step, r * GDN_N + GDN_AT[name])

                def done(a):
                    a.then_inc(gdn_step, 1)

                def gat(g, name):
                    act.wait_ge(group_step[g], r * GROUP_N + GROUP_AT[name])

                flat = lambda t: t.rearrange("p a b -> p (a b)")
                conv_out = (qkT[:, 0:4], qkT[:, 4:8], vT[:, 0:4], vT[:, 4:8])

                def silu(b):
                    act.wait_ge(conv_sum, r * 4 + (b + 1))
                    nc.scalar.activation(flat(conv_out[b]), flat(conv_out[b]), ACT.Silu).then_inc(conv_silu, 1)

                def roots():
                    act.wait_ge(norm_step, r * len(NORM_STEPS) + NORM_AT["sums"])
                    nc.scalar.activation(qk_rms[:, 0, :], aux[0][:, 0:8], ACT.Sqrt, bias=epsc[:, 1:2], scale=float(GD))
                    nc.scalar.activation(qk_rms[:, 1, :], aux[0][:, 8:16], ACT.Sqrt, bias=epsc[:, 0:1], scale=1.0
                                         ).then_inc(norm_step, 1)

                def tok_out(n):
                    act.wait_ge(tok_tr, r * 3 + (n + 1))
                    if n < 2:
                        a = nc.scalar.activation(v_tok[:, :, n * NB:(n + 1) * NB], aux[1][:, :].rearrange("p (m n) -> p m n", m=M), ACT.Copy)
                    else:
                        a = nc.scalar.activation(flat(k_tok[:]), aux[0][:, :], ACT.Copy)
                    a.then_inc(tok_copy, 1)
                for b in range(4):
                    if b:
                        yield
                    act.wait_ge(conv_tr, r * 4 + (b + 1))
                    for t in range(4):
                        a = nc.scalar.activation(conv_out[b][:, t, :], aux[b % 2][:, t * SEQ:(t + 1) * SEQ], ACT.Copy,
                                                 scale=conv_r[:, 4 * b + t, CW - 1:CW])
                    a.then_inc(conv_tap, 1)
                    if b:
                        silu(b - 1)
                yield
                silu(3)
                roots()
                yield
                tok_out(0)
                yield
                yield
                tok_out(1)
                yield
                tok_out(2)

                def square_o(c):
                    for g in range(2):
                        gat(g, f"t{c}_o")
                    done(nc.scalar.activation(v_tok[:, c, :], o_r[:, c, :], ACT.Square))

                def root_o(c):
                    at(f"o{c}_sum")
                    done(nc.scalar.activation(o_ms[:, c, :], o_ms[:, c, :], ACT.Sqrt, bias=epsc[:, 0:1], scale=1.0 / GD))
                for c in range(M):
                    u = f"t{c}_"
                    yield
                    for g in range(2):
                        gat(g, u + "d_psum")
                        nc.scalar.activation(flat(EA[g][:]), aux[g][:, 0:NB], ACT.Exp).then_inc(group_step[g], 1)
                    if c:
                        square_o(0)
                    yield
                    for n in range(len(LEVELS)):
                        yield
                        if n == 2 and c:
                            root_o(0)
                        if n:
                            for g in range(2):
                                gat(g, u + f"l{n}_q_psum")
                                nc.scalar.activation(flat(Q1[g][:]), aux[g][:, 0:NB], ACT.Copy).then_inc(group_step[g], 1)
                            yield
                    if c:
                        yield
                    yield
                    for g in range(2):
                        gat(g, u + "vn_psum")
                        nc.scalar.activation(flat(Vn[g][:]), aux[g][:, 0:NB], ACT.Copy).then_inc(group_step[g], 1)
                    yield
                    if not c:
                        for g in range(2):
                            gat(g, u + "o")
                            nc.scalar.activation(flat(St[:, 4 * g:4 * g + 4, :]), aux[g][:, 0:NB], ACT.Copy).then_inc(group_step[g], 1)
                yield
                square_o(M - 1)
                root_o(M - 1)

            def qkv_out(name, n, b, q):
                copy_out(name, n, b % 2, lambda m: qkv[:, m, q * NB:(q + 1) * NB])

            def z_out(n):
                if n:
                    act.wait_ge(gated, n)
                copy_out("l1z", n, n % 2, lambda m: zs[n][:, m, :], ACT.Silu)

            gates = gdn_gates()

            def hook_p(i, b, j):
                if b == 0 and j == 3:
                    last_x_block("dn0")
                if b == 0 and j == 4:
                    root(2)
                if b == 1 and j == 3:
                    qkv_out("l1p", 0, 0, 0)

            def hook_q(i, b, j):
                if b == 0 and j == 0:
                    gate_hi(1)
                if b == 0 and j == 4:
                    gates_copy(1)
                if j == 3:
                    qkv_out("l1p" if b == 0 else "l1q", 1 - b, 1 - b, 1 + b)
                if b * UPB["l1q"] + j in (GATES_AT - 3, GATES_AT + AHEAD):
                    next(gates, None)

            def hook_r(r, b, j):
                if j == 3 and b:
                    qkv_out("l1r", r * 4 + (b - 1), b - 1, b - 1)
                if b * UPB["l1r"] + j >= AHEAD:
                    next(mixer, None)

            def o_split(n):
                act.wait_ge(o_tr, 2 * n + 2)
                for g in range(2):
                    t = O_ORDER[n] * HV + 4 * g
                    nc.scalar.activation(oT_hi[:, t:t + 4, :].rearrange("p a b -> p (a b)"), aux[g][:, :], ACT.Copy
                                         ).then_inc(o_hi, 1)

            def hook_z(i, b, j):
                w = b * UPB["l1z"] + j
                if j == 3 and b:
                    z_out(b - 1)
                if w >= AHEAD:
                    next(mixer, None)
                if w == 6 + AHEAD:
                    act.wait_ge(conv_tr, ROUNDS * 4)
                    act.wait_ge(o_stored, 16 * (ROUNDS - 1))
                    for r in range(ROUNDS - 1):
                        act.dma_start(o_z[r][:], o_dram[:, r * HV * GD:(r + 1) * HV * GD].rearrange("(m p) n -> p m n", p=P)
                                      ).then_inc(o_loaded[r], 16)
                if w - AHEAD in O_SLOTS:
                    o_split(O_SLOTS.index(w - AHEAD))

            body("l1p", 0, 2, hook_p)
            act.wait_ge(xs_copied, 8)
            body("l1q", 0, 2, hook_q)
            qkv_out("l1q", 1, 1, 3)
            with act.Fori(0, ROUNDS - 1) as r:
                mixer = gdn(r)
                body("l1r", r, 4, hook_r)
                for _ in range(AHEAD + 1):
                    next(mixer)
                qkv_out("l1r", r * 4 + 3, 3, 3)
                for _ in mixer:
                    pass
            mixer = gdn(ROUNDS - 1)
            body("l1z", 0, 8, hook_z)
            z_out(7)
            o_split(3)
            residual_phase("out1")
            ffn("gu1", "out1", FF // NB)
            residual_phase("dn1")
            last_x_block("dn1")
            root(4)

        @block.vector
        def _(dve):
            V = nc.vector

            def body(name, i, n_body, hook):
                upb = UPB[name]
                for b in range(n_body):
                    for j in range(upb):
                        w = b * upb + j
                        s = w % SLOTS
                        if name in ("l1r", "l1z"):
                            if w in POOL_UNITS:
                                hook(i, b, j)
                                continue
                            if w == POOL_UNITS[-1] + 1:
                                dve.wait_ge(lo_done, i * (n_body * upb) + (UNIT0[name] + w))
                        dve.wait_ge(hi_done, i * (n_body * upb) + (UNIT0[name] + w + 1))
                        if not (isinstance(i, int) and i * n_body * upb + UNIT0[name] + w < SLOTS):
                            dve.wait_ge(unit_used, i * (n_body * upb) + (UNIT0[name] + w - SLOTS + 1))
                        V.tensor_tensor(wlo[:, s, :], wraw[:, s, :], whi[:, s, :].bitcast(F32), ALU.subtract).then_inc(lo_done, 1)
                        hook(i, b, j)

            def gate_lo(layer):
                dve.wait_ge(gw_hi_done, layer + 1)
                V.tensor_tensor(gw_lo[layer][:], gw_raw[layer][:], gw_hi[layer][:].bitcast(F32), ALU.subtract
                                ).then_inc(gw_lo_done, 1)

            def recip(norm):
                dve.wait_ge(rms_done, norm + 1)
                V.reciprocal(rstd[:], rms[:]).then_inc(rstd_done, 1)
                dve.drain()

            def x_lo(norm, n):
                dve.wait_ge(xhi_done, n + (4 * norm + 1))
                xt = aux[0] if norm else first_xt[n]
                if norm < 4:
                    for t in range(4):
                        a = V.scalar_tensor_tensor(
                            hT_lo[:, bass.ds(n * 4 + t, 1), :].rearrange("p a b -> p (a b)"),
                            xt[:, t * SEQ:(t + 1) * SEQ], gains[:, norm, bass.ds(n * 4 + t, 1)],
                            hT_hi[:, bass.ds(n * 4 + t, 1), :].rearrange("p a b -> p (a b)").bitcast(F32),
                            op0=ALU.mult, op1=ALU.subtract)
                    a.then_inc(xlo_done, 1)

            def mean_square():
                V.tensor_reduce(mean[:], ssq[:], AX.X, ALU.add).then_inc(mean_done, 1)

            def residual_phase(name):
                norm = NORM_OF[name]

                def add(n, parity):
                    dve.wait_ge(unit_used, n * UPB[name] + (UNIT0[name] + UPB[name]))
                    if not (norm == 1 and isinstance(n, int) and n == 0):
                        dve.wait_ge(xs_copied, n + 4 * (norm - 1))
                    dve.wait_ge(xhi_done, n + 4 * norm)
                    V.tensor_tensor(xs[:], acc[parity][:, :, :], x[:, :, bass.ds(n * NB, NB)], ALU.add
                                    ).then_inc(acc_read[parity], 1)

                def hook(i, b, j):
                    if b == 0 and isinstance(i, int) and i == 0:
                        return
                    if j == 3:
                        add(i * 2 + (b - 1), (b + 1) % 2)
                    if j == 7:
                        x_lo(norm, i * 2 + (b - 1))
                body(name, 0, 2, hook)
                with dve.Fori(1, 2) as i:
                    body(name, i, 2, hook)

                def last_x_block(j):
                    if j == 1:
                        add(3, 1)
                    if j == 3:
                        x_lo(norm, 3)
                        mean_square()
                    if j == 4:
                        recip(norm)
                return last_x_block

            def ffn(name, after, last_x_block, n0):
                norm = NORM_OF[after]

                def up(i):
                    dve.wait_ge(acc_read[0], i + BLOCK0[name] // 2)
                    dve.wait_ge(unit_used, i * (2 * UPB[name]) + UNIT0[name])
                    if isinstance(i, int) and i == 1:
                        dve.wait_ge(xs_copied, 4 * norm)
                    else:
                        dve.wait_ge(ft_ready, i + (n0 - 1))
                    for m in range(M):
                        a = V.scalar_tensor_tensor(prod[:, m, :], acc[1][:, m, :], rstd[:, m:m + 1], sg[:, m, :],
                                                   op0=ALU.mult, op1=ALU.mult)
                    a.then_inc(acc_read[1], 1)

                def f_lo(i):
                    dve.wait_ge(fhi_done, i + n0)
                    V.tensor_tensor(fT_lo[:, bass.ds(i * 4 - 4, 4), :].rearrange("p a b -> p (a b)"), aux[1][:, :],
                                    fT_hi[:, bass.ds(i * 4 - 4, 4), :].rearrange("p a b -> p (a b)").bitcast(F32), ALU.subtract
                                    ).then_inc(flo_done, 1)

                def hook(i, b, j):
                    first = isinstance(i, int) and i == 0
                    if first and b == 0:
                        last_x_block(j)
                    if b == 0 and not first:
                        if j == 3:
                            up(i)
                        if j == 7:
                            f_lo(i)
                body(name, 0, 2, hook)
                body(name, 1, 2, hook)
                with dve.Fori(2, FF // NB) as i:
                    body(name, i, 2, hook)
                up(FF // NB)
                f_lo(FF // NB)

            def log1p(dst, y, w):
                z, z2, p = (gate_t[:, k, 0:w] for k in (5, 6, 7))
                V.tensor_scalar(z, y, 2.0, None, ALU.add)
                dve.drain()
                V.reciprocal(z, z)
                dve.drain()
                V.tensor_tensor(z, z, y, ALU.mult)
                dve.drain()
                V.tensor_tensor(z2, z, z, ALU.mult)
                dve.drain()
                V.tensor_scalar(p, z2, 1.0 / 15, None, ALU.mult)
                for k in (13, 11, 9, 7, 5, 3):
                    dve.drain()
                    V.scalar_tensor_tensor(p, p, 1.0 / k, z2, op0=ALU.add, op1=ALU.mult)
                dve.drain()
                V.scalar_tensor_tensor(p, p, 1.0, z, op0=ALU.add, op1=ALU.mult)
                dve.drain()
                V.tensor_scalar(dst, p, 2.0, None, ALU.mult)
                dve.drain()

            V.memset(epsc[:, 0:1], EPS)
            V.memset(epsc[:, 1:2], GD * EPS).then_inc(eps_set, 1)
            dve.wait_ge(first_in, 16 * 2)
            for n in range(4):
                x_lo(0, n)
            mean_square()
            nothing = lambda i, b, j: None
            flat2 = lambda t: t.rearrange("p a b -> p (a b)")
            col = lambda k, a, b: gate_t[:, k, a:b]

            def l0(name):
                dve.wait_ge(l0_step, L0_AT[name])

            def done(a):
                a.then_inc(l0_step, 1)

            def projected(blocks):
                for b in range(2):
                    dve.wait_ge(acc_read[b], blocks // 2)

            def head_norm(base, gate_col, row):
                V.reciprocal(col(6, 16, 24), col(9, 8, 16))
                dve.drain()
                for h in range(4):
                    for m in range(M):
                        y = pr[:, m, base + h * 256:base + (h + 1) * 256]
                        s = col(6, 16 + 2 * h + m, 17 + 2 * h + m)
                        other = row[:, h * 256:(h + 1) * 256] if row is not None else pr[:, m, gate_col + h * 256:gate_col + (h + 1) * 256]
                        a = V.scalar_tensor_tensor(y, y, s, other, op0=ALU.mult, op1=ALU.mult)
                if row is not None:
                    dve.drain()
                    a = V.tensor_tensor(pr[:, :, base:base + 1024], pr[:, :, base:base + 1024],
                                        pr[:, :, gate_col:gate_col + 1024], ALU.mult)
                done(a)

            def rows(h):
                lf = [col(4, 4 * m + h, 4 * m + h + 1) for m in range(M)]
                li = [col(0, 8 * m + h, 8 * m + h + 1) for m in range(M)]
                V.tensor_scalar(d_rows[:, 0, :], C["after"], lf[0], None, ALU.mult)
                V.tensor_scalar(d_rows[:, 1, :], C["ones"], lf[1], None, ALU.mult)
                V.tensor_scalar(d_rows[:, 2, :], C["after"], lf[1], None, ALU.mult)
                V.tensor_scalar(d_rows[:, 4, :], ident, li[1], None, ALU.mult)
                V.tensor_scalar(d_rows[:, 5, :], ident, li[0], None, ALU.mult)
                dve.drain()
                done(V.tensor_tensor(d_rows[:, 3, :], d_rows[:, 0, :], d_rows[:, 5, :], ALU.add))

            def rotate(i):
                m = i % M
                src = pr[:, m, (QR, KR)[i // M]:(QR, KR)[i // M] + 1024].rearrange("p (h n two) -> p h n two", h=RH, two=2)
                t1, t2 = src[:, :, :, 0], src[:, :, :, 1]
                cos, sin = (cs[:, k, m, :].unsqueeze(1).to_broadcast([P, RH, P]) for k in (0, 1))
                for half, (f1, f2, op) in enumerate(((cos, sin, ALU.subtract), (sin, cos, ALU.add))):
                    V.tensor_tensor(rot_a[:], t1, f1, ALU.mult)
                    V.tensor_tensor(rot_b[:], t2, f2, ALU.mult)
                    dve.drain()
                    a = V.tensor_tensor(rot[:, :, half, :], rot_a[:], rot_b[:], op)
                    if half == 0:
                        dve.drain()
                done(a)

            def l0_mixer():
                dve.wait_ge(consts_in, 16 * 4)
                V.tensor_copy(col(9, 2, 4), gate_t[:, 9, 0:2].bitcast(I32))
                dve.drain()
                for m in range(M):
                    V.tensor_scalar(ang[:, 1, m, :], C["freq"], col(9, 2 + m, 3 + m), None, ALU.mult)
                dve.drain()
                sin_a, cos_a = flat2(ang[:, 1]), flat2(ang[:, 0])
                turns = rot_a[:, 0:2, :].rearrange("p a b -> p (a b)")
                MAGIC = 12582912.0
                V.tensor_scalar(turns, sin_a, 1.0 / (2 * np.pi), None, ALU.mult)
                dve.drain()
                V.tensor_scalar(turns, turns, MAGIC, None, ALU.add)
                dve.drain()
                V.tensor_scalar(turns, turns, -MAGIC, None, ALU.add)
                dve.drain()
                for part in TWO_PI:
                    V.scalar_tensor_tensor(sin_a, turns, -part, sin_a, op0=ALU.mult, op1=ALU.add)
                    dve.drain()
                V.tensor_scalar(cos_a, sin_a, float(np.pi / 2), None, ALU.add)
                dve.drain()
                V.tensor_scalar(turns, cos_a, float(np.pi), -2 * float(np.pi), ALU.is_gt, ALU.mult)
                dve.drain()
                V.tensor_tensor(cos_a, cos_a, turns, ALU.add)
                dve.drain()
                both = ang[:].rearrange("p a b c -> p (a b c)")
                done(V.tensor_scalar(both, both, PI_BELOW, -PI_BELOW, ALU.min, ALU.max))
                l0("sincos")
                projected(2)
                rotate(0)
                for i in range(2 * M):
                    yield
                    if i < 2 * M - 1:
                        l0(f"rot{i}_copy")
                        projected(2 if i == 0 else 4)
                        rotate(i + 1)
                yield
                l0("rot3_copy")
                dve.wait_ge(gates_tr, 1)
                for m in range(M):
                    a = V.scalar_tensor_tensor(col(0, 8 * m, 8 * m + 8), aux4[2 + m][:, 0:8], rstd[:, m:m + 1], col(8, 0, 8),
                                               op0=ALU.mult, op1=ALU.add)
                done(a)
                l0("tanh")
                V.tensor_scalar(col(0, 0, 16), col(0, 0, 16), SOFTCAP, None, ALU.mult)
                dve.drain()
                fg = col(0, 0, 16).rearrange("p (m c) -> p m c", m=M)[:, :, 4:8]
                pair = lambda k: col(k, 0, 8).rearrange("p (m c) -> p m c", m=M)
                done(V.scalar_tensor_tensor(pair(2), fg, -1.0, fg, op0=ALU.mult, op1=ALU.max))
                l0("exp")
                log1p(col(3, 0, 8), col(2, 0, 8), 8)
                done(V.scalar_tensor_tensor(pair(4), fg, 0.0, pair(3), op0=ALU.min, op1=ALU.subtract))
                dve.drain()
                yield
                for h in range(RH):
                    yield
                    l0(f"r{h}_s_psum")
                    dec = C["decay"][:, h * 256:(h + 1) * 256]
                    V.tensor_tensor(rs_sb[:, 0:256], aux4[0][:, 0:256], dec, ALU.mult)
                    done(V.tensor_tensor(rs_sb[:, 256:384], aux4[0][:, 256:384], dec[:, 0:P], ALU.mult))
                    yield
                for h in range(MH):
                    l0("r3_o_copy" if h == 0 else f"m{h - 1}_num_div")
                    rows(h)
                    yield
                    l0(f"m{h}_d_psum")
                    V.tensor_tensor(d_sb[:], aux4[0][:, 0:3 * P], C["neg"], ALU.add)
                    dve.drain()
                    V.tensor_reduce(col(6, 0, 1), d_sb[:, 0:P], AX.X, ALU.max)
                    V.tensor_reduce(col(6, 1, 2), d_sb[:, P:3 * P], AX.X, ALU.max)
                    dve.drain()
                    done(V.tensor_scalar(col(5, 0, 2), col(6, 0, 2), -1.0, None, ALU.mult))
                    yield
                    l0(f"m{h}_s_psum")
                    V.scalar_tensor_tensor(d_sb[:, 0:P], aux4[2][:, 0:P], MDQK ** -0.5, p_sb[:, 0:P],
                                           op0=ALU.mult, op1=ALU.mult, accum_out=col(6, 2, 3))
                    V.scalar_tensor_tensor(d_sb[:, P:3 * P], aux4[2][:, P:3 * P], MDQK ** -0.5, p_sb[:, P:3 * P],
                                           op0=ALU.mult, op1=ALU.mult, accum_out=col(6, 3, 4))
                    dve.drain()
                    V.scalar_tensor_tensor(col(6, 4, 6), col(6, 2, 4), -1.0, col(6, 2, 4), op0=ALU.mult, op1=ALU.max)
                    dve.drain()
                    V.tensor_tensor(col(6, 4, 6), col(6, 4, 6), col(5, 2, 4), ALU.max)
                    dve.drain()
                    done(V.reciprocal(col(6, 6, 8), col(6, 4, 6)))
                    yield
                    yield
                    l0(f"m{h}_num_psum")
                    for m in range(M):
                        a = V.tensor_scalar(pr[:, m, VM + h * MDV:VM + (h + 1) * MDV], aux4[2][:, m * 256:(m + 1) * 256],
                                            col(6, 6 + m, 7 + m), None, ALU.mult)
                    done(a)
                yield
                l0("m_sq")
                head_norm(VM, OM, mnorm[:])
                for g in range(4):
                    if g == 2:
                        yield
                        l0("r_sq")
                        head_norm(VR, GR, None)
                    yield
                    l0(f"mix{g}_hi")
                    done(V.tensor_tensor(flat2(mixT_lo[:, 4 * g:4 * g + 4, :]), aux[g % 2][:, :],
                                         flat2(mixT_hi[:, 4 * g:4 * g + 4, :]).bitcast(F32), ALU.subtract))

            body("l0a", 0, 2, lambda i, b, j: recip(0) if b == 0 and j == 1 else None)
            gate_lo(0)
            body("l0a", 1, 2, nothing)
            mixer = l0_mixer()
            body("l0b", 0, 2, lambda i, b, j: l0_slots(mixer, b * UPB["l0b"] + j - AHEAD))
            body("l0c", 0, 8, lambda i, b, j: l0_slots(mixer, 16 + b * UPB["l0c"] + j - AHEAD))
            for _ in mixer:
                pass

            last_x_block = residual_phase("out0")
            ffn("gu0", "out0", last_x_block, 0)
            last_x_block = residual_phase("dn0")

            def gdn_gates():
                dve.wait_ge(l1_const, 16 * 4)
                dve.wait_ge(gates_tr, 2)
                for m in range(M):
                    mm = slice(32 * m, 32 * m + 32)
                    V.tensor_scalar(gate_t[:, 0, mm], aux4[2 + m][:, 0:32], rstd[:, m:m + 1], None, ALU.mult)
                    V.scalar_tensor_tensor(gate_t[:, 1, mm], aux4[2 + m][:, 32:64], rstd[:, m:m + 1], gate_t[:, 8, 32:64],
                                           op0=ALU.mult, op1=ALU.add)
                dve.drain()
                a_pre = gate_t[:, 1, :]
                V.scalar_tensor_tensor(gate_t[:, 2, :], a_pre, -1.0, a_pre, op0=ALU.mult, op1=ALU.max).then_inc(gate_step, 1)
                yield
                dve.wait_ge(gate_step, GATE_AT["exp"])
                log1p(gate_t[:, 3, :], gate_t[:, 2, :], 64)
                V.scalar_tensor_tensor(gate_t[:, 3, :], a_pre, 0.0, gate_t[:, 3, :], op0=ALU.max, op1=ALU.add)
                dve.drain()
                for m in range(M):
                    mm = slice(32 * m, 32 * m + 32)
                    a = V.scalar_tensor_tensor(gate_t[:, 1, mm], gate_t[:, 3, mm], -1.0, gate_t[:, 8, 0:32], op0=ALU.mult, op1=ALU.mult)
                a.then_inc(gate_step, 1)
                yield
                dve.wait_ge(gate_step, GATE_AT["sums_exp"])
                V.memset(gate_t[:, 2:4, :], 0.0)
                V.memset(gate_t[:, 6, :], 0.0)
                V.scalar_tensor_tensor(gate_t[:, 7, :], gate_t[:, 0, :], -1.0, gate_t[:, 4, :], op0=ALU.mult, op1=ALU.mult
                                       ).then_inc(gdn_step, 1)
                dve.drain()

            def gdn(r):
                def at(name):
                    dve.wait_ge(gdn_step, r * GDN_N + GDN_AT[name])

                def done(a):
                    a.then_inc(gdn_step, 1)

                dve.wait_ge(acc_read[0], r * 2 + BLOCK0["l1r"] // 2)
                dve.wait_ge(acc_read[1], r * 2 + BLOCK0["l1r"] // 2)
                per_round = gate_t[:, 0:8, :].rearrange("p s (m h) -> p (s m) h", m=M)
                V.tensor_copy(gr[:].rearrange("p s m h -> p (s m) h"), per_round[:, :, bass.ds(r * HV, HV)])
                V.tensor_copy(conv_r[:, 0:4, :], conv_w[:, bass.ds(r * 4, 4), :])
                V.tensor_copy(conv_r[:, 4:8, :], conv_w[:, bass.ds(r * 4 + 16, 4), :])
                done(V.tensor_copy(conv_r[:, 8:16, :], conv_w[:, bass.ds(r * 8 + 32, 8), :]))
                dve.drain()

                def per_head(slot, c, g):
                    return gr[:, slot, c, 4 * g:4 * g + 4].unsqueeze(2).to_broadcast([P, 4, P])

                def all_heads(t, n=4):
                    return t.unsqueeze(1).to_broadcast([P, n, t.shape[1]])

                heads = lambda t: t.rearrange("p (h n) -> p h n", n=P)
                twice = lambda t: t.rearrange("p (q e) n -> p q e n", e=2)
                for b in range(4):
                    if b:
                        yield
                    dve.wait_ge(conv_tap, r * 4 + (b + 1))
                    dst = (qkT[:, 0:4], qkT[:, 4:8], vT[:, 0:4], vT[:, 4:8])[b]
                    for lag in range(1, CW):
                        for t in range(4):
                            a = V.scalar_tensor_tensor(dst[:, t, lag:], aux[b % 2][:, t * SEQ:(t + 1) * SEQ - lag],
                                                       conv_r[:, 4 * b + t, CW - 1 - lag:CW - lag], dst[:, t, lag:],
                                                       op0=ALU.mult, op1=ALU.add)
                        if lag < CW - 1:
                            dve.drain()
                    a.then_inc(conv_sum, 1)

                def norm(name):
                    dve.wait_ge(norm_step, r * len(NORM_STEPS) + NORM_AT[name])

                def normalise(b, rows):
                    blk = qkT[:, 4 * b:4 * b + 4, :]
                    V.tensor_tensor(blk, blk, rows.rearrange("p (h n) -> p h n", n=SEQ), ALU.mult).then_inc(norm_step, 1)
                yield
                norm("roots")
                V.reciprocal(qk_rms[:], qk_rms[:]).then_inc(norm_step, 1)
                yield
                yield
                norm("k_row")
                normalise(1, aux[0][:, :])
                yield
                yield
                norm("q_row")
                normalise(0, aux[1][:, :])

                def gat(g, name):
                    dve.wait_ge(group_step[g], r * GROUP_N + GROUP_AT[name])

                def gdone(g, a):
                    a.then_inc(group_step[g], 1)

                def sum_o(c):
                    at(f"o{c}_sq")
                    done(V.tensor_reduce(o_ms[:, c, :], v_tok[:, c, :].rearrange("p (h n) -> p h n", n=GD), AX.X, ALU.add))

                def norm_o(c):
                    at(f"o{c}_rs")
                    V.reciprocal(o_ms[:, c, :], o_ms[:, c, :])
                    dve.drain()
                    o = o_r[:, c, :].rearrange("p (h n) -> p h n", n=GD)
                    V.tensor_tensor(o, o, o_ms[:, c, :].unsqueeze(2).to_broadcast([P, HV, GD]), ALU.mult)
                    dve.drain()
                    done(V.tensor_tensor(o, o, all_heads(gnorm[:], HV), ALU.mult))

                for c in range(M):
                    u = f"t{c}_"
                    for g in range(2):
                        if c:
                            gat(g, "t0_s_copy")
                        gdone(g, V.tensor_tensor(lam[g][:], all_heads(C["after"]), per_head(1, c, g), ALU.mult))
                    yield
                    yield
                    for g in range(2):
                        gat(g, u + "kq_psum")
                        V.tensor_tensor(kq[g][:], aux[g][:, 0:NB].rearrange("p (h n) -> p h n", h=2),
                                        all_heads(C["low_up"], 2), ALU.mult)
                        V.tensor_tensor(EA[g][:], EA[g][:], per_head(0, c, g), ALU.mult)
                        pair_of = lambda half: kq[g][:, :, half * P:(half + 1) * P].unsqueeze(2).to_broadcast([P, 2, 2, P])
                        dve.drain()
                        V.tensor_tensor(twice(ET[g][:]), twice(heads(aux[g][:, NB:])), pair_of(1), ALU.mult)
                        gdone(g, V.tensor_tensor(twice(EA[g][:]), twice(EA[g][:]), pair_of(0), ALU.mult))
                    for n in range(len(LEVELS)):
                        yield
                        if n == 0:
                            for g in range(2):
                                gat(g, u + "l0_q_psum")
                                V.tensor_tensor(T[g][:], all_heads(ident), Bm[g][0][:], ALU.subtract)
                                gdone(g, V.tensor_tensor(TT[g][:], all_heads(ident), heads(aux[g][:, 0:NB]), ALU.subtract))
                        else:
                            if c and n == 1:
                                sum_o(0)
                            if c and n == 3:
                                norm_o(0)
                            yield
                            for g in range(2):
                                gat(g, u + f"l{n}_t_psum")
                                if n < LAST:
                                    V.tensor_tensor(T[g][:], T[g][:], heads(aux[g][:, 0:NB]), ALU.subtract)
                                gdone(g, V.tensor_tensor(TT[g][:], TT[g][:], heads(aux[g][:, NB:]), ALU.subtract))
                    if c:
                        yield
                    if c == 0:
                        dve.wait_ge(tok_copy, r * 3 + 3)
                    for g in range(2):
                        bv = heads(v_tok[:, c, g * NB:(g + 1) * NB])
                        if c:
                            gat(g, u + "res_psum")
                            V.tensor_tensor(Rm[g][:], bv, per_head(0, c, g), ALU.mult)
                            V.tensor_tensor(qs_sb[g][:], heads(aux[g][:, NB:]), per_head(4, c, g), ALU.mult)
                            V.tensor_tensor(B0[g][:], heads(aux[g][:, 0:NB]), per_head(7, c, g), ALU.mult)
                            dve.drain()
                            gdone(g, V.tensor_tensor(Rm[g][:], Rm[g][:], B0[g][:], ALU.add))
                        else:
                            kt2 = heads(k_tok[:, c, g * 256:(g + 1) * 256]).unsqueeze(2).to_broadcast([P, 2, 2, P])
                            et2 = gr[:, 5, c, 4 * g:4 * g + 4].rearrange("p (q e) -> p q e", e=2).unsqueeze(3).to_broadcast([P, 2, 2, P])
                            V.tensor_tensor(twice(k_tail[g][:]), kt2, et2, ALU.mult)
                            gdone(g, V.tensor_tensor(Rm[g][:], bv, per_head(0, c, g), ALU.mult))
                    yield
                    yield
                    for g in range(2):
                        gat(g, u + "o_psum")
                        dst = o_r[:, c, g * NB:(g + 1) * NB]
                        if c:
                            gdone(g, V.tensor_tensor(dst, aux[g][:, NB:], flat2(qs_sb[g][:]), ALU.add))
                        else:
                            gdone(g, V.tensor_copy(dst, aux[g][:, NB:]))
                yield
                sum_o(M - 1)
                norm_o(M - 1)

            def hook_r(r, b, j):
                if b * UPB["l1r"] + j >= AHEAD:
                    next(mixer, None)

            def gate(n):
                if n == 6:
                    dve.drain()
                elif n % 2 == 0:
                    dve.wait_ge(o_loaded[n // 2], 16)
                dve.wait_ge(acc_read[n % 2], BLOCK0["l1z"] // 2 + n // 2 + 1)
                o = o_z[n // 2][:, :, n % 2 * NB:(n % 2 + 1) * NB]
                V.tensor_tensor(o, o, zs[n][:], ALU.mult).then_inc(gated, 1)

            def o_split(n):
                for g in range(2):
                    t = O_ORDER[n] * HV + 4 * g
                    dve.wait_ge(o_hi, 2 * n + g + 1)
                    V.tensor_tensor(flat2(oT_lo[:, t:t + 4, :]), aux[g][:, :], flat2(oT_hi[:, t:t + 4, :]).bitcast(F32),
                                    ALU.subtract).then_inc(o_lo, 1)

            def hook_z(i, b, j):
                w = b * UPB["l1z"] + j
                if j == 5 and b:
                    gate(b - 1)
                if w >= AHEAD:
                    next(mixer, None)
                if w - AHEAD in O_SLOTS:
                    o_split(O_SLOTS.index(w - AHEAD))

            body("l1p", 0, 2, lambda i, b, j: last_x_block(j) if b == 0 else None)
            gates = gdn_gates()

            def hook_q(i, b, j):
                w = b * UPB["l1q"] + j
                if w == 0:
                    gate_lo(1)
                if w in (GATES_AT - 4, GATES_AT - 2, GATES_AT + AHEAD + 1):
                    next(gates, None)
            body("l1q", 0, 2, hook_q)
            with dve.Fori(0, ROUNDS - 1) as r:
                mixer = gdn(r)
                body("l1r", r, 4, hook_r)
                for _ in mixer:
                    pass
            mixer = gdn(ROUNDS - 1)
            body("l1z", 0, 8, hook_z)
            gate(7)
            o_split(3)
            last_x_block = residual_phase("out1")
            ffn("gu1", "out1", last_x_block, FF // NB)
            last_x_block = residual_phase("dn1")
            for j in (1, 3, 4):
                last_x_block(j)
            dve.wait_ge(xs_copied, 16)
            dve.wait_ge(consts_in, 16 * 5)
            for m in range(M):
                V.scalar_tensor_tensor(x[:, m, :], x[:, m, :], rstd[:, m:m + 1], fgain[:], op0=ALU.mult, op1=ALU.mult
                                       ).then_inc(epi_step, 1)


WEIGHTS = ["x", "l0_w_in", "l0_gate_bias", "l0_mlstm_norm", "l0_w_out", "l0_w_gate", "l0_w_up", "l0_w_down",
           "l1_w_in", "l1_a_log", "l1_dt_bias", "l1_gdn_norm", "l1_w_out", "l1_w_gate", "l1_w_up", "l1_w_down",
           "final_norm"]


def layout(inputs):
    arrays = {f"in_{name}": np.ascontiguousarray(inputs[name]) for name in WEIGHTS}
    gains = [np.asarray(inputs[n]).reshape(KT, P).T for n in ("l0_norm_mix", "l0_norm_ffn", "l1_norm_mix", "l1_norm_ffn")]
    arrays["in_gains"] = np.ascontiguousarray(np.concatenate(gains, 1))
    conv = np.asarray(inputs["l1_conv_w"]).reshape(CW, -1, P)
    arrays["in_conv"] = np.ascontiguousarray(conv.transpose(2, 1, 0).reshape(P, -1))
    arrays["in_positions"] = np.ascontiguousarray(np.asarray(inputs["positions"]).reshape(M, P).T)
    arrays["in_shape_constants"] = shape_constants()
    return arrays


def kernel(**inputs):
    import concourse.bacc as bacc
    from concourse.bass_utils import run_bass_kernel_spmd

    nc = bacc.Bacc("TRN2", target_bir_lowering=False, num_devices=1)
    arrays = layout(inputs)
    aps = {name[3:]: nc.dram_tensor(name, a.shape, mybir.dt.from_np(a.dtype), kind="ExternalInput").ap()
           for name, a in arrays.items()}
    out = nc.dram_tensor("out_y", (SEQ, D), F32, kind="ExternalOutput").ap()
    build(nc, aps, out)
    r = run_bass_kernel_spmd(nc, [arrays], core_ids=[0])
    return r.results[0]["out_y"].reshape(1, SEQ, D)
```
